# Optimizing a Trainium2 kernel written in Bass

```python
import jax, jax.numpy as jnp
from jax import lax
import numpy as np

D_MODEL = 1024
BATCH = 1
SEQ = 128
DEPTH = 1
DEC_BATCH = 1
DEC_SEQ = 1024
PAST_LEN = 256

GRID_W = 64
EPS = 1e-6
HG_HEADS = 4
HG_DK = 128
HG_DV = 128
HG_KW = HG_HEADS * HG_DK
HG_VW = HG_HEADS * HG_DV
HG_CHUNK = 32
LRU_W = D_MODEL // 2
LRU_BLOCKS = 8
LRU_BW = LRU_W // LRU_BLOCKS
CONV_W = 4
LRU_C = 8.0
PK_HEADS = 8
N_KEYS = 128
N_EXPERTS = N_KEYS * N_KEYS
PK_TOPK = 16
PK_DQ = 256
PK_DH = PK_DQ // 2
PK_TOKEN_BLOCK = 128
IN_SIZES = (HG_KW, HG_KW, HG_KW, HG_VW, HG_VW, LRU_W, LRU_W, D_MODEL, D_MODEL)
IN_W = sum(IN_SIZES)
IN_SPLITS = tuple(sum(IN_SIZES[:i + 1]) for i in range(len(IN_SIZES) - 1))

kernel_name = 'hybrid_hgrn2_rglru_peer_diffusion_step'

def _rmsnorm(x, w):
    xf = x.astype(jnp.float32)
    y = xf * lax.rsqrt(jnp.mean(xf * xf, axis=-1, keepdims=True) + EPS)
    return (y * w.astype(jnp.float32)).astype(x.dtype)

def _flip(t):
    return jnp.flip(t, axis=1)

def _to_col_major(t):
    b, n, w = t.shape
    rows = n // GRID_W
    return t.reshape(b, rows, GRID_W, w).transpose(0, 2, 1, 3).reshape(b, n, w)

def _to_row_major(t):
    b, n, w = t.shape
    rows = n // GRID_W
    return t.reshape(b, GRID_W, rows, w).transpose(0, 2, 1, 3).reshape(b, n, w)

def _hgrn2_scan(q, k, v, logf, s0):
    b, n, h, _ = q.shape
    nc = n // HG_CHUNK

    def chunks(t):
        return t.astype(jnp.float32).reshape(b, nc, HG_CHUNK, h, t.shape[-1])

    q, k, v, logf = chunks(q), chunks(k), chunks(v), chunks(logf)
    cum = jnp.cumsum(logf, axis=2)
    tot = cum[:, :, -1:]
    q_dec = q * jnp.exp(cum)
    k_inv = k * jnp.exp(-cum)
    k_end = k * jnp.exp(tot - cum)
    lower = jnp.tril(jnp.ones((HG_CHUNK, HG_CHUNK), dtype=bool))
    att = jnp.where(lower, jnp.einsum('bcthk,bcshk->bchts', q_dec, k_inv), 0.0)
    o_intra = jnp.einsum('bchts,bcshv->bcthv', att, v)
    ds = jnp.einsum('bcshk,bcshv->bchkv', k_end, v)
    decay = jnp.exp(tot[:, :, 0])

    def step(s, inp):
        d, dsc = inp
        return d[..., None] * s + dsc, s

    s_fin, s_prev = lax.scan(step, s0.astype(jnp.float32),
                             (jnp.moveaxis(decay, 1, 0), jnp.moveaxis(ds, 1, 0)))
    o_inter = jnp.einsum('bcthk,bchkv->bcthv', q_dec, jnp.moveaxis(s_prev, 0, 1))
    return (o_intra + o_inter).reshape(b, n, h, -1), s_fin

def _lin_combine(left, right):
    a1, b1 = left
    a2, b2 = right
    return a1 * a2, a2 * b1 + b2

def _rglru(y, w_r, b_r, w_i, b_i, lam, h0):
    b, n, w = y.shape
    yb = y.reshape(b, n, LRU_BLOCKS, LRU_BW)
    r = jax.nn.sigmoid(jnp.einsum('bngi,gij->bngj', yb, w_r.astype(jnp.float32)).reshape(b, n, w)
                       + b_r.astype(jnp.float32))
    i = jax.nn.sigmoid(jnp.einsum('bngi,gij->bngj', yb, w_i.astype(jnp.float32)).reshape(b, n, w)
                       + b_i.astype(jnp.float32))
    log_a = -LRU_C * jax.nn.softplus(-lam.astype(jnp.float32)) * r
    a = jnp.exp(log_a)
    u = jnp.sqrt(-jnp.expm1(2.0 * log_a)) * (i * y)
    u = u.at[:, 0].add(a[:, 0] * h0.astype(jnp.float32))
    _, hs = lax.associative_scan(_lin_combine, (a, u), axis=1)
    return hs, hs[:, -1]

def _short_conv(x, w, bias):
    n = x.shape[1]
    left = CONV_W // 2
    xp = jnp.pad(x, ((0, 0), (left, CONV_W - 1 - left), (0, 0)))
    out = xp[:, 0:n] * w[0]
    for j in range(1, CONV_W):
        out = out + xp[:, j:j + n] * w[j]
    return out + bias

def _mixer(h, p, lb, hg_s0, lru_s0, col_major):
    b, n, _ = h.shape
    f32 = jnp.float32
    z = h @ p['w_in']
    q, f_fw, f_bw, v, g, xr, xg, ga, gb = jnp.split(z, IN_SPLITS, axis=-1)

    def heads(t):
        return t.astype(f32).reshape(b, n, HG_HEADS, -1)

    q = jax.nn.silu(heads(q))
    v = heads(v)

    def forget(f_raw, lb_dir):
        f = lb_dir + (1.0 - lb_dir) * jax.nn.sigmoid(f_raw.astype(f32))
        return heads(1.0 - f), heads(jnp.log(f))

    k_fw, lf_fw = forget(f_fw, lb[0])
    k_bw, lf_bw = forget(f_bw, lb[1])
    o_fw, s_fw = _hgrn2_scan(q, k_fw, v, lf_fw, hg_s0[:, 0])
    o_bw, s_bw = _hgrn2_scan(_flip(q), _flip(k_bw), _flip(v), _flip(lf_bw), hg_s0[:, 1])
    o = o_fw + _flip(o_bw)
    o = _rmsnorm(o, p['hg_norm']) * jax.nn.silu(heads(g))
    y_a = o.reshape(b, n, HG_VW).astype(h.dtype) @ p['w_branch_a']

    xr = xr.astype(f32)
    if col_major:
        xr = _to_col_major(xr)
    xc = _short_conv(xr, p['lru_conv_w'].astype(f32), p['lru_conv_b'].astype(f32))
    h_fw, e_fw = _rglru(xc, p['lru_w_r'][0], p['lru_b_r'][0], p['lru_w_i'][0], p['lru_b_i'][0],
                        p['lru_lambda'][0], lru_s0[:, 0])
    h_bw, e_bw = _rglru(_flip(xc), p['lru_w_r'][1], p['lru_b_r'][1], p['lru_w_i'][1], p['lru_b_i'][1],
                        p['lru_lambda'][1], lru_s0[:, 1])
    hr = h_fw + _flip(h_bw)
    if col_major:
        hr = _to_row_major(hr)
    y_b = (hr.astype(h.dtype) * jax.nn.gelu(xg)) @ p['w_branch_b']

    merged = jax.nn.sigmoid(ga) * y_a + jax.nn.sigmoid(gb) * y_b
    return (merged @ p['w_out'],
            jnp.stack([s_fw, s_bw], axis=1),
            jnp.stack([e_fw, e_bw], axis=1))

def _peer(h, p):
    b, n, d = h.shape
    t = b * n
    ht = h.reshape(t, d)
    qh = (ht @ p['pk_w_q']).astype(jnp.float32).reshape(t, PK_HEADS, 2, PK_DH)
    s = jnp.einsum('thpd,phkd->pthk', qh, p['pk_sub_keys'].astype(jnp.float32))
    sv, si = lax.top_k(s, PK_TOPK)
    cand = (sv[0][..., :, None] + sv[1][..., None, :]).reshape(t, PK_HEADS, PK_TOPK * PK_TOPK)
    cidx = (si[0][..., :, None] * N_KEYS + si[1][..., None, :]).reshape(t, PK_HEADS, PK_TOPK * PK_TOPK)
    best, pos = lax.top_k(cand, PK_TOPK)
    eidx = jnp.take_along_axis(cidx, pos, axis=-1)
    gate = jax.nn.softmax(best, axis=-1)
    nb = t // PK_TOKEN_BLOCK
    u_tab, v_tab = p['pk_u'], p['pk_v']

    def block(args):
        hb, eb, gb = args
        act = jax.nn.gelu(jnp.einsum('td,thkd->thk', hb, u_tab[eb]).astype(jnp.float32))
        return jnp.einsum('thk,thkd->td', (gb * act).astype(hb.dtype), v_tab[eb])

    out = lax.map(block, (ht.reshape(nb, PK_TOKEN_BLOCK, d),
                          eidx.reshape(nb, PK_TOKEN_BLOCK, PK_HEADS, PK_TOPK),
                          gate.reshape(nb, PK_TOKEN_BLOCK, PK_HEADS, PK_TOPK)))
    return out.reshape(b, n, d)

def _layer(x, cond, p, lb, hg_s0, lru_s0, col_major):
    m = (jax.nn.silu(cond.astype(jnp.float32)) @ p['w_mod'].astype(jnp.float32)
         + p['b_mod'].astype(jnp.float32))
    sh1, sc1, g1, sh2, sc2, g2 = jnp.split(m[:, None, :].astype(x.dtype), 6, axis=-1)
    h = _rmsnorm(x, p['norm1']) * (1.0 + sc1) + sh1
    mix, hg_fin, lru_fin = _mixer(h, p, lb, hg_s0, lru_s0, col_major)
    x = x + g1 * mix
    h = _rmsnorm(x, p['norm2']) * (1.0 + sc2) + sh2
    x = x + g2 * _peer(h, p)
    return x, hg_fin, lru_fin

def setup_inputs(seed: int = 0) -> dict:
    key = jax.random.key(seed)
    ks = jax.random.split(key, 32)
    D = D_MODEL

    def nrm(k, shape, s):
        return jax.random.normal(k, shape, jnp.float32) * s

    a_c = jax.random.uniform(ks[18], (DEPTH, 2, LRU_W), jnp.float32, 0.9, 0.999)
    sig = a_c ** (1.0 / LRU_C)
    lru_lambda = jnp.log(sig) - jnp.log1p(-sig)
    return {
        'x_prompt': nrm(ks[0], (BATCH, SEQ, D), 1.0),
        'x_sample': nrm(ks[1], (DEC_BATCH, DEC_SEQ, D), 1.0),
        'state_hgrn': nrm(ks[2], (DEC_BATCH, DEPTH, 2, HG_HEADS, HG_DK, HG_DV), 0.5),
        'state_rglru': nrm(ks[3], (DEC_BATCH, DEPTH, 2, LRU_W), 0.5),
        'c': nrm(ks[4], (DEC_BATCH, D), 1.0),
        'c_ctx': nrm(ks[5], (D,), 1.0),
        'w_mod': nrm(ks[6], (DEPTH, D, 6 * D), 0.5 * D ** -0.5),
        'b_mod': nrm(ks[7], (DEPTH, 6 * D), 0.01),
        'norm1': 1.0 + nrm(ks[8], (DEPTH, D), 0.02),
        'w_in': nrm(ks[9], (DEPTH, D, IN_W), D ** -0.5),
        'hg_lb_logits': nrm(ks[10], (2, DEPTH + 1, HG_KW), 0.5),
        'hg_norm': 1.0 + nrm(ks[11], (DEPTH, HG_DV), 0.02),
        'lru_conv_w': nrm(ks[12], (DEPTH, CONV_W, LRU_W), CONV_W ** -0.5),
        'lru_conv_b': nrm(ks[13], (DEPTH, LRU_W), 0.01),
        'lru_w_r': nrm(ks[14], (DEPTH, 2, LRU_BLOCKS, LRU_BW, LRU_BW), LRU_BW ** -0.5),
        'lru_b_r': nrm(ks[15], (DEPTH, 2, LRU_W), 0.01),
        'lru_w_i': nrm(ks[16], (DEPTH, 2, LRU_BLOCKS, LRU_BW, LRU_BW), LRU_BW ** -0.5),
        'lru_b_i': nrm(ks[17], (DEPTH, 2, LRU_W), 0.01),
        'lru_lambda': lru_lambda,
        'w_branch_a': nrm(ks[19], (DEPTH, HG_VW, D), HG_VW ** -0.5),
        'w_branch_b': nrm(ks[20], (DEPTH, LRU_W, D), LRU_W ** -0.5),
        'w_out': nrm(ks[21], (DEPTH, D, D), D ** -0.5),
        'norm2': 1.0 + nrm(ks[22], (DEPTH, D), 0.02),
        'pk_w_q': nrm(ks[23], (DEPTH, D, PK_HEADS * PK_DQ), D ** -0.5),
        'pk_sub_keys': nrm(ks[24], (DEPTH, 2, PK_HEADS, N_KEYS, PK_DH), PK_DH ** -0.5),
        'pk_u': nrm(ks[25], (DEPTH, N_EXPERTS, D), D ** -0.5),
        'pk_v': nrm(ks[26], (DEPTH, N_EXPERTS, D), PK_HEADS ** -0.5),
        'norm_f': 1.0 + nrm(ks[27], (D,), 0.02),
    }

def reference(x_prompt, x_sample, state_hgrn, state_rglru, c, c_ctx, w_mod, b_mod, norm1, w_in,
              hg_lb_logits, hg_norm, lru_conv_w, lru_conv_b, lru_w_r, lru_b_r, lru_w_i, lru_b_i,
              lru_lambda, w_branch_a, w_branch_b, w_out, norm2, pk_w_q, pk_sub_keys, pk_u, pk_v,
              norm_f):
    lb_all = jnp.cumsum(jax.nn.softmax(hg_lb_logits.astype(jnp.float32), axis=1), axis=1)
    xp, xs = x_prompt, x_sample
    cond_ctx = c_ctx[None, :]
    n_ctx = x_prompt.shape[0]
    hg_new, lru_new = [], []
    for l in range(DEPTH):
        p = {'w_mod': w_mod[l], 'b_mod': b_mod[l], 'norm1': norm1[l], 'w_in': w_in[l],
             'hg_norm': hg_norm[l], 'lru_conv_w': lru_conv_w[l], 'lru_conv_b': lru_conv_b[l],
             'lru_w_r': lru_w_r[l], 'lru_b_r': lru_b_r[l], 'lru_w_i': lru_w_i[l],
             'lru_b_i': lru_b_i[l], 'lru_lambda': lru_lambda[l], 'w_branch_a': w_branch_a[l],
             'w_branch_b': w_branch_b[l], 'w_out': w_out[l], 'norm2': norm2[l],
             'pk_w_q': pk_w_q[l], 'pk_sub_keys': pk_sub_keys[l], 'pk_u': pk_u[l], 'pk_v': pk_v[l]}
        lb = lb_all[:, l]
        hg0 = jnp.zeros((n_ctx, 2, HG_HEADS, HG_DK, HG_DV), jnp.float32)
        lr0 = jnp.zeros((n_ctx, 2, LRU_W), jnp.float32)
        xp, hg_fin, lru_fin = _layer(xp, cond_ctx, p, lb, hg0, lr0, False)
        hg_new.append(hg_fin)
        lru_new.append(lru_fin)
        xs, _, _ = _layer(xs, c, p, lb, state_hgrn[:, l], state_rglru[:, l], True)
    y_prompt = _rmsnorm(xp, norm_f)
    y_sample = _rmsnorm(xs, norm_f)
    new_state_hgrn = jnp.stack(hg_new, axis=1)
    new_state_rglru = jnp.stack(lru_new, axis=1)
    return (y_prompt, y_sample, new_state_hgrn, new_state_rglru)


_drawn_inputs = setup_inputs


def setup_inputs(seed=0):
    import zlib

    import numpy as np

    out = dict(_drawn_inputs(seed))
    spreads = {}
    factors = {'state_hgrn': 25.897,
     'state_rglru': 3.644,
     'norm1': 3.446,
     'hg_norm': 8.0,
     'lru_b_r': 41.112,
     'lru_b_i': 31.492,
     'norm2': 23.061,
     'norm_f': 9.453,
     'lru_conv_b': 4.316}
    for name, (base, spread) in spreads.items():
        noise = np.random.default_rng([zlib.crc32(name.encode()), seed]).standard_normal(out[name].shape)
        drawn = base * np.exp(spread * noise) if base else spread * noise
        out[name] = __import__('jax').numpy.asarray(drawn.astype(out[name].dtype))
    for name, factor in factors.items():
        out[name] = (out[name] * factor).astype(out[name].dtype)
    return out
```

```python
from contextlib import ExitStack

import numpy as np
import concourse.bass as bass
from concourse import mybir

ALU = mybir.AluOpType
ACT = mybir.ActivationFunctionType
F32 = mybir.dt.float32
I32 = mybir.dt.int32
U32 = mybir.dt.uint32
AX_X = mybir.AxisListType.X

P = 128
D = 1024
KD = D // P
N_CTX = 128
N_LAT = 1024
T = N_CTX + N_LAT
TILES = T // P
NCH = 3
CH = T // NCH
GRID_W = 64
GRID_H = N_LAT // GRID_W
EPS = 1e-6
HEADS = 4
CHUNK = 32
CPT = P // CHUNK
NCK = T // CHUNK
LRU_C = 8.0
MODW = 6 * D
MODC = MODW // 512
PK_HEADS = 8
TOPK = 16
NKEYS = 128
NEG = -3.0e38
RING = 8
ROUNDS = PK_HEADS * TOPK // RING
PAIRS = PK_HEADS // 2
RPP = ROUNDS // PAIRS
DVE_HEAD = 33
GRP = 2

P_LB, P_CW, P_CB, P_BR, P_BI, P_LAM, P_HN, P_H0, NPAR = 0, 4, 8, 9, 11, 13, 15, 16, 18

B_FF, B_Q, B_FB, B_XR, B_G, B_V, B_XG = range(7)
NB = 7
B_GATES = NB
B_SSQ = NB + 4
ZC = (NB + 5) * NCH
TI = 2 * TILES

A_HT = 0
A_OA = A_HT + KD * T
A_HB = A_OA + HEADS * T
A_W = A_HB + HEADS * T
A_BUF = A_W + NB * D
XR_W = T + 8
A_S = A_BUF + 17 * T + XR_W
NS = 12
A_ATT = A_S + NS * P
A_KET = A_ATT + 4 * P
A_SM = A_KET + 2 * CPT * P
A_WRI = A_SM + T + CHUNK
A_S0 = A_WRI + 4 * P
A_SF = A_S0 + 2 * P
A_END = A_SF + 2 * P
A_MG = A_BUF
A_WM = A_MG + KD * T
WM = 24 * P
A_SIG = A_WM + 2 * WM
A_WO = A_SIG + 4 * CH
A_X = A_WM
A_WQ = 0
A_KEY = A_WQ + 16 * D
A_RING = A_W
A_B = A_RING + RING * 2 * D
assert A_KEY + 16 * P <= A_RING and A_WO + KD * D <= A_END and A_X + 6 * D <= A_SIG
assert A_B >= A_WM - 8


def wait_alone(eng, sem, value):
    eng.wait_ge(sem, value)
    eng.nop(nofuse=True)


class Chain:

    def __init__(self, eng, sem, base=0):
        self.eng, self.sem, self.base, self.n = eng, sem, base, 0

    def __call__(self, ins, alone=False):
        self.n += 1
        ins.then_inc(self.sem, 1)
        if alone:
            wait_alone(self.eng, self.sem, self.base + self.n)
        else:
            self.eng.wait_ge(self.sem, self.base + self.n)


def build(nc, xT, x_tok, cT, w_mod, b_mod, n1T, w_in, par, wri, s0, w_mg, w_out, n2, nf, w_q, keys,
          uv, y_out, hg_out, lru_out, mod_d, x1_d):
    ctx = ExitStack()
    sb = lambda name, shape, dt=F32: nc.alloc_sbuf_tensor(name, shape, dt)
    sem = lambda name: nc.alloc_semaphore(name)

    AR = sb("arena", [P, A_END])
    ident = sb("ident", [P, P])
    ones = sb("ones", [P, P])
    zero = sb("zero", [P, P])
    mask_f = sb("mask_f", [P, P])
    mask_b = sb("mask_b", [P, P])
    cs = sb("cs", [P, KD, 2])
    n1 = sb("n1", [P, KD])
    sh1 = sb("sh1", [P, KD, 2])
    w1 = sb("w1", [P, KD, 2])
    eps = sb("eps", [P, 1])
    pr = sb("pr", [P, NPAR])
    ps_ = sb("ps_", [P, 40])
    dec = sb("dec", [P, 2, NCK])
    ef = sb("ef", [P, 2])
    PS = nc.alloc_psum_tensor("ps", [P, 8, 512], F32)

    hT = AR[:, A_HT:A_OA].rearrange("p (k t) -> p k t", k=KD)
    oA = AR[:, A_OA:A_HB].rearrange("p (k t) -> p k t", k=HEADS)
    hB = AR[:, A_HB:A_W].rearrange("p (k t) -> p k t", k=HEADS)
    W = AR[:, A_W:A_BUF].rearrange("p (b k c) -> p b k c", b=NB, k=KD)
    buf = lambda n: AR[:, A_BUF + n * T:A_BUF + (n + 1) * T]
    Q, SG, K, CUM = buf(0), [buf(1), buf(2)], [buf(3), buf(4)], buf(5)
    QD, KI, KE = [buf(6), buf(7)], [buf(8), buf(9)], [buf(10), buf(11)]
    V, XC, R, I = buf(12), buf(13), [buf(14), buf(15)], [buf(16), AR[:, A_BUF + 17 * T + 0:A_BUF + 17 * T + 0 + T]]
    XR = AR[:, A_BUF + 17 * T:A_BUF + 17 * T + XR_W]
    S = AR[:, A_S:A_ATT].rearrange("p (n v) -> p n v", n=NS)
    ATT = AR[:, A_ATT:A_KET].rearrange("p (d n t) -> p d n t", d=2, n=2)
    KET = AR[:, A_KET:A_SM].rearrange("p (n j k) -> p n j k", n=2, j=CPT)
    SM = AR[:, A_SM:A_WRI]
    WRI = AR[:, A_WRI:A_S0].rearrange("p (g c) -> p g c", g=4)
    S0 = AR[:, A_S0:A_SF].rearrange("p (d v) -> p d v", d=2)
    SF = AR[:, A_SF:A_END].rearrange("p (d v) -> p d v", d=2)
    WMOD = AR[:, A_BUF:A_BUF + 2 * 4096].rearrange("p (n k c) -> p n k c", n=2, k=KD)
    MROW = AR[0:2, A_BUF + 8192:A_BUF + 8192 + MODW]
    BROW = AR[0:2, A_BUF + 8192 + MODW:A_BUF + 8192 + 2 * MODW]
    SQ = [AR[:, A_W + n * T:A_W + (n + 1) * T] for n in range(2)]
    RS = AR[:, A_W + 2 * T:A_W + 3 * T]
    Vt = V.rearrange("p (t v) -> p t v", t=TILES)

    s_c, s_ms = sem("consts_ready"), sem("consts_step")
    l_x, l_c, l_b, s_silu = sem("l_x"), sem("l_c"), sem("l_b"), sem("silu_ready")
    l_mw = [sem("l_mw0"), sem("l_mw1")]
    m_ready, m_evac, s_dv = sem("mod_ready"), sem("mod_evac"), sem("dve_chain")
    s_act = sem("act_chain")
    t_ready, w1_ready = sem("modT_ready"), sem("w1_ready")
    sq_r, ssq_r, sd_r, h_ready = sem("square_ready"), sem("ssq_ready"), sem("sd_ready"), sem("h_ready")
    md_out = sem("mod_written")
    l_w = [sem(f"l_w{b}") for b in range(NB)]
    l_par = sem("l_par")
    z_ready, z_free = sem("z_ready"), sem("z_free")
    pa = [sem(f"par_{n}") for n in range(6)]
    f_r = [sem("f0_ready"), sem("f1_ready")]
    lf_r = [sem("lf0_ready"), sem("lf1_ready")]
    cum_r = [sem("cum0_ready"), sem("cum1_ready")]
    e_r = [sem("exp0_ready"), sem("exp1_ready")]
    tc_r = [sem("tc0_ready"), sem("tc1_ready")]
    e3_r = [sem("expend0_ready"), sem("expend1_ready")]
    k_r = [sem("kq0_ready"), sem("kq1_ready")]
    xc_r = sem("conv_ready")
    t2_r = [sem("tanh0_ready"), sem("tanh1_ready")]
    lru_done, hg_done = sem("lru_done"), sem("hg_done")
    ket_r, ket_e = sem("ket_ready"), sem("ket_evac")
    att_r, att_m = sem("att_ready"), sem("att_masked")
    ds_r, s_r = sem("ds_ready"), sem("state_ready")
    o_r, o_a = sem("o_ready"), sem("o_added")
    osq_r = sem("osq_ready")
    st_out = sem("state_out")

    W_ORDER = range(NB)
    def tile_of(it):
        return it if it < TILES else TI - 1 - it

    count, reads, writes = 0, {}, {}
    slot = 0
    for it in range(TI):
        d, tt = it // TILES, tile_of(it)
        first_ctx, first_lat = tt == 0, tt == (1 if d == 0 else TILES - 1)
        for jj in range(CPT):
            if jj == 0 and first_ctx:
                cur = (zero[:], None)
            elif jj == 0 and first_lat:
                cur = (S0[:, d, :], None)
            reads[it, jj] = cur
            last_lat = jj == CPT - 1 and tt == (TILES - 1 if d == 0 else 1)
            if last_lat:
                continue
            count += 1
            if jj == CPT - 1 and tt == 0:
                writes[it, jj] = (SF[:, d, :], count, True)
                cur = None
            else:
                writes[it, jj] = (S[:, slot % NS, :], count, False)
                cur = (S[:, slot % NS, :], count)
                slot += 1
    NSU = count
    LAST_CTX = max(k for _, k, final in writes.values() if final)
    state_of = lambda it, jj: reads[it, jj]


    MG = AR[:, A_MG:A_WM].rearrange("p (k t) -> p k t", k=KD)
    WMG = [AR[:, A_WM + n * WM:A_WM + (n + 1) * WM].rearrange("p (b c) -> p b c", c=P) for n in range(2)]
    SIG = [[AR[:, A_SIG + (2 * n + g) * CH:A_SIG + (2 * n + g + 1) * CH] for g in range(2)] for n in range(2)]
    WO = AR[:, A_WO:A_WO + KD * D].rearrange("p (k c) -> p k c", k=KD)
    XT = [AR[:, A_X + n * D:A_X + (n + 1) * D] for n in range(6)]
    l_wm = [sem("l_wm0"), sem("l_wm1")]
    mg_ready, mg_sig, mg_free, mg_ch = sem("merge_ready"), sem("merge_gates"), sem("merged"), sem("merge_step")
    l_wo, l_g1, l_xt = sem("l_wo"), sem("l_g1"), [sem("l_xt0"), sem("l_xt1")]
    mix_r, mix_f, x1_r = sem("mix_ready"), sem("mix_read"), sem("x1_ready")
    x1_st = [sem("x1_st0"), sem("x1_st1")]
    NMG = KD * NCH

    WQ = AR[:, A_WQ:A_WQ + 16 * D].rearrange("p (k c) -> p k c", k=KD)
    KEYS = AR[:, A_KEY:A_KEY + 16 * P]
    RG = AR[:, A_RING:A_B].rearrange("p (s c) -> p s c", s=RING)
    bt = lambda n: AR[:, A_B + n * D:A_B + (n + 1) * D]
    XN, XE, H2N, H2C, H2T_, W2B, SH2B, G2B, NFB, _, QQ, DG_, Y, SC_, CD_, OH_ = [bt(n) for n in range(16)]
    assert A_B + 16 * D <= A_END
    H2T = H2T_.rearrange("p (k t) -> p k t", k=KD)
    QS, QTS = QQ[:, 0:512], QQ[:, 512:1024]
    DG = DG_.rearrange("p (s c) -> p s c", s=RING)
    SCS, SCW = SC_[:, 0:512], SC_[:, 512:1024]
    CAND, CANDW = CD_[:, 0:512], CD_[:, 512:1024]
    OH = [OH_[:, 0:512], OH_[:, 512:1024]]
    small = [A_B + 9 * D]

    def sm(*shape, dt=F32):
        n = int(np.prod(shape))
        ap = AR[:, small[0]:small[0] + n]
        small[0] += n
        assert small[0] <= A_B + 10 * D
        if dt != F32:
            ap = ap.bitcast(dt)
        names = "abc"[:len(shape)]
        return ap if len(shape) == 1 else ap.rearrange(
            f"p ({' '.join(names)}) -> p {' '.join(names)}", **{k: d for k, d in zip(names, shape)})

    EIDX, GATE = sm(2 * P, dt=U32), sm(2 * P)
    IDXS = sm(2, RING, dt=U32)
    iota = sm(TOPK)
    SV, SI, SIF = sm(4, TOPK), sm(4, TOPK, dt=U32), sm(4, TOPK)
    BEST, POS = sm(2, TOPK), sm(2, TOPK, dt=U32)
    PRE, GEL, COEF, st = sm(RING), sm(RING), sm(RING), sm(8)
    PHL = sb("places", [P, 2, 2, TOPK], U32)[:]
    PHF, EE = sb("places_f", [P, 2, 2, TOPK])[:], sb("key_numbers", [P, 2, 2, TOPK])[:]

    l_wq, l_rows, l_rows2, l_g2, l_nf = sem("l_wq"), sem("l_rows"), sem("l_rows_lat"), sem("l_g2"), sem("l_nf")
    l_xn, l_xe = sem("l_xn"), sem("l_xe")
    n_sq, n_sd, h2_r, h2t_r, h2t_e = sem("n_square"), sem("n_sd"), sem("h2_ready"), sem("h2T_ready"), sem("h2T_evac")
    q_r, q_e, qt_r, qt_e, sc_r, sc_e = (sem(x) for x in ("q_ready", "q_evac", "qT_ready", "qT_evac",
                                                         "scores_ready", "scores_evac"))
    top_r, ge_r = sem("top_ready"), sem("gate_exp_ready")
    c_pair, c_front, c_end = sem("pair_step"), sem("front_step"), sem("end_step")
    pair_done, idx_r = sem("pair_done"), sem("round_index_ready")
    gathered = [sem(f"gathered{n}") for n in range(RING)]
    dots, gel_r, coef_r, diag_r, v_used = (sem(x) for x in ("dots", "gelu_ready", "coef_ready", "diag_ready",
                                                            "v_used"))
    acc_free, e_sq, e_sd, y_r, y_st = (sem(x) for x in ("acc_free", "end_square", "end_sd", "y_ready", "y_stored"))
    it_r = sem("iota_ready")
    PAIR_STEPS, FRONT_STEPS, END_STEPS = 16, 2, 3

    def row(ap):
        return ap.partition_broadcast(P)

    def stage_b_sp(sp):
        for n in range(2):
            sp.dma_start(WMG[n], w_mg[n]).then_inc(l_wm[n], 16)
        sp.dma_start(WO, w_out).then_inc(l_wo, 16)
        with sp.Fori(0, KD // 2 - 1) as i:
            for u in range(2):
                sp.wait_ge(mg_ready, i * 2 * NCH + (u + 1) * NCH)
                sp.dma_start(WMG[u], w_mg[2 * i + 2 + u]).then_inc(l_wm[u], 16)
        sp.wait_ge(mg_free, NMG)
        sp.wait_ge(md_out, 16)
        for s in range(2):
            sp.dma_start(XT[4 + s], row(mod_d[s, 2 * D:3 * D])).then_inc(l_g1, 16)
        for t in range(2):
            sp.dma_start(XT[t], x_tok[t]).then_inc(l_xt[t], 16)
        for k in range(4):
            sp.dma_start(WQ[:, 2 * k:2 * k + 2, :], w_q[:, 2 * k:2 * k + 2, :]).then_inc(l_wq, 16)
        sp.dma_start(KEYS, keys).then_inc(l_wq, 16)
        for t in range(TILES):
            sp.wait_ge(x1_r, t + 1)
            sp.dma_start(x1_d[t], XT[2 + t % 2]).then_inc(x1_st[t % 2], 16)
            if t + 2 < TILES:
                sp.dma_start(XT[t % 2], x_tok[t + 2]).then_inc(l_xt[t % 2], 16)
        sp.wait_ge(x1_st[0], 16 * ((TILES + 1) // 2))
        sp.wait_ge(x1_st[1], 16 * (TILES // 2))

        sp.dma_start(XN, x1_d[0]).then_inc(l_xn, 16)
        sp.dma_start(XE, x1_d[0]).then_inc(l_xe, 16)
        sp.dma_start(W2B, row(mod_d[0, 4 * D:5 * D])).then_inc(l_rows, 16)
        sp.dma_start(Y, row(n2)).then_inc(l_rows, 16)
        sp.dma_start(SH2B, row(mod_d[0, 3 * D:4 * D])).then_inc(l_rows, 16)
        sp.dma_start(G2B, row(mod_d[0, 5 * D:6 * D])).then_inc(l_g2, 16)
        sp.dma_start(NFB, row(nf)).then_inc(l_nf, 16)
        sp.wait_ge(h2_r, 1)
        sp.dma_start(W2B, row(mod_d[1, 4 * D:5 * D])).then_inc(l_rows2, 16)
        sp.dma_start(SH2B, row(mod_d[1, 3 * D:4 * D])).then_inc(l_rows2, 16)
        sp.dma_start(XN, x1_d[1]).then_inc(l_xn, 16)

        def tile(t, last):
            if not last:
                sp.wait_ge(h2_r, t + 2)
                sp.dma_start(XN, x1_d[t + 2]).then_inc(l_xn, 16)
            sp.wait_ge(y_r, t + 1)
            sp.dma_start(y_out[t], Y).then_inc(y_st, 16)
            sp.dma_start(XE, x1_d[t + 1]).then_inc(l_xe, 16)

        tile(0, False)
        sp.dma_start(G2B, row(mod_d[1, 5 * D:6 * D])).then_inc(l_g2, 16)
        with sp.Fori(1, TILES - 2) as t:
            tile(t, False)
        tile(TILES - 2, True)
        sp.wait_ge(y_r, TILES)
        sp.dma_start(y_out[TILES - 1], Y).then_inc(y_st, 16)
        sp.wait_ge(y_st, 16 * TILES)
        sp.wait_ge(st_out, 48 * HEADS)

    def stage_b_pool(pool):
        pool.wait_ge(x1_r, TILES)
        nc.gpsimd.iota(iota, pattern=[[1, TOPK]], base=0, channel_multiplier=0,
                       allow_small_or_imprecise_dtypes=True).then_inc(it_r, 1)

        def fetch(r, par_, first=False):
            pool.wait_ge(idx_r, r + 1)
            for s in range(RING):
                if not first:
                    wait_alone(pool, v_used, r * RING + (s + 1 - RING))
                nc.gpsimd.indirect_dma_start(
                    out=RG[:, s, :], out_offset=None, in_=uv,
                    in_offset=bass.IndirectOffsetOnAxis(ap=IDXS[:, par_, s:s + 1], axis=0),
                ).then_inc(gathered[s], 16)

        fetch(0, 0, first=True)
        fetch(1, 1)
        with pool.Fori(0, (TILES * ROUNDS - 2) // 2) as i:
            fetch(i * 2 + 2, 0)
            fetch(i * 2 + 3, 1)

    def stage_b_pe(pe):
        with pe.Fori(0, KD // 2) as i:
            for u in range(2):
                pe.wait_ge(l_wm[u], i * 16 + 16)
                for n in range(NCH):
                    b = 4 * ((u * NCH + n) % 2)
                    sl = slice(n * CH, (n + 1) * CH)
                    for g, (src, w0, nk) in enumerate(((hT, 0, KD), (hT, KD, KD), (oA, 2 * KD, HEADS),
                                                       (hB, 2 * KD + HEADS, HEADS))):
                        for k in range(nk):
                            mm = nc.tensor.matmul(PS[:, b + g, 0:CH], WMG[u][:, w0 + k, :], src[:, k, sl],
                                                  start=(k == 0), stop=(k == nk - 1))
                    mm.then_inc(mg_ready, 1)
                    if u or n:
                        pe.wait_ge(mg_free, i * 2 * NCH + (u * NCH + n))
            wait_alone(pe, mg_free, i * 2 * NCH + 2 * NCH)
        pe.wait_ge(l_wo, 16)
        for t in range(TILES):
            if t >= 2:
                pe.wait_ge(mix_f, t - 1)
            for n in range(2):
                for k in range(KD):
                    mm = nc.tensor.matmul(PS[:, 2 * (t % 2) + n, :], MG[:, k, t * P:(t + 1) * P],
                                          WO[:, k, n * 512:(n + 1) * 512], start=(k == 0), stop=(k == KD - 1))
            mm.then_inc(mix_r, 1)
        pe.wait_ge(mix_f, TILES)
        pe.wait_ge(l_wq, 80)

        def front(tn):
            pe.wait_ge(h2_r, tn + 1)
            for k in range(KD):
                mm = nc.tensor.transpose(PS[:, 2 + k // 4, (k % 4) * P:(k % 4 + 1) * P],
                                         H2N[:, k * P:(k + 1) * P], ident[:])
            mm.then_inc(h2t_r, 1)
            wait_alone(pe, h2t_e, tn + 1)

        def pair(tn, i):
            m = tn * PAIRS + i + 1
            for k in range(KD):
                mm = nc.tensor.matmul(PS[:, 4, :], H2T[:, k, :], WQ[:, k, bass.ds(i * 512, 512)],
                                      start=(k == 0), stop=(k == KD - 1))
            mm.then_inc(q_r, 1)
            pe.wait_ge(q_e, m)
            for c in range(4):
                mm = nc.tensor.transpose(PS[:, 5, c * P:(c + 1) * P], QS[:, c * P:(c + 1) * P], ident[:])
            mm.then_inc(qt_r, 1)
            pe.wait_ge(qt_e, m)
            for c in range(4):
                mm = nc.tensor.matmul(PS[:, 6, c * P:(c + 1) * P], QTS[:, c * P:(c + 1) * P],
                                      KEYS[:, bass.ds(i * 512 + c * P, P)], start=True, stop=True)
            mm.then_inc(sc_r, 1)

        def rounds(t, i):
            for q in range(RPP):
                for s in range(RING):
                    n0 = (t * ROUNDS + i * RPP + q) * RING + s + 1
                    pe.wait_ge(diag_r, n0)
                    for n in range(2):
                        mm = nc.tensor.matmul(PS[:, n, :], DG[:, s, :], RG[:, s, D + n * 512:D + (n + 1) * 512],
                                              start=False, stop=False, skip_group_check=True)
                    mm.then_inc(v_used, 1)

        def clear():
            for n in range(2):
                nc.tensor.matmul(PS[:, n, :], zero[:], zero[:, 0:1].to_broadcast([P, 512]),
                                 start=True, stop=False, skip_group_check=True)

        def tile(t):
            pe.wait_ge(acc_free, t)
            clear()
            front(t + 1)
            with pe.Fori(0, PAIRS) as i:
                pair(t + 1, i)
                rounds(t, i)

        front(0)
        with pe.Fori(0, PAIRS) as i:
            pair(0, i)
        clear()
        front(1)
        with pe.Fori(0, PAIRS) as i:
            pair(1, i)
            rounds(0, i)
        with pe.Fori(1, TILES - 1) as t:
            tile(t)
        pe.wait_ge(acc_free, TILES - 1)
        clear()
        with pe.Fori(0, PAIRS) as i:
            rounds(TILES - 1, i)

    def stage_b_act(act):
        A = nc.scalar.activation
        with act.Fori(0, KD // 2) as i:
            for u in range(2):
                for n in range(NCH):
                    c = u * NCH + n
                    act.wait_ge(mg_ready, i * 2 * NCH + c + 1)
                    for g in range(2):
                        ins = A(SIG[c % 2][g], PS[:, 4 * (c % 2) + g, 0:CH], ACT.Sigmoid)
                    ins.then_inc(mg_sig, 1)

        def front(tn):
            act.wait_ge(l_xn, tn * 16 + 16)
            A(QQ, XN, ACT.Square, accum_out=st[:, 0:1]).then_inc(n_sq, 1)
            act.wait_ge(n_sq, tn + 1)
            A(st[:, 1:2], st[:, 0:1], ACT.Sqrt, bias=eps[:], scale=1.0 / D).then_inc(n_sd, 1)
            act.wait_ge(h2t_r, tn + 1)
            for n in range(2):
                cp = A(H2T_[:, n * 512:(n + 1) * 512], PS[:, 2 + n, :], ACT.Copy)
            cp.then_inc(h2t_e, 1)

        def pair(tn, i):
            m = tn * PAIRS + i
            act.wait_ge(q_r, m + 1)
            A(QS, PS[:, 4, :], ACT.Copy).then_inc(q_e, 1)
            act.wait_ge(qt_r, m + 1)
            A(QTS, PS[:, 5, :], ACT.Copy).then_inc(qt_e, 1)
            act.wait_ge(sc_r, m + 1)
            A(SCS, PS[:, 6, :], ACT.Copy).then_inc(sc_e, 1)

        def gates(tn, i):
            act.wait_ge(top_r, tn * PAIRS + i + 1)
            A(BEST, BEST, ACT.Exp).then_inc(ge_r, 1)

        def rounds(t, i, qs):
            def diag(q, g):
                n = (t * ROUNDS + i * RPP + q) * (RING // GRP) + g
                act.wait_ge(coef_r, n + 1)
                for s in range(g * GRP, (g + 1) * GRP):
                    A(DG[:, s, :], ident[:], ACT.Copy, scale=COEF[:, s:s + 1]).then_inc(diag_r, 1)

            todo = None
            for q in qs:
                for g in range(RING // GRP):
                    n = (t * ROUNDS + i * RPP + q) * (RING // GRP) + g
                    act.wait_ge(dots, n + 1)
                    sl = slice(g * GRP, (g + 1) * GRP)
                    A(GEL[:, sl], PRE[:, sl], ACT.Gelu_apprx_tanh).then_inc(gel_r, 1)
                    if todo:
                        diag(*todo)
                    todo = (q, g)
            diag(*todo)

        def end(t):
            act.wait_ge(e_sq, t + 1)
            A(st[:, 3:4], st[:, 2:3], ACT.Sqrt, bias=eps[:], scale=1.0 / D).then_inc(e_sd, 1)

        def tile(t):
            front(t + 1)
            with act.Fori(0, PAIRS) as i:
                pair(t + 1, i)
                rounds(t, i, (0, 1))
                gates(t + 1, i)
                rounds(t, i, (2, 3))
            end(t)

        front(0)
        with act.Fori(0, PAIRS) as i:
            pair(0, i)
            gates(0, i)
        tile(0)
        with act.Fori(1, TILES - 1) as t:
            tile(t)
        with act.Fori(0, PAIRS) as i:
            rounds(TILES - 1, i, (0, 1, 2, 3))
        end(TILES - 1)

    def stage_b_dve(dve):
        v = nc.vector
        with dve.Fori(0, KD // 2) as i:
            for u in range(2):
                for n in range(NCH):
                    c = u * NCH + n
                    dve.wait_ge(mg_sig, i * 2 * NCH + c + 1)
                    for g in range(2):
                        ins = v.tensor_tensor(SIG[c % 2][g], PS[:, 4 * (c % 2) + 2 + g, 0:CH], SIG[c % 2][g],
                                              ALU.mult)
                    ins.then_inc(mg_ch, 1)
                    dve.wait_ge(mg_ch, i * 2 * NCH + c + 1)
                    v.tensor_tensor(MG[:, i * 2 + u, n * CH:(n + 1) * CH], SIG[c % 2][0], SIG[c % 2][1],
                                    ALU.add).then_inc(mg_free, 1)
        dve.wait_ge(l_g1, 32)
        for t in range(TILES):
            dve.wait_ge(mix_r, t + 1)
            if t >= 2:
                dve.wait_ge(x1_st[t % 2], 16 * (t // 2))
            o = XT[2 + t % 2]
            g1 = XT[4 + (t > 0)]
            v.tensor_tensor(o, PS[:, 2 * (t % 2):2 * (t % 2) + 2, :].rearrange("p b c -> p (b c)"), g1,
                            ALU.mult).then_inc(mix_f, 1)
            dve.wait_ge(mix_f, t + 1)
            dve.wait_ge(l_xt[t % 2], 16 * (t // 2 + 1))
            v.tensor_tensor(o, o, XT[t % 2], ALU.add).then_inc(x1_r, 1)

        def front(tn, rows):
            ch = Chain(dve, c_front, tn * FRONT_STEPS)
            dve.wait_ge(n_sd, tn + 1)
            rows()
            ch(v.reciprocal(st[:, 4:5], st[:, 1:2]))
            ch(v.scalar_tensor_tensor(out=H2N, in0=XN, scalar=st[:, 4:5], in1=W2B, op0=ALU.mult, op1=ALU.mult))
            v.tensor_tensor(H2N, H2N, SH2B, ALU.add).then_inc(h2_r, 1)
            assert ch.n == FRONT_STEPS

        def top16(ch, n, vals, idx, src, work):
            lo, hi = slice(0, 8), slice(8, 16)
            for c in range(n):
                ins = v.max(vals(c, lo), src(c))
            ch(ins, alone=True)
            for c in range(n):
                v.match_replace(work(c), vals(c, lo), src(c), NEG)
                ins = v.max_index(idx(c, lo), vals(c, lo), src(c))
            ch(ins, alone=True)
            for c in range(n):
                ins = v.max(vals(c, hi), work(c))
            ch(ins, alone=True)
            for c in range(n):
                ins = v.max_index(idx(c, hi), vals(c, hi), work(c))
            ch(ins)

        def pair(tn, i):
            m = tn * PAIRS + i
            ch = Chain(dve, c_pair, m * PAIR_STEPS)
            wait_alone(dve, sc_e, m + 1)
            top16(ch, 4, lambda c, s: SV[:, c, s], lambda c, s: SI[:, c, s],
                  lambda c: SCS[:, c * P:(c + 1) * P], lambda c: SCW[:, c * P:(c + 1) * P])
            v.tensor_copy(SIF, SI)
            sv = SV.rearrange("p (a h) k -> p a h k", h=2)
            four = [P, 2, TOPK, TOPK]
            cand = CAND.rearrange("p (a x y) -> p a x y", a=2, x=TOPK)
            ch(v.tensor_tensor(cand, sv[:, :, 0, :].unsqueeze(3).to_broadcast(four),
                               sv[:, :, 1, :].unsqueeze(2).to_broadcast(four), ALU.add), alone=True)
            half = TOPK * TOPK
            top16(ch, 2, lambda c, s: BEST[:, c, s], lambda c, s: POS[:, c, s],
                  lambda c: CAND[:, c * half:(c + 1) * half], lambda c: CANDW[:, c * half:(c + 1) * half])
            v.tensor_copy(EE[:, 0, :, 0:1], BEST[:, :, 0:1])
            v.tensor_scalar(PHL[:, 0], POS, 4, None, ALU.logical_shift_right)
            ch(v.tensor_scalar(PHL[:, 1], POS, TOPK - 1, None, ALU.bitwise_and))
            v.tensor_tensor(BEST, BEST, EE[:, 0, :, 0:1].to_broadcast([P, 2, TOPK]),
                            ALU.subtract).then_inc(top_r, 1)
            ch(v.tensor_copy(PHF, PHL))
            sif = SIF.rearrange("p (a h) k -> p a h k", h=2)
            oh = [x.rearrange("p (a x y) -> p a x y", a=2, x=TOPK) for x in OH]
            for z in range(2):
                ins = v.tensor_tensor(oh[z], PHF[:, z].unsqueeze(3).to_broadcast(four),
                                      iota.unsqueeze(1).unsqueeze(1).to_broadcast(four), ALU.is_equal)
            ch(ins)
            for z in range(2):
                ins = v.tensor_tensor(oh[z], oh[z], sif[:, :, z, :].unsqueeze(2).to_broadcast(four), ALU.mult)
            ch(ins)
            for z in range(2):
                ins = v.tensor_reduce(EE[:, z], oh[z], AX_X, ALU.add)
            ch(ins)
            at = bass.ds(i * 2 * TOPK + P, 2 * TOPK)
            v.scalar_tensor_tensor(out=EIDX[:, at], in0=EE[:, 0].rearrange("p a k -> p (a k)"),
                                   scalar=float(NKEYS), in1=EE[:, 1].rearrange("p a k -> p (a k)"),
                                   op0=ALU.mult, op1=ALU.add)
            dve.wait_ge(ge_r, m + 1)
            ch(v.tensor_reduce(st[:, 5:7], BEST, AX_X, ALU.add))
            ch(v.reciprocal(st[:, 5:7], st[:, 5:7]))
            v.tensor_tensor(GATE[:, at].rearrange("p (a k) -> p a k", a=2), BEST,
                            st[:, 5:7].unsqueeze(2).to_broadcast([P, 2, TOPK]), ALU.mult).then_inc(pair_done, 1)
            dve.wait_ge(pair_done, m + 1)
            assert ch.n == PAIR_STEPS, ch.n

        def coef(t, i, q, g):
            n = (t * ROUNDS + i * RPP + q) * (RING // GRP) + g
            dve.wait_ge(gel_r, n + 1)
            sl = slice(g * GRP, (g + 1) * GRP)
            v.tensor_tensor(COEF[:, sl], GEL[:, sl],
                            GATE[:, bass.ds(i * RPP * RING + q * RING + g * GRP, GRP)],
                            ALU.mult).then_inc(coef_r, 1)

        def rounds(t, i, qs, copies=True):
            todo = None
            for q in qs:
                for g in range(RING // GRP):
                    for s in range(g * GRP, (g + 1) * GRP):
                        dve.wait_ge(gathered[s], (t * ROUNDS + i * RPP + q) * 16 + 16)
                        ins = v.tensor_tensor_reduce(RG[:, s, 0:D], RG[:, s, 0:D], H2C, 1.0, 0.0, ALU.mult,
                                                     ALU.add, PRE[:, s:s + 1])
                    ins.then_inc(dots, 1)
                    if todo:
                        coef(t, i, *todo)
                    todo = (q, g)
                if copies:
                    v.tensor_copy(IDXS[:, q % 2, :], EIDX[:, bass.ds(i * RPP * RING + (q + 2) * RING, RING)])\
                        .then_inc(idx_r, 1)
            coef(t, i, *todo)

        def shift():
            v.tensor_copy(H2C, H2N)
            v.tensor_copy(EIDX[:, 0:P], EIDX[:, P:2 * P])
            return v.tensor_copy(GATE[:, 0:P], GATE[:, P:2 * P])

        def end(t):
            ch = Chain(dve, c_end, t * END_STEPS)
            dve.wait_ge(v_used, (t + 1) * ROUNDS * RING)
            dve.wait_ge(l_g2, 32 if not isinstance(t, int) or t else 16)
            if not isinstance(t, int) or t:
                dve.wait_ge(y_st, t * 16)
            v.tensor_tensor(Y, PS[:, 0:2, :].rearrange("p b c -> p (b c)"), G2B, ALU.mult).then_inc(acc_free, 1)
            dve.wait_ge(acc_free, t + 1)
            dve.wait_ge(l_xe, t * 16 + 16)
            ch(v.tensor_tensor(Y, Y, XE, ALU.add))
            v.tensor_tensor_reduce(XE, Y, Y, 1.0, 0.0, ALU.mult, ALU.add, st[:, 2:3]).then_inc(e_sq, 1)
            dve.wait_ge(e_sd, t + 1)
            ch(v.reciprocal(st[:, 7:8], st[:, 3:4]))
            v.scalar_tensor_tensor(out=Y, in0=Y, scalar=st[:, 7:8], in1=NFB, op0=ALU.mult,
                                   op1=ALU.mult).then_inc(y_r, 1)
            ch(shift())
            assert ch.n == END_STEPS, ch.n

        def tile(t):
            front(t + 1, lambda: dve.wait_ge(l_rows2, 32))
            with dve.Fori(0, PAIRS) as i:
                rounds(t, i, (0, 1))
                pair(t + 1, i)
                rounds(t, i, (2, 3))
            end(t)

        def first_rows():
            dve.wait_ge(l_rows, 48)
            v.scalar_tensor_tensor(out=W2B, in0=W2B, scalar=1.0, in1=Y, op0=ALU.add, op1=ALU.mult)

        dve.wait_ge(it_r, 1)
        front(0, first_rows)
        with dve.Fori(0, PAIRS) as i:
            pair(0, i)
        dve.wait_ge(l_nf, 16)
        shift().then_inc(c_shift, 1)
        dve.wait_ge(c_shift, 1)
        for q in range(2):
            v.tensor_copy(IDXS[:, q, :], EIDX[:, q * RING:(q + 1) * RING]).then_inc(idx_r, 1)
        dve.wait_ge(l_rows2, 32)
        v.scalar_tensor_tensor(out=W2B, in0=W2B, scalar=1.0, in1=Y, op0=ALU.add, op1=ALU.mult).then_inc(c_shift, 1)
        dve.wait_ge(c_shift, 2)
        tile(0)
        with dve.Fori(1, TILES - 1) as t:
            tile(t)
        with dve.Fori(0, PAIRS - 1) as i:
            rounds(TILES - 1, i, (0, 1, 2, 3))
        rounds(TILES - 1, PAIRS - 1, (0, 1))
        rounds(TILES - 1, PAIRS - 1, (2, 3), copies=False)
        end(TILES - 1)

    c_shift = sem("shifted")
    block = ctx.enter_context(nc.Block())

    @block.sync
    def _(sp):
        sp.dma_start(cs[:], cT).then_inc(l_c, 16)
        sp.dma_start(n1[:], n1T).then_inc(l_c, 16)
        for c in range(2):
            sp.dma_start(WMOD[:, c], w_mod[c]).then_inc(l_mw[c], 16)
        sp.dma_start(BROW, b_mod).then_inc(l_b, 16)
        sp.dma_start(hT, xT).then_inc(l_x, 16)
        for c in range(2, MODC):
            sp.wait_ge(m_ready, c - 1)
            sp.dma_start(WMOD[:, c % 2], w_mod[c]).then_inc(l_mw[c % 2], 16)
        sp.wait_ge(m_evac, MODC)
        sp.dma_start(mod_d, MROW).then_inc(md_out, 16)
        sp.wait_ge(h_ready, KD)

        def weights(h, b):
            sp.dma_start(W[:, b], w_in[h, b]).then_inc(l_w[b], 16)

        def params(h):
            sp.dma_start(pr[:], par[h]).then_inc(l_par, 16)
            for half in range(2):
                a = half * 64
                sp.dma_start(WRI[a:a + 64, :, a:a + 64], wri[h, half]).then_inc(l_par, 16)
            sp.dma_start(S0, s0[h]).then_inc(l_par, 16)

        def results(h):
            sp.wait_ge(s_r, h * NSU + LAST_CTX)
            for d in range(2):
                sp.dma_start(hg_out[d, h], SF[:, d]).then_inc(st_out, 16)
            sp.wait_ge(hg_done, h + 1)
            sp.wait_ge(lru_done, h + 1)
            sp.dma_start(lru_out[h], ef[:]).then_inc(st_out, 16)

        for b in W_ORDER:
            weights(0, b)
        sp.wait_ge(s_c, 2)
        params(0)
        with sp.Fori(0, HEADS - 1) as h:
            for b in W_ORDER:
                sp.wait_ge(z_ready, h * ZC + (b + 1) * NCH)
                weights(h + 1, b)
            results(h)
            params(h + 1)
            wait_alone(sp, st_out, (h + 1) * 48)
        results(HEADS - 1)
        stage_b_sp(sp)

    @block.gpsimd
    def _(pool):
        ch = Chain(pool, s_ms)
        ch(nc.gpsimd.memset(ones[:], 1.0))
        keep = dict(fill=0.0)
        ch(nc.gpsimd.affine_select(out=mask_f[:], in_=ones[:], compare_op=ALU.is_ge, fill=0.0, base=0,
                                   pattern=[[1, P]], channel_multiplier=-1))
        ch(nc.gpsimd.affine_select(out=mask_b[:], in_=ones[:], compare_op=ALU.is_ge, fill=0.0, base=0,
                                   pattern=[[-1, P]], channel_multiplier=1))
        ch(nc.gpsimd.affine_select(out=ident[:], in_=mask_f[:], compare_op=ALU.is_ge, fill=0.0, base=0,
                                   pattern=[[-1, P]], channel_multiplier=1))
        for m in (mask_f, mask_b):
            v = m[:].rearrange("p (c t) -> p c t", c=CPT)
            ch(nc.gpsimd.affine_select(out=v, in_=v, compare_op=ALU.is_ge, fill=0.0, base=0,
                                       pattern=[[-CHUNK, CPT], [0, CHUNK]], channel_multiplier=1))
            ch(nc.gpsimd.affine_select(out=v, in_=v, compare_op=ALU.is_ge, fill=0.0, base=CHUNK - 1,
                                       pattern=[[CHUNK, CPT], [0, CHUNK]], channel_multiplier=-1))
        nc.gpsimd.memset(zero[:], 0.0)
        nc.gpsimd.memset(eps[:], EPS).then_inc(s_c, 1)
        ch(nc.gpsimd.memset(AR[:, A_ATT:A_SM], 0.0))
        ch(nc.gpsimd.memset(AR[:, A_SM:A_WRI], 1.0))
        ch(nc.gpsimd.memset(SM.rearrange("p (n c) -> p n c", c=CHUNK)[:, :, 0:1], 0.0))
        nc.gpsimd.memset(AR[:, A_WRI:A_S0], 0.0).then_inc(s_c, 1)
        stage_b_pool(pool)

    @block.tensor
    def _(pe):
        pe.wait_ge(s_silu, 1)
        for c in range(MODC):
            pe.wait_ge(l_mw[c % 2], 16 * (c // 2 + 1))
            if c >= 2:
                pe.wait_ge(m_evac, c - 1)
            for k in range(KD):
                mm = nc.tensor.matmul(PS[0:2, c % 2, :], cs[:, k, :], WMOD[:, c % 2, k, :],
                                      start=(k == 0), stop=(k == KD - 1))
            mm.then_inc(m_ready, 1)
        pe.wait_ge(s_c, 1)
        pe.wait_ge(m_evac, MODC)
        for n in range(2 * KD):
            mm = nc.tensor.transpose(PS[:, 2, 2 * n:2 * n + 2], MROW[:, n * P:(n + 1) * P], ident[0:2, 0:2])
        mm.then_inc(t_ready, 1)
        for k in range(KD):
            pe.wait_ge(sq_r, k + 1)
            for n in range(NCH):
                mm = nc.tensor.matmul(PS[:, 3 + n, 0:CH], ones[:], SQ[k % 2][:, n * CH:(n + 1) * CH],
                                      start=(k == 0), stop=(k == KD - 1))
            mm.then_inc(ssq_r, 1)

        pe.wait_ge(h_ready, KD)
        with pe.Fori(0, HEADS) as h:
            def z_bank(b, n, rel=False):
                c = b * NCH + n
                if c >= NCH:
                    pe.wait_ge(z_free, h * ZC + c - NCH + 1)
                return PS[:, n, 0:CH]

            for b in range(NB):
                pe.wait_ge(l_w[b], h * 16 + 16)
                for n in range(NCH):
                    z = z_bank(b, n)
                    if b == B_V:
                        for u in range(CH // P):
                            t = n * (CH // P) + u
                            for k in range(KD):
                                mm = nc.tensor.matmul(z[:, u * P:(u + 1) * P], hT[:, k, t * P:(t + 1) * P],
                                                      W[:, b, k, :], start=(k == 0), stop=(k == KD - 1))
                    else:
                        for k in range(KD):
                            mm = nc.tensor.matmul(z, W[:, b, k, :], hT[:, k, n * CH:(n + 1) * CH],
                                                  start=(k == 0), stop=(k == KD - 1))
                    mm.then_inc(z_ready, 1)

            pe.wait_ge(xc_r, h + 1)
            pe.wait_ge(l_par, h * 64 + 64)
            for g in range(4):
                for n in range(NCH):
                    z = z_bank(B_GATES + g, n)
                    nc.tensor.matmul(z, WRI[:, g, :], XC[:, n * CH:(n + 1) * CH],
                                     start=True, stop=True).then_inc(z_ready, 1)

            def scores(it):
                d, tt = it // TILES, tile_of(it)
                if it % TILES == 0:
                    pe.wait_ge(k_r[d], h + 1)
                sl = slice(tt * P, (tt + 1) * P)
                nc.tensor.transpose(PS[:, 3, 0:P], KE[d][:, sl], ident[:]).then_inc(ket_r, 1)
                if it:
                    pe.wait_ge(att_m, h * TI + it)
                nc.tensor.matmul(PS[:, 4, 0:P], KI[d][:, sl], QD[d][:, sl],
                                 start=True, stop=True).then_inc(att_r, 1)
                pe.wait_ge(ket_e, h * TI + it + 1)
                for j in range(CPT):
                    mm = nc.tensor.matmul(PS[:, 5 + it % 2, j * P:(j + 1) * P], KET[:, it % 2, j, :],
                                          Vt[:, tt, :], start=True, stop=True)
                mm.then_inc(ds_r, 1)

            def outputs(it):
                d, tt = it // TILES, tile_of(it)
                pe.wait_ge(att_m, h * TI + it + 1)
                if it:
                    pe.wait_ge(o_a, h * TI + it)
                nc.tensor.matmul(PS[:, 7, 0:P], Vt[:, tt, :], ATT[:, d, it % 2, :], start=True, stop=False)
                for jj in range(CPT):
                    j = jj if d == 0 else CPT - 1 - jj
                    st, cnt = state_of(it, jj)
                    if cnt is not None:
                        pe.wait_ge(s_r, h * NSU + cnt)
                    c = slice(tt * P + j * CHUNK, tt * P + (j + 1) * CHUNK)
                    mm = nc.tensor.matmul(PS[:, 7, j * CHUNK:(j + 1) * CHUNK], st, QD[d][:, c],
                                          start=False, stop=(jj == CPT - 1))
                mm.then_inc(o_r, 1)

            scores(0)
            for it in range(TI):
                if it + 1 < TI:
                    scores(it + 1)
                outputs(it)
            for n in range(NCH):
                pe.wait_ge(osq_r, h * NCH + n + 1)
                z = z_bank(B_SSQ, n)
                nc.tensor.matmul(z, ones[:], K[1][:, n * CH:(n + 1) * CH], start=True, stop=True)\
                    .then_inc(z_ready, 1)
            pe.wait_ge(z_free, (h + 1) * ZC)
        stage_b_pe(pe)

    @block.scalar
    def _(act):
        A = nc.scalar.activation
        act.wait_ge(l_c, 32)
        A(cs[:], cs[:], ACT.Silu).then_inc(s_silu, 1)
        act.wait_ge(l_x, 16)
        for k in range(KD):
            if k >= 2:
                act.wait_ge(ssq_r, k - 1)
            A(SQ[k % 2], hT[:, k, :], ACT.Square).then_inc(sq_r, 1)
        act.wait_ge(ssq_r, KD)
        act.wait_ge(s_c, 1)
        for n in range(NCH):
            last = A(RS[:, n * CH:(n + 1) * CH], PS[:, 3 + n, 0:CH], ACT.Sqrt, bias=eps[:], scale=1.0 / D)
        last.then_inc(sd_r, 1)
        act.wait_ge(h_ready, KD)

        act.wait_ge(s_c, 2)
        with act.Fori(0, HEADS) as h:
            def evac(b, n, out, func, in_=None, **kw):
                act.wait_ge(z_ready, h * ZC + b * NCH + n + 1)
                return A(out, PS[:, n, 0:CH] if in_ is None else in_, func, **kw)

            def block_out(b, out, func, **kw):
                for n in range(NCH):
                    evac(b, n, out[:, n * CH:(n + 1) * CH], func, **kw).then_inc(z_free, 1)

            act.wait_ge(pa[0], h + 1)
            A(ps_[:, 8:12], ps_[:, 4:8], ACT.Exp)
            A(ps_[:, 16:18], ps_[:, 14:16], ACT.Exp, scale=-1.0).then_inc(pa[1], 1)
            act.wait_ge(pa[2], h + 1)
            A(ps_[:, 20:22], ps_[:, 18:20], ACT.Ln).then_inc(pa[3], 1)
            block_out(B_FF, SG[0], ACT.Sigmoid)
            block_out(B_Q, Q, ACT.Silu)
            act.wait_ge(f_r[0], h + 1)
            A(SG[0], SG[0], ACT.Ln).then_inc(lf_r[0], 1)
            block_out(B_FB, SG[1], ACT.Sigmoid)

            def exps(d):
                act.wait_ge(cum_r[d], h + 1)
                A(QD[d], CUM, ACT.Exp)
                A(KI[d], CUM, ACT.Exp, scale=-1.0)
                e = CHUNK - 1 if d == 0 else 0
                ends = CUM.rearrange("p (c t) -> p c t", t=CHUNK)[:, :, e]
                A(dec[:, d, :], ends, ACT.Exp).then_inc(e_r[d], 1)
                act.wait_ge(tc_r[d], h + 1)
                A(KE[d], KE[d], ACT.Exp).then_inc(e3_r[d], 1)

            act.wait_ge(f_r[1], h + 1)
            A(SG[1], SG[1], ACT.Ln).then_inc(lf_r[1], 1)
            exps(0)
            xl = XR[:, N_CTX + 5:N_CTX + 5 + N_LAT].rearrange("p (c r) -> p r c", r=GRID_H)
            evac(B_XR, 0, XR[:, 2:2 + N_CTX], ACT.Copy, in_=PS[:, 0, 0:N_CTX])
            r0 = 0
            for n in range(NCH):
                lo = N_CTX if n == 0 else 0
                rows = (CH - lo) // GRID_W
                src = PS[:, n, lo:CH].rearrange("p (r c) -> p r c", c=GRID_W)
                evac(B_XR, n, xl[:, r0:r0 + rows, :], ACT.Copy, in_=src).then_inc(z_free, 1)
                r0 += rows
            block_out(B_G, oA[:, h, :], ACT.Silu)
            exps(1)
            block_out(B_V, V, ACT.Copy)
            block_out(B_XG, hB[:, h, :], ACT.Gelu_apprx_tanh)
            act.wait_ge(pa[4], h + 1)
            for d in range(2):
                for g, out, bias in ((0, R[d], P_BR), (1, I[d], P_BI)):
                    block_out(B_GATES + 2 * d + g, out, ACT.Sigmoid, bias=pr[:, bias + d:bias + d + 1])
            act.wait_ge(z_free, h * ZC + B_SSQ * NCH)
            for d in range(2):
                A(R[d], R[d], ACT.Tanh, scale=ps_[:, 34 + d:35 + d]).then_inc(s_act, 1)
            act.wait_ge(s_act, h * 2 + 2)
            for d in range(2):
                A((CUM, SG[1])[d], R[d], ACT.Sqrt).then_inc(t2_r[d], 1)
            for it in range(TI):
                act.wait_ge(ket_r, h * TI + it + 1)
                if it >= 2:
                    act.wait_ge(ds_r, h * TI + it - 1)
                for j in range(CPT):
                    rows = slice(j * CHUNK, (j + 1) * CHUNK)
                    cp = A(KET[rows, it % 2, j, :], PS[rows, 3, 0:P], ACT.Copy)
                cp.then_inc(ket_e, 1)
            block_out(B_SSQ, QD[0], ACT.Sqrt, bias=eps[:], scale=1.0 / P)
            act.wait_ge(hg_done, h + 1)
            act.wait_ge(lru_done, h + 1)
        stage_b_act(act)

    @block.vector
    def _(dve):
        v = nc.vector
        ch = Chain(dve, s_dv)
        dve.wait_ge(l_b, 16)
        for c in range(MODC):
            dve.wait_ge(m_ready, c + 1)
            sl = slice(c * 512, (c + 1) * 512)
            v.tensor_tensor(MROW[:, sl], PS[0:2, c % 2, :], BROW[:, sl], ALU.add).then_inc(m_evac, 1)
        dve.wait_ge(t_ready, 1)
        mt = PS[:, 2, 0:4 * KD].rearrange("p (s k c) -> p s k c", s=2, c=2)
        v.tensor_copy(sh1[:], mt[:, 0])
        ch(v.tensor_scalar(w1[:], mt[:, 1], 1.0, None, ALU.add))
        ch(v.tensor_tensor(w1[:], w1[:], n1[:].unsqueeze(2).to_broadcast([P, KD, 2]), ALU.mult))
        dve.wait_ge(sd_r, 1)
        ch(v.reciprocal(RS, RS))
        for k in range(KD):
            for s, sl in enumerate((slice(0, N_CTX), slice(N_CTX, T))):
                ins = v.scalar_tensor_tensor(out=hT[:, k, sl], in0=hT[:, k, sl], scalar=w1[:, k, s:s + 1],
                                             in1=RS[:, sl], op0=ALU.mult, op1=ALU.mult)
                if s == 1:
                    ch(ins)
            for s, sl in enumerate((slice(0, N_CTX), slice(N_CTX, T))):
                ins = v.tensor_scalar(hT[:, k, sl], hT[:, k, sl], sh1[:, k, s:s + 1], None, ALU.add)
            ins.then_inc(h_ready, 1)
        base = ch.n
        dve.wait_ge(s_c, 2)
        per_head = DVE_HEAD
        with dve.Fori(0, HEADS) as h:
            ch = Chain(dve, s_dv, base + h * per_head)
            dve.wait_ge(l_par, h * 64 + 64)
            lg = pr[:, P_LB:P_LB + 4].rearrange("p (d l) -> p d l", d=2)
            ch(v.tensor_tensor(ps_[:, 0:2], lg[:, :, 0], lg[:, :, 1], ALU.max))
            v.tensor_tensor(ps_[:, 4:8].rearrange("p (d l) -> p d l", d=2), lg,
                            ps_[:, 0:2].unsqueeze(2).to_broadcast([P, 2, 2]), ALU.subtract)
            lam = pr[:, P_LAM:P_LAM + 2]
            v.scalar_tensor_tensor(out=ps_[:, 14:16], in0=lam, scalar=-1.0, in1=lam, op0=ALU.mult,
                                   op1=ALU.max).then_inc(pa[0], 1)
            dve.wait_ge(pa[1], h + 1)
            ex = ps_[:, 8:12].rearrange("p (d l) -> p d l", d=2)
            v.tensor_scalar(ps_[:, 18:20], ps_[:, 16:18], 1.0, None, ALU.add).then_inc(pa[2], 1)
            ch(v.tensor_tensor(ps_[:, 2:4], ex[:, :, 0], ex[:, :, 1], ALU.add))
            ch(v.reciprocal(ps_[:, 2:4], ps_[:, 2:4]))
            ch(v.tensor_tensor(ps_[:, 24:26], ex[:, :, 0], ps_[:, 2:4], ALU.mult))
            v.tensor_scalar(ps_[:, 26:28], ps_[:, 24:26], -1.0, 1.0, ALU.mult, ALU.add)
            ch(v.tensor_scalar(ps_[:, 22:24], ps_[:, 18:20], -1.0, None, ALU.add))
            ch(v.tensor_scalar(ps_[:, 28:30], ps_[:, 22:24], 0.0, None, ALU.is_equal))
            ch(v.tensor_tensor(ps_[:, 22:24], ps_[:, 22:24], ps_[:, 28:30], ALU.add))
            ch(v.reciprocal(ps_[:, 22:24], ps_[:, 22:24]))
            dve.wait_ge(pa[3], h + 1)
            ch(v.tensor_tensor(ps_[:, 20:22], ps_[:, 20:22], ps_[:, 28:30], ALU.add))
            ch(v.tensor_tensor(ps_[:, 20:22], ps_[:, 20:22], ps_[:, 22:24], ALU.mult))
            ch(v.tensor_tensor(ps_[:, 20:22], ps_[:, 20:22], ps_[:, 16:18], ALU.mult))
            ch(v.tensor_scalar(ps_[:, 30:32], lam, -1.0, 0.0, ALU.mult, ALU.max))
            ch(v.tensor_tensor(ps_[:, 20:22], ps_[:, 20:22], ps_[:, 30:32], ALU.add))
            v.tensor_scalar(ps_[:, 34:36], ps_[:, 20:22], LRU_C / 2, None, ALU.mult).then_inc(pa[4], 1)

            def forget(d):
                dve.wait_ge(z_free, h * ZC + NCH * ((B_FF, B_FB)[d] + 1))
                ch(v.tensor_scalar(SG[d], SG[d], ps_[:, 26 + d:27 + d], ps_[:, 24 + d:25 + d],
                                   ALU.mult, ALU.add))
                v.tensor_scalar(K[d], SG[d], -1.0, 1.0, ALU.mult, ALU.add).then_inc(f_r[d], 1)

            def sums(d):
                dve.wait_ge(lf_r[d], h + 1)
                if d:
                    dve.wait_ge(e_r[0], h + 1)
                if d == 0:
                    ins = v.tensor_tensor_scan(CUM, SM[:, 0:T], SG[0], 0.0, ALU.mult, ALU.add)
                else:
                    ins = v.tensor_tensor_scan(CUM[:, ::-1], SM[:, 1:T + 1][:, ::-1], SG[1][:, ::-1], 0.0,
                                               ALU.mult, ALU.add)
                ins.then_inc(cum_r[d], 1)
                dve.wait_ge(cum_r[d], h + 1)
                cv = CUM.rearrange("p (c t) -> p c t", t=CHUNK)
                e = CHUNK - 1 if d == 0 else 0
                v.tensor_tensor(KE[d].rearrange("p (c t) -> p c t", t=CHUNK),
                                cv[:, :, e:e + 1].to_broadcast([P, NCK, CHUNK]), cv,
                                ALU.subtract).then_inc(tc_r[d], 1)

            def keys_(d):
                dve.wait_ge(e_r[d], h + 1)
                if d == 0:
                    dve.wait_ge(z_free, h * ZC + NCH * (B_Q + 1))
                v.tensor_tensor(QD[d], QD[d], Q, ALU.mult)
                v.tensor_tensor(KI[d], KI[d], K[d], ALU.mult)
                dve.wait_ge(e3_r[d], h + 1)
                v.tensor_tensor(KE[d], KE[d], K[d], ALU.mult).then_inc(k_r[d], 1)

            forget(0)
            sums(0)
            forget(1)
            keys_(0)
            sums(1)
            for a, n in ((0, 2), (N_CTX + 2, 3), (N_CTX + 5 + N_LAT, 1)):
                last = v.memset(XR[:, a:a + n], 0.0)
            ch(last)
            dve.wait_ge(z_free, h * ZC + NCH * (B_XR + 1))
            for j in range(4):
                for a, o, n in ((0, 0, N_CTX), (N_CTX + 3, N_CTX, N_LAT)):
                    xs, xo = XR[:, a + j:a + j + n], XC[:, o:o + n]
                    cw = pr[:, P_CW + j:P_CW + j + 1]
                    if j == 0:
                        ins = v.tensor_scalar(xo, xs, cw, pr[:, P_CB:P_CB + 1], ALU.mult, ALU.add)
                    else:
                        ins = v.scalar_tensor_tensor(out=xo, in0=xs, scalar=cw, in1=xo, op0=ALU.mult,
                                                     op1=ALU.add)
                if j < 3:
                    ch(ins)
                else:
                    ins.then_inc(xc_r, 1)
            keys_(1)

            for d in range(2):
                root = (CUM, SG[1])[d]
                dve.wait_ge(t2_r[d], h + 1)
                v.tensor_tensor(I[d], I[d], XC, ALU.mult)
                ch(v.tensor_scalar(SG[0], R[d], -1.0, -1.0, ALU.mult, ALU.add))
                ch(v.reciprocal(SG[0], SG[0]))
                v.scalar_tensor_tensor(out=R[d], in0=R[d], scalar=1.0, in1=SG[0], op0=ALU.subtract, op1=ALU.mult)
                ch(v.scalar_tensor_tensor(out=root, in0=root, scalar=-2.0, in1=SG[0], op0=ALU.mult, op1=ALU.mult))
                ch(v.tensor_tensor(I[d], I[d], root, ALU.mult))
                for a, n, first in ((0, N_CTX, 0.0), (N_CTX, N_LAT, pr[:, P_H0 + d:P_H0 + d + 1])):
                    views = [x[:, a:a + n] for x in (I[d], R[d])]
                    if d:
                        views = [x[:, ::-1] for x in views]
                    ins = v.tensor_tensor_scan(views[0], views[1], views[0], first, ALU.mult, ALU.add)
                ch(ins)
            v.tensor_copy(ef[:, 0:1], I[0][:, N_CTX - 1:N_CTX])
            ch(v.tensor_copy(ef[:, 1:2], I[1][:, 0:1]))
            ch(v.tensor_tensor(I[0], I[0], I[1], ALU.add))
            hc = hB[:, h, 0:N_CTX]
            v.tensor_tensor(hc, hc, I[0][:, 0:N_CTX], ALU.mult)
            hl = hB[:, h, N_CTX:T].rearrange("p (r c) -> p r c", c=GRID_W)
            v.tensor_tensor(hl, hl, I[0][:, N_CTX:T].rearrange("p (c r) -> p r c", r=GRID_H),
                            ALU.mult).then_inc(lru_done, 1)

            O, OS = K[0], K[1]

            def out_of(it):
                tt = tile_of(it)
                dve.wait_ge(o_r, h * TI + it + 1)
                o = O[:, tt * P:(tt + 1) * P]
                if it < TILES:
                    v.tensor_copy(o, PS[:, 7, 0:P]).then_inc(o_a, 1)
                else:
                    v.tensor_tensor(o, PS[:, 7, 0:P], o, ALU.add).then_inc(o_a, 1)

            for it in range(TI):
                d, tt = it // TILES, tile_of(it)
                wait_alone(dve, att_r, h * TI + it + 1)
                v.copy_predicated(ATT[:, d, it % 2, :], (mask_f, mask_b)[d][:].bitcast(I32),
                                  PS[:, 4, 0:P]).then_inc(att_m, 1)
                dve.wait_ge(ds_r, h * TI + it + 1)
                for jj in range(CPT):
                    if (it, jj) not in writes:
                        continue
                    j = jj if d == 0 else CPT - 1 - jj
                    st, cnt = reads[it, jj]
                    to, k, final = writes[it, jj]
                    if cnt is not None:
                        dve.wait_ge(s_r, h * NSU + cnt)
                    c = tt * CPT + j
                    ins = v.scalar_tensor_tensor(out=to, in0=st, scalar=dec[:, d, c:c + 1],
                                                 in1=PS[:, 5 + it % 2, j * P:(j + 1) * P],
                                                 op0=ALU.mult, op1=ALU.add)
                    ins.then_inc(s_r, 1)
                if it:
                    out_of(it - 1)
            out_of(TI - 1)
            dve.wait_ge(o_a, h * TI + TI)
            for n in range(NCH):
                sl = slice(n * CH, (n + 1) * CH)
                v.tensor_tensor(OS[:, sl], O[:, sl], O[:, sl], ALU.mult).then_inc(osq_r, 1)
            dve.wait_ge(z_free, (h + 1) * ZC)
            ch(v.reciprocal(QD[0], QD[0]))
            ch(v.scalar_tensor_tensor(out=O, in0=O, scalar=pr[:, P_HN:P_HN + 1], in1=QD[0], op0=ALU.mult,
                                      op1=ALU.mult))
            v.tensor_tensor(oA[:, h, :], oA[:, h, :], O, ALU.mult).then_inc(hg_done, 1)
            assert ch.n == per_head, ch.n
        stage_b_dve(dve)
    ctx.close()


def layout(x_prompt, x_sample, state_hgrn, state_rglru, c, c_ctx, w_mod, b_mod, norm1, w_in,
           hg_lb_logits, hg_norm, lru_conv_w, lru_conv_b, lru_w_r, lru_b_r, lru_w_i, lru_b_i,
           lru_lambda, w_branch_a, w_branch_b, w_out, norm2, pk_w_q, pk_sub_keys, pk_u, pk_v, norm_f):
    cat, cg = np.concatenate, np.ascontiguousarray
    x = cat([x_prompt[0], x_sample[0]], axis=0)
    blocks = lambda w: w.reshape(w.shape[0] // P, P, w.shape[1] // P, P).transpose(2, 1, 0, 3)
    wi = blocks(w_in[0])
    q, ff, fb, v, g, xr, xg = (wi[4 * n:4 * n + 4] for n in range(7))
    ga, gb = wi[28:36], wi[36:44]
    per = lambda a: a.reshape(a.shape[0], HEADS, P).transpose(1, 2, 0)
    lb = hg_lb_logits.transpose(2, 0, 1).reshape(HEADS, P, 4)
    par = cat([lb, per(lru_conv_w[0]), per(lru_conv_b), per(lru_b_r[0]), per(lru_b_i[0]), per(lru_lambda[0]),
               np.broadcast_to(hg_norm[0][None, :, None], (HEADS, P, 1)),
               per(state_rglru[0, 0])], axis=2)
    gate_w = np.stack([lru_w_r[0, 0], lru_w_i[0, 0], lru_w_r[0, 1], lru_w_i[0, 1]])
    return {
        "xT": cg(x.T.reshape(KD, P, T).transpose(1, 0, 2)),
        "x_tok": x.reshape(TILES, P, D),
        "cT": cg(np.stack([c_ctx, c[0]], axis=1).reshape(KD, P, 2).transpose(1, 0, 2)),
        "w_mod": cg(w_mod[0].reshape(KD, P, MODC, 512).transpose(2, 1, 0, 3)),
        "b_mod": cg(np.broadcast_to(b_mod[0], (2, MODW))),
        "n1T": cg(norm1[0].reshape(KD, P).T),
        "w_in": cg(np.stack([ff, q, fb, xr, g, v, xg], axis=1)),
        "par": cg(par),
        "wri": cg(gate_w.reshape(4, HEADS, 2, 64, 64).transpose(1, 2, 3, 0, 4)),
        "s0": cg(state_hgrn[0, 0].transpose(1, 2, 0, 3)),
        "w_mg": cg(cat([ga, gb, blocks(w_branch_a[0]), blocks(w_branch_b[0])], axis=2)),
        "w_out": cg(w_out[0].reshape(KD, P, D).transpose(1, 0, 2)),
        "n2": norm2[0],
        "nf": norm_f,
        "w_q": cg(pk_w_q[0].reshape(KD, P, 2 * D).transpose(1, 0, 2)),
        "keys": cg(pk_sub_keys[0].transpose(3, 1, 0, 2).reshape(P, 16 * P)),
        "uv": cg(cat([pk_u[0], pk_v[0]], axis=1)),
    }


_OUTS = {"y_out": (TILES, P, D), "hg_out": (2, HEADS, P, P), "lru_out": (HEADS, P, 2)}


def make(nc, shapes):
    args = [nc.dram_tensor(f"in_{n}", s, F32, kind="ExternalInput").ap() for n, s in shapes.items()]
    args += [nc.dram_tensor(f"out_{n}", s, F32, kind="ExternalOutput").ap() for n, s in _OUTS.items()]
    args.append(nc.dram_tensor("mod_scratch", (2, MODW), F32).ap())
    args.append(nc.dram_tensor("x1_scratch", (TILES, P, D), F32).ap())
    build(nc, *args)


def kernel(**inputs):
    import concourse.bacc as _bacc
    from concourse.bass_utils import run_bass_kernel_spmd as _run

    arrays = layout(**{k: np.asarray(a) for k, a in inputs.items()})
    nc = _bacc.Bacc("TRN2", target_bir_lowering=False, num_devices=1)
    make(nc, {n: a.shape for n, a in arrays.items()})
    r = _run(nc, [{f"in_{n}": a for n, a in arrays.items()}], core_ids=[0])
    y, hg, lru = (r.results[0][f"out_{n}"] for n in _OUTS)
    y = y.reshape(T, D)
    return (y[None, :N_CTX], y[None, N_CTX:], hg[None, None],
            np.ascontiguousarray(lru.transpose(2, 0, 1)).reshape(1, 1, 2, HEADS * P))
```

```python
from contextlib import ExitStack

import numpy as np
import concourse.bass as bass
from concourse import mybir

ALU = mybir.AluOpType
ACT = mybir.ActivationFunctionType
F32 = mybir.dt.float32
I32 = mybir.dt.int32
U32 = mybir.dt.uint32
AX_X = mybir.AxisListType.X

P = 128
D = 1024
KD = D // P
N_CTX = 128
N_LAT = 1024
T = N_CTX + N_LAT
TILES = T // P
NCH = 3
CH = T // NCH
GRID_W = 64
GRID_H = N_LAT // GRID_W
EPS = 1e-6
HEADS = 4
CHUNK = 32
CPT = P // CHUNK
NCK = T // CHUNK
LRU_C = 8.0
MODW = 6 * D
MODC = MODW // 512
PK_HEADS = 8
TOPK = 16
NKEYS = 128
NEG = -3.0e38
RING = 8
ROUNDS = PK_HEADS * TOPK // RING
PAIRS = PK_HEADS // 2
RPP = ROUNDS // PAIRS
DVE_HEAD = 33
GRP = 2

P_LB, P_CW, P_CB, P_BR, P_BI, P_LAM, P_HN, P_H0, NPAR = 0, 4, 8, 9, 11, 13, 15, 16, 18

B_FF, B_Q, B_FB, B_XR, B_G, B_V, B_XG = range(7)
NB = 7
B_GATES = NB
B_SSQ = NB + 4
ZC = (NB + 5) * NCH
TI = 2 * TILES

A_HT = 0
A_OA = A_HT + KD * T
A_HB = A_OA + HEADS * T
A_W = A_HB + HEADS * T
A_BUF = A_W + NB * D
XR_W = T + 8
A_S = A_BUF + 17 * T + XR_W
NS = 12
A_ATT = A_S + NS * P
A_KET = A_ATT + 4 * P
A_SM = A_KET + 2 * CPT * P
A_WRI = A_SM + T + CHUNK
A_S0 = A_WRI + 4 * P
A_SF = A_S0 + 2 * P
A_END = A_SF + 2 * P
A_MG = A_BUF
A_WM = A_MG + KD * T
WM = 24 * P
A_SIG = A_WM + 2 * WM
A_WO = A_SIG + 4 * CH
A_X = A_WM
A_WQ = 0
A_KEY = A_WQ + 16 * D
A_RING = A_W
A_B = A_RING + RING * 2 * D
assert A_KEY + 16 * P <= A_RING and A_WO + KD * D <= A_END and A_X + 6 * D <= A_SIG
assert A_B >= A_WM - 8


def wait_alone(eng, sem, value):
    eng.wait_ge(sem, value)
    eng.nop(nofuse=True)


class Chain:

    def __init__(self, eng, sem, base=0):
        self.eng, self.sem, self.base, self.n = eng, sem, base, 0

    def __call__(self, ins, alone=False):
        self.n += 1
        ins.then_inc(self.sem, 1)
        if alone:
            wait_alone(self.eng, self.sem, self.base + self.n)
        else:
            self.eng.wait_ge(self.sem, self.base + self.n)


def build(nc, xT, x_tok, cT, w_mod, b_mod, n1T, w_in, par, wri, s0, w_mg, w_out, n2, nf, w_q, keys,
          uv, y_out, hg_out, lru_out, mod_d, x1_d):
    ctx = ExitStack()
    sb = lambda name, shape, dt=F32: nc.alloc_sbuf_tensor(name, shape, dt)
    sem = lambda name: nc.alloc_semaphore(name)

    AR = sb("arena", [P, A_END])
    ident = sb("ident", [P, P])
    ones = sb("ones", [P, P])
    zero = sb("zero", [P, P])
    mask_f = sb("mask_f", [P, P])
    mask_b = sb("mask_b", [P, P])
    cs = sb("cs", [P, KD, 2])
    n1 = sb("n1", [P, KD])
    sh1 = sb("sh1", [P, KD, 2])
    w1 = sb("w1", [P, KD, 2])
    eps = sb("eps", [P, 1])
    pr = sb("pr", [P, NPAR])
    ps_ = sb("ps_", [P, 40])
    dec = sb("dec", [P, 2, NCK])
    ef = sb("ef", [P, 2])
    PS = nc.alloc_psum_tensor("ps", [P, 8, 512], F32)

    hT = AR[:, A_HT:A_OA].rearrange("p (k t) -> p k t", k=KD)
    oA = AR[:, A_OA:A_HB].rearrange("p (k t) -> p k t", k=HEADS)
    hB = AR[:, A_HB:A_W].rearrange("p (k t) -> p k t", k=HEADS)
    W = AR[:, A_W:A_BUF].rearrange("p (b k c) -> p b k c", b=NB, k=KD)
    buf = lambda n: AR[:, A_BUF + n * T:A_BUF + (n + 1) * T]
    Q, SG, K, CUM = buf(0), [buf(1), buf(2)], [buf(3), buf(4)], buf(5)
    QD, KI, KE = [buf(6), buf(7)], [buf(8), buf(9)], [buf(10), buf(11)]
    V, XC, R, I = buf(12), buf(13), [buf(14), buf(15)], [buf(16), AR[:, A_BUF + 17 * T + 0:A_BUF + 17 * T + 0 + T]]
    XR = AR[:, A_BUF + 17 * T:A_BUF + 17 * T + XR_W]
    S = AR[:, A_S:A_ATT].rearrange("p (n v) -> p n v", n=NS)
    ATT = AR[:, A_ATT:A_KET].rearrange("p (d n t) -> p d n t", d=2, n=2)
    KET = AR[:, A_KET:A_SM].rearrange("p (n j k) -> p n j k", n=2, j=CPT)
    SM = AR[:, A_SM:A_WRI]
    WRI = AR[:, A_WRI:A_S0].rearrange("p (g c) -> p g c", g=4)
    S0 = AR[:, A_S0:A_SF].rearrange("p (d v) -> p d v", d=2)
    SF = AR[:, A_SF:A_END].rearrange("p (d v) -> p d v", d=2)
    WMOD = AR[:, A_BUF:A_BUF + 2 * 4096].rearrange("p (n k c) -> p n k c", n=2, k=KD)
    MROW = AR[0:2, A_BUF + 8192:A_BUF + 8192 + MODW]
    BROW = AR[0:2, A_BUF + 8192 + MODW:A_BUF + 8192 + 2 * MODW]
    SQ = [AR[:, A_W + n * T:A_W + (n + 1) * T] for n in range(2)]
    RS = AR[:, A_W + 2 * T:A_W + 3 * T]
    Vt = V.rearrange("p (t v) -> p t v", t=TILES)

    s_c, s_ms = sem("consts_ready"), sem("consts_step")
    l_x, l_c, l_b, s_silu = sem("l_x"), sem("l_c"), sem("l_b"), sem("silu_ready")
    l_mw = [sem("l_mw0"), sem("l_mw1")]
    m_ready, m_evac, s_dv = sem("mod_ready"), sem("mod_evac"), sem("dve_chain")
    s_act = sem("act_chain")
    t_ready, w1_ready = sem("modT_ready"), sem("w1_ready")
    sq_r, ssq_r, sd_r, h_ready = sem("square_ready"), sem("ssq_ready"), sem("sd_ready"), sem("h_ready")
    md_out = sem("mod_written")
    l_w = [sem(f"l_w{b}") for b in range(NB)]
    l_par = sem("l_par")
    z_ready, z_free = sem("z_ready"), sem("z_free")
    pa = [sem(f"par_{n}") for n in range(6)]
    f_r = [sem("f0_ready"), sem("f1_ready")]
    lf_r = [sem("lf0_ready"), sem("lf1_ready")]
    cum_r = [sem("cum0_ready"), sem("cum1_ready")]
    e_r = [sem("exp0_ready"), sem("exp1_ready")]
    tc_r = [sem("tc0_ready"), sem("tc1_ready")]
    e3_r = [sem("expend0_ready"), sem("expend1_ready")]
    k_r = [sem("kq0_ready"), sem("kq1_ready")]
    xc_r = sem("conv_ready")
    t2_r = [sem("tanh0_ready"), sem("tanh1_ready")]
    lru_done, hg_done = sem("lru_done"), sem("hg_done")
    ket_r, ket_e = sem("ket_ready"), sem("ket_evac")
    att_r, att_m = sem("att_ready"), sem("att_masked")
    ds_r, s_r = sem("ds_ready"), sem("state_ready")
    o_r, o_a = sem("o_ready"), sem("o_added")
    osq_r = sem("osq_ready")
    st_out = sem("state_out")

    W_ORDER = range(NB)
    def tile_of(it):
        return it if it < TILES else TI - 1 - it

    count, reads, writes = 0, {}, {}
    slot = 0
    for it in range(TI):
        d, tt = it // TILES, tile_of(it)
        first_ctx, first_lat = tt == 0, tt == (1 if d == 0 else TILES - 1)
        for jj in range(CPT):
            if jj == 0 and first_ctx:
                cur = (zero[:], None)
            elif jj == 0 and first_lat:
                cur = (S0[:, d, :], None)
            reads[it, jj] = cur
            last_lat = jj == CPT - 1 and tt == (TILES - 1 if d == 0 else 1)
            if last_lat:
                continue
            count += 1
            if jj == CPT - 1 and tt == 0:
                writes[it, jj] = (SF[:, d, :], count, True)
                cur = None
            else:
                writes[it, jj] = (S[:, slot % NS, :], count, False)
                cur = (S[:, slot % NS, :], count)
                slot += 1
    NSU = count
    LAST_CTX = max(k for _, k, final in writes.values() if final)
    state_of = lambda it, jj: reads[it, jj]


    MG = AR[:, A_MG:A_WM].rearrange("p (k t) -> p k t", k=KD)
    WMG = [AR[:, A_WM + n * WM:A_WM + (n + 1) * WM].rearrange("p (b c) -> p b c", c=P) for n in range(2)]
    SIG = [[AR[:, A_SIG + (2 * n + g) * CH:A_SIG + (2 * n + g + 1) * CH] for g in range(2)] for n in range(2)]
    WO = AR[:, A_WO:A_WO + KD * D].rearrange("p (k c) -> p k c", k=KD)
    XT = [AR[:, A_X + n * D:A_X + (n + 1) * D] for n in range(6)]
    l_wm = [sem("l_wm0"), sem("l_wm1")]
    mg_ready, mg_sig, mg_free, mg_ch = sem("merge_ready"), sem("merge_gates"), sem("merged"), sem("merge_step")
    l_wo, l_g1, l_xt = sem("l_wo"), sem("l_g1"), [sem("l_xt0"), sem("l_xt1")]
    mix_r, mix_f, x1_r = sem("mix_ready"), sem("mix_read"), sem("x1_ready")
    x1_st = [sem("x1_st0"), sem("x1_st1")]
    NMG = KD * NCH

    WQ = AR[:, A_WQ:A_WQ + 16 * D].rearrange("p (k c) -> p k c", k=KD)
    KEYS = AR[:, A_KEY:A_KEY + 16 * P]
    RG = AR[:, A_RING:A_B].rearrange("p (s c) -> p s c", s=RING)
    bt = lambda n: AR[:, A_B + n * D:A_B + (n + 1) * D]
    XN, XE, H2N, H2C, H2T_, W2B, SH2B, G2B, NFB, _, QQ, DG_, Y, SC_, CD_, OH_ = [bt(n) for n in range(16)]
    assert A_B + 16 * D <= A_END
    H2T = H2T_.rearrange("p (k t) -> p k t", k=KD)
    QS, QTS = QQ[:, 0:512], QQ[:, 512:1024]
    DG = DG_.rearrange("p (s c) -> p s c", s=RING)
    SCS, SCW = SC_[:, 0:512], SC_[:, 512:1024]
    CAND, CANDW = CD_[:, 0:512], CD_[:, 512:1024]
    OH = [OH_[:, 0:512], OH_[:, 512:1024]]
    small = [A_B + 9 * D]

    def sm(*shape, dt=F32):
        n = int(np.prod(shape))
        ap = AR[:, small[0]:small[0] + n]
        small[0] += n
        assert small[0] <= A_B + 10 * D
        if dt != F32:
            ap = ap.bitcast(dt)
        names = "abc"[:len(shape)]
        return ap if len(shape) == 1 else ap.rearrange(
            f"p ({' '.join(names)}) -> p {' '.join(names)}", **{k: d for k, d in zip(names, shape)})

    EIDX, GATE = sm(2 * P, dt=U32), sm(2 * P)
    IDXS = sm(2, RING, dt=U32)
    iota = sm(TOPK)
    SV, SI, SIF = sm(4, TOPK), sm(4, TOPK, dt=U32), sm(4, TOPK)
    BEST, POS = sm(2, TOPK), sm(2, TOPK, dt=U32)
    PRE, GEL, COEF, st = sm(RING), sm(RING), sm(RING), sm(8)
    PHL = sb("places", [P, 2, 2, TOPK], U32)[:]
    PHF, EE = sb("places_f", [P, 2, 2, TOPK])[:], sb("key_numbers", [P, 2, 2, TOPK])[:]

    l_wq, l_rows, l_rows2, l_g2, l_nf = sem("l_wq"), sem("l_rows"), sem("l_rows_lat"), sem("l_g2"), sem("l_nf")
    l_xn, l_xe = sem("l_xn"), sem("l_xe")
    n_sq, n_sd, h2_r, h2t_r, h2t_e = sem("n_square"), sem("n_sd"), sem("h2_ready"), sem("h2T_ready"), sem("h2T_evac")
    q_r, q_e, qt_r, qt_e, sc_r, sc_e = (sem(x) for x in ("q_ready", "q_evac", "qT_ready", "qT_evac",
                                                         "scores_ready", "scores_evac"))
    top_r, ge_r = sem("top_ready"), sem("gate_exp_ready")
    c_pair, c_front, c_end = sem("pair_step"), sem("front_step"), sem("end_step")
    pair_done, idx_r = sem("pair_done"), sem("round_index_ready")
    gathered = [sem(f"gathered{n}") for n in range(RING)]
    dots, gel_r, coef_r, diag_r, v_used = (sem(x) for x in ("dots", "gelu_ready", "coef_ready", "diag_ready",
                                                            "v_used"))
    acc_free, e_sq, e_sd, y_r, y_st = (sem(x) for x in ("acc_free", "end_square", "end_sd", "y_ready", "y_stored"))
    it_r = sem("iota_ready")
    PAIR_STEPS, FRONT_STEPS, END_STEPS = 16, 2, 2

    def row(ap):
        return ap.partition_broadcast(P)

    def stage_b_sp(sp):
        for n in range(2):
            sp.dma_start(WMG[n], w_mg[n]).then_inc(l_wm[n], 16)
        sp.dma_start(WO, w_out).then_inc(l_wo, 16)
        with sp.Fori(0, KD // 2 - 1) as i:
            for u in range(2):
                sp.wait_ge(mg_ready, i * 2 * NCH + (u + 1) * NCH)
                sp.dma_start(WMG[u], w_mg[2 * i + 2 + u]).then_inc(l_wm[u], 16)
        sp.wait_ge(mg_free, NMG)
        sp.wait_ge(md_out, 16)
        for s in range(2):
            sp.dma_start(XT[4 + s], row(mod_d[s, 2 * D:3 * D])).then_inc(l_g1, 16)
        for t in range(2):
            sp.dma_start(XT[t], x_tok[t]).then_inc(l_xt[t], 16)
        for k in range(4):
            sp.dma_start(WQ[:, 2 * k:2 * k + 2, :], w_q[:, 2 * k:2 * k + 2, :]).then_inc(l_wq, 16)
        sp.dma_start(KEYS, keys).then_inc(l_wq, 16)
        for t in range(TILES):
            sp.wait_ge(x1_r, t + 1)
            sp.dma_start(x1_d[t], XT[2 + t % 2]).then_inc(x1_st[t % 2], 16)
            if t + 2 < TILES:
                sp.dma_start(XT[t % 2], x_tok[t + 2]).then_inc(l_xt[t % 2], 16)
        sp.wait_ge(x1_st[0], 16 * ((TILES + 1) // 2))
        sp.wait_ge(x1_st[1], 16 * (TILES // 2))

        sp.dma_start(XN, x1_d[0]).then_inc(l_xn, 16)
        sp.dma_start(XE, x1_d[0]).then_inc(l_xe, 16)
        sp.dma_start(W2B, row(mod_d[0, 4 * D:5 * D])).then_inc(l_rows, 16)
        sp.dma_start(Y, row(n2)).then_inc(l_rows, 16)
        sp.dma_start(SH2B, row(mod_d[0, 3 * D:4 * D])).then_inc(l_rows, 16)
        sp.dma_start(G2B, row(mod_d[0, 5 * D:6 * D])).then_inc(l_g2, 16)
        sp.dma_start(NFB, row(nf)).then_inc(l_nf, 16)
        sp.wait_ge(h2_r, 1)
        sp.dma_start(W2B, row(mod_d[1, 4 * D:5 * D])).then_inc(l_rows2, 16)
        sp.dma_start(SH2B, row(mod_d[1, 3 * D:4 * D])).then_inc(l_rows2, 16)
        sp.dma_start(XN, x1_d[1]).then_inc(l_xn, 16)

        def tile(t, last):
            if not last:
                sp.wait_ge(h2_r, t + 2)
                sp.dma_start(XN, x1_d[t + 2]).then_inc(l_xn, 16)
            sp.wait_ge(y_r, t + 1)
            sp.dma_start(y_out[t], Y).then_inc(y_st, 16)
            sp.dma_start(XE, x1_d[t + 1]).then_inc(l_xe, 16)

        tile(0, False)
        sp.dma_start(G2B, row(mod_d[1, 5 * D:6 * D])).then_inc(l_g2, 16)
        with sp.Fori(1, TILES - 2) as t:
            tile(t, False)
        tile(TILES - 2, True)
        sp.wait_ge(y_r, TILES)
        sp.dma_start(y_out[TILES - 1], Y).then_inc(y_st, 16)
        sp.wait_ge(y_st, 16 * TILES)
        sp.wait_ge(st_out, 48 * HEADS)

    def stage_b_pool(pool):
        pool.wait_ge(x1_r, TILES)
        nc.gpsimd.iota(iota, pattern=[[1, TOPK]], base=0, channel_multiplier=0,
                       allow_small_or_imprecise_dtypes=True).then_inc(it_r, 1)

        def fetch(r, par_, first=False):
            pool.wait_ge(idx_r, r + 1)
            for s in range(RING):
                if not first:
                    wait_alone(pool, v_used, r * RING + (s + 1 - RING))
                nc.gpsimd.indirect_dma_start(
                    out=RG[:, s, :], out_offset=None, in_=uv,
                    in_offset=bass.IndirectOffsetOnAxis(ap=IDXS[:, par_, s:s + 1], axis=0),
                ).then_inc(gathered[s], 16)

        fetch(0, 0, first=True)
        fetch(1, 1)
        with pool.Fori(0, (TILES * ROUNDS - 2) // 2) as i:
            fetch(i * 2 + 2, 0)
            fetch(i * 2 + 3, 1)

    def stage_b_pe(pe):
        with pe.Fori(0, KD // 2) as i:
            for u in range(2):
                pe.wait_ge(l_wm[u], i * 16 + 16)
                for n in range(NCH):
                    b = 4 * ((u * NCH + n) % 2)
                    sl = slice(n * CH, (n + 1) * CH)
                    for g, (src, w0, nk) in enumerate(((hT, 0, KD), (hT, KD, KD), (oA, 2 * KD, HEADS),
                                                       (hB, 2 * KD + HEADS, HEADS))):
                        for k in range(nk):
                            mm = nc.tensor.matmul(PS[:, b + g, 0:CH], WMG[u][:, w0 + k, :], src[:, k, sl],
                                                  start=(k == 0), stop=(k == nk - 1))
                    mm.then_inc(mg_ready, 1)
                    if u or n:
                        pe.wait_ge(mg_free, i * 2 * NCH + (u * NCH + n))
            wait_alone(pe, mg_free, i * 2 * NCH + 2 * NCH)
        pe.wait_ge(l_wo, 16)
        for t in range(TILES):
            if t >= 2:
                pe.wait_ge(mix_f, t - 1)
            for n in range(2):
                for k in range(KD):
                    mm = nc.tensor.matmul(PS[:, 2 * (t % 2) + n, :], MG[:, k, t * P:(t + 1) * P],
                                          WO[:, k, n * 512:(n + 1) * 512], start=(k == 0), stop=(k == KD - 1))
            mm.then_inc(mix_r, 1)
        pe.wait_ge(mix_f, TILES)
        pe.wait_ge(l_wq, 80)

        def front(tn):
            pe.wait_ge(h2_r, tn + 1)
            for k in range(KD):
                mm = nc.tensor.transpose(PS[:, 2 + k // 4, (k % 4) * P:(k % 4 + 1) * P],
                                         H2N[:, k * P:(k + 1) * P], ident[:])
            mm.then_inc(h2t_r, 1)

        def queries(tn, i, ks):
            if ks[0] == 0:
                wait_alone(pe, h2t_e, tn + 1)
            for k in ks:
                mm = nc.tensor.matmul(PS[:, 4, :], H2T[:, k, :], WQ[:, k, bass.ds(i * 512, 512)],
                                      start=(k == 0), stop=(k == KD - 1))
            if ks[-1] == KD - 1:
                mm.then_inc(q_r, 1)

        def turn(tn, i):
            pe.wait_ge(q_e, tn * PAIRS + i + 1)
            for c in range(4):
                mm = nc.tensor.transpose(PS[:, 5, c * P:(c + 1) * P], QS[:, c * P:(c + 1) * P], ident[:])
            mm.then_inc(qt_r, 1)

        def score(tn, i):
            pe.wait_ge(qt_e, tn * PAIRS + i + 1)
            for c in range(4):
                mm = nc.tensor.matmul(PS[:, 6, c * P:(c + 1) * P], QTS[:, c * P:(c + 1) * P],
                                      KEYS[:, bass.ds(i * 512 + c * P, P)], start=True, stop=True)
            mm.then_inc(sc_r, 1)

        def pair(tn, i):
            queries(tn, i, range(KD))
            turn(tn, i)
            score(tn, i)

        def pair_between(tn, i):
            return {2: lambda: queries(tn, i, range(4)), 3: lambda: queries(tn, i, range(4, KD)),
                    4: lambda: turn(tn, i), 5: lambda: score(tn, i)}

        def rounds(t, i, between):
            for q in range(RPP):
                for s in range(RING):
                    n0 = (t * ROUNDS + i * RPP + q) * RING + s + 1
                    pe.wait_ge(diag_r, n0)
                    for n in range(2):
                        mm = nc.tensor.matmul(PS[:, n, :], DG[:, s, :], RG[:, s, D + n * 512:D + (n + 1) * 512],
                                              start=False, stop=False, skip_group_check=True)
                    mm.then_inc(v_used, 1)
                    at = (q * RING + s + 1) / GRP - 1
                    if at in between:
                        between[at]()

        def tile(t, first=False, last=False):
            if not first:
                pe.wait_ge(acc_free, t)
            for n in range(2):
                nc.tensor.matmul(PS[:, n, :], zero[:], zero[:, 0:1].to_broadcast([P, 512]),
                                 start=True, stop=False, skip_group_check=True)
            rounds(t, 0, {} if last else {1: lambda: front(t + 1)} | pair_between(t + 1, 0))
            with pe.Fori(1, PAIRS) as i:
                rounds(t, i, {} if last else pair_between(t + 1, i))

        front(0)
        with pe.Fori(0, PAIRS) as i:
            pair(0, i)
        tile(0, first=True)
        with pe.Fori(1, TILES - 1) as t:
            tile(t)
        tile(TILES - 1, last=True)

    def stage_b_act(act):
        A = nc.scalar.activation
        with act.Fori(0, KD // 2) as i:
            for u in range(2):
                for n in range(NCH):
                    c = u * NCH + n
                    act.wait_ge(mg_ready, i * 2 * NCH + c + 1)
                    for g in range(2):
                        ins = A(SIG[c % 2][g], PS[:, 4 * (c % 2) + g, 0:CH], ACT.Sigmoid)
                    ins.then_inc(mg_sig, 1)

        def row_norm(tn):
            act.wait_ge(l_xn, tn * 16 + 16)
            A(QQ, XN, ACT.Square, accum_out=st[:, 0:1]).then_inc(n_sq, 1)
            act.wait_ge(n_sq, tn + 1)
            A(st[:, 1:2], st[:, 0:1], ACT.Sqrt, bias=eps[:], scale=1.0 / D).then_inc(n_sd, 1)

        def rows_out(tn):
            act.wait_ge(h2t_r, tn + 1)
            for n in range(2):
                cp = A(H2T_[:, n * 512:(n + 1) * 512], PS[:, 2 + n, :], ACT.Copy)
            cp.then_inc(h2t_e, 1)

        def queries_out(tn, i):
            act.wait_ge(q_r, tn * PAIRS + i + 1)
            A(QS, PS[:, 4, :], ACT.Copy).then_inc(q_e, 1)

        def turned_out(tn, i):
            act.wait_ge(qt_r, tn * PAIRS + i + 1)
            A(QTS, PS[:, 5, :], ACT.Copy).then_inc(qt_e, 1)

        def scores_out(tn, i):
            act.wait_ge(sc_r, tn * PAIRS + i + 1)
            A(SCS, PS[:, 6, :], ACT.Copy).then_inc(sc_e, 1)

        def gates(tn, i):
            act.wait_ge(top_r, tn * PAIRS + i + 1)
            A(BEST, BEST, ACT.Exp).then_inc(ge_r, 1)

        def pair_between(tn, i):
            return {4: lambda: queries_out(tn, i), 5: lambda: turned_out(tn, i), 6: lambda: scores_out(tn, i),
                    14: lambda: gates(tn, i)}

        def rounds(t, i, between):
            for q in range(RPP):
                for g in range(RING // GRP):
                    n = (t * ROUNDS + i * RPP + q) * (RING // GRP) + g
                    act.wait_ge(dots, n + 1)
                    sl = slice(g * GRP, (g + 1) * GRP)
                    A(GEL[:, sl], PRE[:, sl], ACT.Gelu_apprx_tanh).then_inc(gel_r, 1)
                    at = q * (RING // GRP) + g
                    if at in between:
                        between[at]()
                    act.wait_ge(coef_r, n + 1)
                    for s in range(g * GRP, (g + 1) * GRP):
                        A(DG[:, s, :], ident[:], ACT.Copy, scale=COEF[:, s:s + 1]).then_inc(diag_r, 1)

        def end(t):
            act.wait_ge(e_sq, t + 1)
            A(st[:, 3:4], st[:, 2:3], ACT.Sqrt, bias=eps[:], scale=1.0 / D).then_inc(e_sd, 1)

        def tile(t, first=False, last=False):
            between = {}
            if not first:
                between |= {3: lambda: end(t - 1)}
            if not last:
                between |= {0: lambda: row_norm(t + 1), 2: lambda: rows_out(t + 1)} | pair_between(t + 1, 0)
            rounds(t, 0, between)
            with act.Fori(1, PAIRS) as i:
                rounds(t, i, {} if last else pair_between(t + 1, i))

        row_norm(0)
        rows_out(0)
        with act.Fori(0, PAIRS) as i:
            queries_out(0, i)
            turned_out(0, i)
            scores_out(0, i)
            gates(0, i)
        tile(0, first=True)
        with act.Fori(1, TILES - 1) as t:
            tile(t)
        tile(TILES - 1, last=True)
        end(TILES - 1)

    def stage_b_dve(dve):
        v = nc.vector
        with dve.Fori(0, KD // 2) as i:
            for u in range(2):
                for n in range(NCH):
                    c = u * NCH + n
                    dve.wait_ge(mg_sig, i * 2 * NCH + c + 1)
                    for g in range(2):
                        ins = v.tensor_tensor(SIG[c % 2][g], PS[:, 4 * (c % 2) + 2 + g, 0:CH], SIG[c % 2][g],
                                              ALU.mult)
                    ins.then_inc(mg_ch, 1)
                    dve.wait_ge(mg_ch, i * 2 * NCH + c + 1)
                    v.tensor_tensor(MG[:, i * 2 + u, n * CH:(n + 1) * CH], SIG[c % 2][0], SIG[c % 2][1],
                                    ALU.add).then_inc(mg_free, 1)
        dve.wait_ge(l_g1, 32)
        for t in range(TILES):
            dve.wait_ge(mix_r, t + 1)
            if t >= 2:
                dve.wait_ge(x1_st[t % 2], 16 * (t // 2))
            o = XT[2 + t % 2]
            g1 = XT[4 + (t > 0)]
            v.tensor_tensor(o, PS[:, 2 * (t % 2):2 * (t % 2) + 2, :].rearrange("p b c -> p (b c)"), g1,
                            ALU.mult).then_inc(mix_f, 1)
            dve.wait_ge(mix_f, t + 1)
            dve.wait_ge(l_xt[t % 2], 16 * (t // 2 + 1))
            v.tensor_tensor(o, o, XT[t % 2], ALU.add).then_inc(x1_r, 1)

        def front(tn, rows):
            ch = Chain(dve, c_front, tn * FRONT_STEPS)
            dve.wait_ge(n_sd, tn + 1)
            rows()
            ch(v.reciprocal(st[:, 4:5], st[:, 1:2]))
            ch(v.scalar_tensor_tensor(out=H2N, in0=XN, scalar=st[:, 4:5], in1=W2B, op0=ALU.mult, op1=ALU.mult))
            v.tensor_tensor(H2N, H2N, SH2B, ALU.add).then_inc(h2_r, 1)
            assert ch.n == FRONT_STEPS

        class Top16:
            lo, hi = slice(0, 8), slice(8, 16)

            def __init__(self, ch, n, vals, idx, src, work):
                self.ch, self.n, self.vals, self.idx, self.src, self.work = ch, n, vals, idx, src, work

            def best8(self):
                for c in range(self.n):
                    ins = v.max(self.vals(c, self.lo), self.src(c))
                self.ch(ins, alone=True)

            def places8(self):
                for c in range(self.n):
                    v.match_replace(self.work(c), self.vals(c, self.lo), self.src(c), NEG)
                    ins = v.max_index(self.idx(c, self.lo), self.vals(c, self.lo), self.src(c))
                self.ch(ins, alone=True)

            def next8(self):
                for c in range(self.n):
                    ins = v.max(self.vals(c, self.hi), self.work(c))
                self.ch(ins, alone=True)

            def next_places8(self):
                for c in range(self.n):
                    ins = v.max_index(self.idx(c, self.hi), self.vals(c, self.hi), self.work(c))
                self.ch(ins)

        four, half = [P, 2, TOPK, TOPK], TOPK * TOPK
        sv, sif = (x.rearrange("p (a h) k -> p a h k", h=2) for x in (SV, SIF))
        oh = [x.rearrange("p (a x y) -> p a x y", a=2, x=TOPK) for x in OH]

        class Pair:

            def __init__(self, tn, i):
                self.m, self.i = tn * PAIRS + i, i
                self.ch = Chain(dve, c_pair, self.m * PAIR_STEPS)
                self.keys = Top16(self.ch, 4, lambda c, s: SV[:, c, s], lambda c, s: SI[:, c, s],
                                  lambda c: SCS[:, c * P:(c + 1) * P], lambda c: SCW[:, c * P:(c + 1) * P])
                self.sums = Top16(self.ch, 2, lambda c, s: BEST[:, c, s], lambda c, s: POS[:, c, s],
                                  lambda c: CAND[:, c * half:(c + 1) * half],
                                  lambda c: CANDW[:, c * half:(c + 1) * half])
                self.at = bass.ds(i * 2 * TOPK + P, 2 * TOPK)

            def keys_best(self):
                wait_alone(dve, sc_e, self.m + 1)
                self.keys.best8()

            def candidates(self):
                self.keys.next_places8()
                v.tensor_copy(SIF, SI)
                cand = CAND.rearrange("p (a x y) -> p a x y", a=2, x=TOPK)
                self.ch(v.tensor_tensor(cand, sv[:, :, 0, :].unsqueeze(3).to_broadcast(four),
                                        sv[:, :, 1, :].unsqueeze(2).to_broadcast(four), ALU.add), alone=True)

            def sums_next(self):
                self.sums.next8()
                self.sums.next_places8()

            def places(self):
                ch = self.ch
                v.tensor_copy(EE[:, 0, :, 0:1], BEST[:, :, 0:1])
                v.tensor_scalar(PHL[:, 0], POS, 4, None, ALU.logical_shift_right)
                ch(v.tensor_scalar(PHL[:, 1], POS, TOPK - 1, None, ALU.bitwise_and))
                v.tensor_tensor(BEST, BEST, EE[:, 0, :, 0:1].to_broadcast([P, 2, TOPK]),
                                ALU.subtract).then_inc(top_r, 1)
                ch(v.tensor_copy(PHF, PHL))

            def key_numbers(self):
                for z in range(2):
                    ins = v.tensor_tensor(oh[z], PHF[:, z].unsqueeze(3).to_broadcast(four),
                                          iota.unsqueeze(1).unsqueeze(1).to_broadcast(four), ALU.is_equal)
                self.ch(ins)
                for z in range(2):
                    ins = v.tensor_tensor(oh[z], oh[z], sif[:, :, z, :].unsqueeze(2).to_broadcast(four), ALU.mult)
                self.ch(ins)

            def experts(self):
                ch, at = self.ch, self.at
                for z in range(2):
                    ins = v.tensor_reduce(EE[:, z], oh[z], AX_X, ALU.add)
                ch(ins)
                v.scalar_tensor_tensor(out=EIDX[:, at], in0=EE[:, 0].rearrange("p a k -> p (a k)"),
                                       scalar=float(NKEYS), in1=EE[:, 1].rearrange("p a k -> p (a k)"),
                                       op0=ALU.mult, op1=ALU.add)
                dve.wait_ge(ge_r, self.m + 1)
                ch(v.tensor_reduce(st[:, 5:7], BEST, AX_X, ALU.add))
                ch(v.reciprocal(st[:, 5:7], st[:, 5:7]))
                v.tensor_tensor(GATE[:, at].rearrange("p (a k) -> p a k", a=2), BEST,
                                st[:, 5:7].unsqueeze(2).to_broadcast([P, 2, TOPK]), ALU.mult).then_inc(pair_done, 1)
                dve.wait_ge(pair_done, self.m + 1)
                assert ch.n == PAIR_STEPS, ch.n

            def between(self):
                return {6: self.keys_best, 7: self.keys.places8, 8: self.keys.next8, 9: self.candidates,
                        10: self.sums.best8, 11: self.sums.places8, 12: self.sums_next, 13: self.places,
                        14: self.key_numbers, 15: self.experts}

            def at_once(self):
                for _, step in sorted(self.between().items()):
                    step()

        def coef(t, i, q, g):
            n = (t * ROUNDS + i * RPP + q) * (RING // GRP) + g
            dve.wait_ge(gel_r, n + 1)
            sl = slice(g * GRP, (g + 1) * GRP)
            v.tensor_tensor(COEF[:, sl], GEL[:, sl],
                            GATE[:, bass.ds(i * RPP * RING + q * RING + g * GRP, GRP)],
                            ALU.mult).then_inc(coef_r, 1)

        def rounds(t, i, between, last=False):
            todo = None
            for q in range(RPP):
                for g in range(RING // GRP):
                    for s in range(g * GRP, (g + 1) * GRP):
                        dve.wait_ge(gathered[s], (t * ROUNDS + i * RPP + q) * 16 + 16)
                        ins = v.tensor_tensor_reduce(RG[:, s, 0:D], RG[:, s, 0:D], H2C, 1.0, 0.0, ALU.mult,
                                                     ALU.add, PRE[:, s:s + 1])
                        if todo:
                            coef(t, i, *todo)
                            todo = None
                    ins.then_inc(dots, 1)
                    todo = (q, g)
                    at = q * (RING // GRP) + g
                    if at in between:
                        between[at]()
                if not last or q < 2:
                    v.tensor_copy(IDXS[:, q % 2, :], EIDX[:, bass.ds(i * RPP * RING + (q + 2) * RING, RING)])\
                        .then_inc(idx_r, 1)
            coef(t, i, *todo)

        def shift():
            v.tensor_copy(EIDX[:, 0:P], EIDX[:, P:2 * P])
            v.tensor_copy(GATE[:, 0:P], GATE[:, P:2 * P])
            v.tensor_copy(H2C, H2N).then_inc(c_shift, 1)

        class End:

            def __init__(self, t):
                self.t, self.ch = t, Chain(dve, c_end, t * END_STEPS)

            def read_sum(self):
                t = self.t
                dve.wait_ge(v_used, (t + 1) * ROUNDS * RING)
                v.tensor_tensor(Y, PS[:, 0:2, :].rearrange("p b c -> p (b c)"), G2B, ALU.mult).then_inc(acc_free, 1)

            def residual(self):
                t = self.t
                dve.wait_ge(acc_free, t + 1)
                dve.wait_ge(l_xe, t * 16 + 16)
                self.ch(v.tensor_tensor(Y, Y, XE, ALU.add))
                v.tensor_tensor_reduce(XE, Y, Y, 1.0, 0.0, ALU.mult, ALU.add, st[:, 2:3]).then_inc(e_sq, 1)

            def norm(self):
                dve.wait_ge(e_sd, self.t + 1)
                self.ch(v.reciprocal(st[:, 7:8], st[:, 3:4]))
                v.scalar_tensor_tensor(out=Y, in0=Y, scalar=st[:, 7:8], in1=NFB, op0=ALU.mult,
                                       op1=ALU.mult).then_inc(y_r, 1)
                assert self.ch.n == END_STEPS, self.ch.n

        def tile(t, prev=True, last=False):
            between = {}
            if prev:
                end = End(t - 1)
                between |= {0: end.read_sum, 2: end.residual, 4: end.norm}
            if not last:
                between |= {1: lambda: front(t + 1, lambda: dve.wait_ge(l_rows2, 32))}
                between |= Pair(t + 1, 0).between()
            rounds(t, 0, between)
            with dve.Fori(1, PAIRS - last) as i:
                rounds(t, i, {} if last else Pair(t + 1, i).between())
            if prev:
                dve.wait_ge(y_st, t * 16)
            dve.wait_ge(l_g2, 32 if prev else 16)
            if last:
                rounds(t, PAIRS - 1, {}, last=True)
            else:
                dve.wait_ge(dots, (t + 1) * ROUNDS * (RING // GRP))
                dve.wait_ge(coef_r, (t + 1) * ROUNDS * (RING // GRP))
                dve.wait_ge(idx_r, (t + 1) * ROUNDS + 2)
                shift()
                dve.wait_ge(c_shift, t + 3)

        def first_rows():
            dve.wait_ge(l_rows, 48)
            v.scalar_tensor_tensor(out=W2B, in0=W2B, scalar=1.0, in1=Y, op0=ALU.add, op1=ALU.mult)

        dve.wait_ge(it_r, 1)
        front(0, first_rows)
        with dve.Fori(0, PAIRS) as i:
            Pair(0, i).at_once()
        dve.wait_ge(l_nf, 16)
        shift()
        dve.wait_ge(c_shift, 1)
        for q in range(2):
            v.tensor_copy(IDXS[:, q, :], EIDX[:, q * RING:(q + 1) * RING]).then_inc(idx_r, 1)
        dve.wait_ge(l_rows2, 32)
        v.scalar_tensor_tensor(out=W2B, in0=W2B, scalar=1.0, in1=Y, op0=ALU.add, op1=ALU.mult).then_inc(c_shift, 1)
        dve.wait_ge(c_shift, 2)
        tile(0, prev=False)
        with dve.Fori(1, TILES - 1) as t:
            tile(t)
        tile(TILES - 1, last=True)
        end = End(TILES - 1)
        end.read_sum()
        end.residual()
        end.norm()

    c_shift = sem("shifted")
    block = ctx.enter_context(nc.Block())

    @block.sync
    def _(sp):
        sp.dma_start(cs[:], cT).then_inc(l_c, 16)
        sp.dma_start(n1[:], n1T).then_inc(l_c, 16)
        for c in range(2):
            sp.dma_start(WMOD[:, c], w_mod[c]).then_inc(l_mw[c], 16)
        sp.dma_start(BROW, b_mod).then_inc(l_b, 16)
        sp.dma_start(hT, xT).then_inc(l_x, 16)
        for c in range(2, MODC):
            sp.wait_ge(m_ready, c - 1)
            sp.dma_start(WMOD[:, c % 2], w_mod[c]).then_inc(l_mw[c % 2], 16)
        sp.wait_ge(m_evac, MODC)
        sp.dma_start(mod_d, MROW).then_inc(md_out, 16)
        sp.wait_ge(h_ready, KD)

        def weights(h, b):
            sp.dma_start(W[:, b], w_in[h, b]).then_inc(l_w[b], 16)

        def params(h):
            sp.dma_start(pr[:], par[h]).then_inc(l_par, 16)
            for half in range(2):
                a = half * 64
                sp.dma_start(WRI[a:a + 64, :, a:a + 64], wri[h, half]).then_inc(l_par, 16)
            sp.dma_start(S0, s0[h]).then_inc(l_par, 16)

        def results(h):
            sp.wait_ge(s_r, h * NSU + LAST_CTX)
            for d in range(2):
                sp.dma_start(hg_out[d, h], SF[:, d]).then_inc(st_out, 16)
            sp.wait_ge(hg_done, h + 1)
            sp.wait_ge(lru_done, h + 1)
            sp.dma_start(lru_out[h], ef[:]).then_inc(st_out, 16)

        for b in W_ORDER:
            weights(0, b)
        sp.wait_ge(s_c, 2)
        params(0)
        with sp.Fori(0, HEADS - 1) as h:
            for b in W_ORDER:
                sp.wait_ge(z_ready, h * ZC + (b + 1) * NCH)
                weights(h + 1, b)
            results(h)
            params(h + 1)
            wait_alone(sp, st_out, (h + 1) * 48)
        results(HEADS - 1)
        stage_b_sp(sp)

    @block.gpsimd
    def _(pool):
        ch = Chain(pool, s_ms)
        ch(nc.gpsimd.memset(ones[:], 1.0))
        keep = dict(fill=0.0)
        ch(nc.gpsimd.affine_select(out=mask_f[:], in_=ones[:], compare_op=ALU.is_ge, fill=0.0, base=0,
                                   pattern=[[1, P]], channel_multiplier=-1))
        ch(nc.gpsimd.affine_select(out=mask_b[:], in_=ones[:], compare_op=ALU.is_ge, fill=0.0, base=0,
                                   pattern=[[-1, P]], channel_multiplier=1))
        ch(nc.gpsimd.affine_select(out=ident[:], in_=mask_f[:], compare_op=ALU.is_ge, fill=0.0, base=0,
                                   pattern=[[-1, P]], channel_multiplier=1))
        for m in (mask_f, mask_b):
            v = m[:].rearrange("p (c t) -> p c t", c=CPT)
            ch(nc.gpsimd.affine_select(out=v, in_=v, compare_op=ALU.is_ge, fill=0.0, base=0,
                                       pattern=[[-CHUNK, CPT], [0, CHUNK]], channel_multiplier=1))
            ch(nc.gpsimd.affine_select(out=v, in_=v, compare_op=ALU.is_ge, fill=0.0, base=CHUNK - 1,
                                       pattern=[[CHUNK, CPT], [0, CHUNK]], channel_multiplier=-1))
        nc.gpsimd.memset(zero[:], 0.0)
        nc.gpsimd.memset(eps[:], EPS).then_inc(s_c, 1)
        ch(nc.gpsimd.memset(AR[:, A_ATT:A_SM], 0.0))
        ch(nc.gpsimd.memset(AR[:, A_SM:A_WRI], 1.0))
        ch(nc.gpsimd.memset(SM.rearrange("p (n c) -> p n c", c=CHUNK)[:, :, 0:1], 0.0))
        nc.gpsimd.memset(AR[:, A_WRI:A_S0], 0.0).then_inc(s_c, 1)
        stage_b_pool(pool)

    @block.tensor
    def _(pe):
        pe.wait_ge(s_silu, 1)
        for c in range(MODC):
            pe.wait_ge(l_mw[c % 2], 16 * (c // 2 + 1))
            if c >= 2:
                pe.wait_ge(m_evac, c - 1)
            for k in range(KD):
                mm = nc.tensor.matmul(PS[0:2, c % 2, :], cs[:, k, :], WMOD[:, c % 2, k, :],
                                      start=(k == 0), stop=(k == KD - 1))
            mm.then_inc(m_ready, 1)
        pe.wait_ge(s_c, 1)
        pe.wait_ge(m_evac, MODC)
        for n in range(2 * KD):
            mm = nc.tensor.transpose(PS[:, 2, 2 * n:2 * n + 2], MROW[:, n * P:(n + 1) * P], ident[0:2, 0:2])
        mm.then_inc(t_ready, 1)
        for k in range(KD):
            pe.wait_ge(sq_r, k + 1)
            for n in range(NCH):
                mm = nc.tensor.matmul(PS[:, 3 + n, 0:CH], ones[:], SQ[k % 2][:, n * CH:(n + 1) * CH],
                                      start=(k == 0), stop=(k == KD - 1))
            mm.then_inc(ssq_r, 1)

        pe.wait_ge(h_ready, KD)
        with pe.Fori(0, HEADS) as h:
            def z_bank(b, n, rel=False):
                c = b * NCH + n
                if c >= NCH:
                    pe.wait_ge(z_free, h * ZC + c - NCH + 1)
                return PS[:, n, 0:CH]

            for b in range(NB):
                pe.wait_ge(l_w[b], h * 16 + 16)
                for n in range(NCH):
                    z = z_bank(b, n)
                    if b == B_V:
                        for u in range(CH // P):
                            t = n * (CH // P) + u
                            for k in range(KD):
                                mm = nc.tensor.matmul(z[:, u * P:(u + 1) * P], hT[:, k, t * P:(t + 1) * P],
                                                      W[:, b, k, :], start=(k == 0), stop=(k == KD - 1))
                    else:
                        for k in range(KD):
                            mm = nc.tensor.matmul(z, W[:, b, k, :], hT[:, k, n * CH:(n + 1) * CH],
                                                  start=(k == 0), stop=(k == KD - 1))
                    mm.then_inc(z_ready, 1)

            pe.wait_ge(xc_r, h + 1)
            pe.wait_ge(l_par, h * 64 + 64)
            for g in range(4):
                for n in range(NCH):
                    z = z_bank(B_GATES + g, n)
                    nc.tensor.matmul(z, WRI[:, g, :], XC[:, n * CH:(n + 1) * CH],
                                     start=True, stop=True).then_inc(z_ready, 1)

            def scores(it):
                d, tt = it // TILES, tile_of(it)
                if it % TILES == 0:
                    pe.wait_ge(k_r[d], h + 1)
                sl = slice(tt * P, (tt + 1) * P)
                nc.tensor.transpose(PS[:, 3, 0:P], KE[d][:, sl], ident[:]).then_inc(ket_r, 1)
                if it:
                    pe.wait_ge(att_m, h * TI + it)
                nc.tensor.matmul(PS[:, 4, 0:P], KI[d][:, sl], QD[d][:, sl],
                                 start=True, stop=True).then_inc(att_r, 1)
                pe.wait_ge(ket_e, h * TI + it + 1)
                for j in range(CPT):
                    mm = nc.tensor.matmul(PS[:, 5 + it % 2, j * P:(j + 1) * P], KET[:, it % 2, j, :],
                                          Vt[:, tt, :], start=True, stop=True)
                mm.then_inc(ds_r, 1)

            def outputs(it):
                d, tt = it // TILES, tile_of(it)
                pe.wait_ge(att_m, h * TI + it + 1)
                if it:
                    pe.wait_ge(o_a, h * TI + it)
                nc.tensor.matmul(PS[:, 7, 0:P], Vt[:, tt, :], ATT[:, d, it % 2, :], start=True, stop=False)
                for jj in range(CPT):
                    j = jj if d == 0 else CPT - 1 - jj
                    st, cnt = state_of(it, jj)
                    if cnt is not None:
                        pe.wait_ge(s_r, h * NSU + cnt)
                    c = slice(tt * P + j * CHUNK, tt * P + (j + 1) * CHUNK)
                    mm = nc.tensor.matmul(PS[:, 7, j * CHUNK:(j + 1) * CHUNK], st, QD[d][:, c],
                                          start=False, stop=(jj == CPT - 1))
                mm.then_inc(o_r, 1)

            scores(0)
            for it in range(TI):
                if it + 1 < TI:
                    scores(it + 1)
                outputs(it)
            for n in range(NCH):
                pe.wait_ge(osq_r, h * NCH + n + 1)
                z = z_bank(B_SSQ, n)
                nc.tensor.matmul(z, ones[:], K[1][:, n * CH:(n + 1) * CH], start=True, stop=True)\
                    .then_inc(z_ready, 1)
            pe.wait_ge(z_free, (h + 1) * ZC)
        stage_b_pe(pe)

    @block.scalar
    def _(act):
        A = nc.scalar.activation
        act.wait_ge(l_c, 32)
        A(cs[:], cs[:], ACT.Silu).then_inc(s_silu, 1)
        act.wait_ge(l_x, 16)
        for k in range(KD):
            if k >= 2:
                act.wait_ge(ssq_r, k - 1)
            A(SQ[k % 2], hT[:, k, :], ACT.Square).then_inc(sq_r, 1)
        act.wait_ge(ssq_r, KD)
        act.wait_ge(s_c, 1)
        for n in range(NCH):
            last = A(RS[:, n * CH:(n + 1) * CH], PS[:, 3 + n, 0:CH], ACT.Sqrt, bias=eps[:], scale=1.0 / D)
        last.then_inc(sd_r, 1)
        act.wait_ge(h_ready, KD)

        act.wait_ge(s_c, 2)
        with act.Fori(0, HEADS) as h:
            def evac(b, n, out, func, in_=None, **kw):
                act.wait_ge(z_ready, h * ZC + b * NCH + n + 1)
                return A(out, PS[:, n, 0:CH] if in_ is None else in_, func, **kw)

            def block_out(b, out, func, **kw):
                for n in range(NCH):
                    evac(b, n, out[:, n * CH:(n + 1) * CH], func, **kw).then_inc(z_free, 1)

            act.wait_ge(pa[0], h + 1)
            A(ps_[:, 8:12], ps_[:, 4:8], ACT.Exp)
            A(ps_[:, 16:18], ps_[:, 14:16], ACT.Exp, scale=-1.0).then_inc(pa[1], 1)
            act.wait_ge(pa[2], h + 1)
            A(ps_[:, 20:22], ps_[:, 18:20], ACT.Ln).then_inc(pa[3], 1)
            block_out(B_FF, SG[0], ACT.Sigmoid)
            block_out(B_Q, Q, ACT.Silu)
            act.wait_ge(f_r[0], h + 1)
            A(SG[0], SG[0], ACT.Ln).then_inc(lf_r[0], 1)
            block_out(B_FB, SG[1], ACT.Sigmoid)

            def exps(d):
                act.wait_ge(cum_r[d], h + 1)
                A(QD[d], CUM, ACT.Exp)
                A(KI[d], CUM, ACT.Exp, scale=-1.0)
                e = CHUNK - 1 if d == 0 else 0
                ends = CUM.rearrange("p (c t) -> p c t", t=CHUNK)[:, :, e]
                A(dec[:, d, :], ends, ACT.Exp).then_inc(e_r[d], 1)
                act.wait_ge(tc_r[d], h + 1)
                A(KE[d], KE[d], ACT.Exp).then_inc(e3_r[d], 1)

            act.wait_ge(f_r[1], h + 1)
            A(SG[1], SG[1], ACT.Ln).then_inc(lf_r[1], 1)
            exps(0)
            xl = XR[:, N_CTX + 5:N_CTX + 5 + N_LAT].rearrange("p (c r) -> p r c", r=GRID_H)
            evac(B_XR, 0, XR[:, 2:2 + N_CTX], ACT.Copy, in_=PS[:, 0, 0:N_CTX])
            r0 = 0
            for n in range(NCH):
                lo = N_CTX if n == 0 else 0
                rows = (CH - lo) // GRID_W
                src = PS[:, n, lo:CH].rearrange("p (r c) -> p r c", c=GRID_W)
                evac(B_XR, n, xl[:, r0:r0 + rows, :], ACT.Copy, in_=src).then_inc(z_free, 1)
                r0 += rows
            block_out(B_G, oA[:, h, :], ACT.Silu)
            exps(1)
            block_out(B_V, V, ACT.Copy)
            block_out(B_XG, hB[:, h, :], ACT.Gelu_apprx_tanh)
            act.wait_ge(pa[4], h + 1)
            for d in range(2):
                for g, out, bias in ((0, R[d], P_BR), (1, I[d], P_BI)):
                    block_out(B_GATES + 2 * d + g, out, ACT.Sigmoid, bias=pr[:, bias + d:bias + d + 1])
            act.wait_ge(z_free, h * ZC + B_SSQ * NCH)
            for d in range(2):
                A(R[d], R[d], ACT.Tanh, scale=ps_[:, 34 + d:35 + d]).then_inc(s_act, 1)
            act.wait_ge(s_act, h * 2 + 2)
            for d in range(2):
                A((CUM, SG[1])[d], R[d], ACT.Sqrt).then_inc(t2_r[d], 1)
            for it in range(TI):
                act.wait_ge(ket_r, h * TI + it + 1)
                if it >= 2:
                    act.wait_ge(ds_r, h * TI + it - 1)
                for j in range(CPT):
                    rows = slice(j * CHUNK, (j + 1) * CHUNK)
                    cp = A(KET[rows, it % 2, j, :], PS[rows, 3, 0:P], ACT.Copy)
                cp.then_inc(ket_e, 1)
            block_out(B_SSQ, QD[0], ACT.Sqrt, bias=eps[:], scale=1.0 / P)
            act.wait_ge(hg_done, h + 1)
            act.wait_ge(lru_done, h + 1)
        stage_b_act(act)

    @block.vector
    def _(dve):
        v = nc.vector
        ch = Chain(dve, s_dv)
        dve.wait_ge(l_b, 16)
        for c in range(MODC):
            dve.wait_ge(m_ready, c + 1)
            sl = slice(c * 512, (c + 1) * 512)
            v.tensor_tensor(MROW[:, sl], PS[0:2, c % 2, :], BROW[:, sl], ALU.add).then_inc(m_evac, 1)
        dve.wait_ge(t_ready, 1)
        mt = PS[:, 2, 0:4 * KD].rearrange("p (s k c) -> p s k c", s=2, c=2)
        v.tensor_copy(sh1[:], mt[:, 0])
        ch(v.tensor_scalar(w1[:], mt[:, 1], 1.0, None, ALU.add))
        ch(v.tensor_tensor(w1[:], w1[:], n1[:].unsqueeze(2).to_broadcast([P, KD, 2]), ALU.mult))
        dve.wait_ge(sd_r, 1)
        ch(v.reciprocal(RS, RS))
        for k in range(KD):
            for s, sl in enumerate((slice(0, N_CTX), slice(N_CTX, T))):
                ins = v.scalar_tensor_tensor(out=hT[:, k, sl], in0=hT[:, k, sl], scalar=w1[:, k, s:s + 1],
                                             in1=RS[:, sl], op0=ALU.mult, op1=ALU.mult)
                if s == 1:
                    ch(ins)
            for s, sl in enumerate((slice(0, N_CTX), slice(N_CTX, T))):
                ins = v.tensor_scalar(hT[:, k, sl], hT[:, k, sl], sh1[:, k, s:s + 1], None, ALU.add)
            ins.then_inc(h_ready, 1)
        base = ch.n
        dve.wait_ge(s_c, 2)
        per_head = DVE_HEAD
        with dve.Fori(0, HEADS) as h:
            ch = Chain(dve, s_dv, base + h * per_head)
            dve.wait_ge(l_par, h * 64 + 64)
            lg = pr[:, P_LB:P_LB + 4].rearrange("p (d l) -> p d l", d=2)
            ch(v.tensor_tensor(ps_[:, 0:2], lg[:, :, 0], lg[:, :, 1], ALU.max))
            v.tensor_tensor(ps_[:, 4:8].rearrange("p (d l) -> p d l", d=2), lg,
                            ps_[:, 0:2].unsqueeze(2).to_broadcast([P, 2, 2]), ALU.subtract)
            lam = pr[:, P_LAM:P_LAM + 2]
            v.scalar_tensor_tensor(out=ps_[:, 14:16], in0=lam, scalar=-1.0, in1=lam, op0=ALU.mult,
                                   op1=ALU.max).then_inc(pa[0], 1)
            dve.wait_ge(pa[1], h + 1)
            ex = ps_[:, 8:12].rearrange("p (d l) -> p d l", d=2)
            v.tensor_scalar(ps_[:, 18:20], ps_[:, 16:18], 1.0, None, ALU.add).then_inc(pa[2], 1)
            ch(v.tensor_tensor(ps_[:, 2:4], ex[:, :, 0], ex[:, :, 1], ALU.add))
            ch(v.reciprocal(ps_[:, 2:4], ps_[:, 2:4]))
            ch(v.tensor_tensor(ps_[:, 24:26], ex[:, :, 0], ps_[:, 2:4], ALU.mult))
            v.tensor_scalar(ps_[:, 26:28], ps_[:, 24:26], -1.0, 1.0, ALU.mult, ALU.add)
            ch(v.tensor_scalar(ps_[:, 22:24], ps_[:, 18:20], -1.0, None, ALU.add))
            ch(v.tensor_scalar(ps_[:, 28:30], ps_[:, 22:24], 0.0, None, ALU.is_equal))
            ch(v.tensor_tensor(ps_[:, 22:24], ps_[:, 22:24], ps_[:, 28:30], ALU.add))
            ch(v.reciprocal(ps_[:, 22:24], ps_[:, 22:24]))
            dve.wait_ge(pa[3], h + 1)
            ch(v.tensor_tensor(ps_[:, 20:22], ps_[:, 20:22], ps_[:, 28:30], ALU.add))
            ch(v.tensor_tensor(ps_[:, 20:22], ps_[:, 20:22], ps_[:, 22:24], ALU.mult))
            ch(v.tensor_tensor(ps_[:, 20:22], ps_[:, 20:22], ps_[:, 16:18], ALU.mult))
            ch(v.tensor_scalar(ps_[:, 30:32], lam, -1.0, 0.0, ALU.mult, ALU.max))
            ch(v.tensor_tensor(ps_[:, 20:22], ps_[:, 20:22], ps_[:, 30:32], ALU.add))
            v.tensor_scalar(ps_[:, 34:36], ps_[:, 20:22], LRU_C / 2, None, ALU.mult).then_inc(pa[4], 1)

            def forget(d):
                dve.wait_ge(z_free, h * ZC + NCH * ((B_FF, B_FB)[d] + 1))
                ch(v.tensor_scalar(SG[d], SG[d], ps_[:, 26 + d:27 + d], ps_[:, 24 + d:25 + d],
                                   ALU.mult, ALU.add))
                v.tensor_scalar(K[d], SG[d], -1.0, 1.0, ALU.mult, ALU.add).then_inc(f_r[d], 1)

            def sums(d):
                dve.wait_ge(lf_r[d], h + 1)
                if d:
                    dve.wait_ge(e_r[0], h + 1)
                if d == 0:
                    ins = v.tensor_tensor_scan(CUM, SM[:, 0:T], SG[0], 0.0, ALU.mult, ALU.add)
                else:
                    ins = v.tensor_tensor_scan(CUM[:, ::-1], SM[:, 1:T + 1][:, ::-1], SG[1][:, ::-1], 0.0,
                                               ALU.mult, ALU.add)
                ins.then_inc(cum_r[d], 1)
                dve.wait_ge(cum_r[d], h + 1)
                cv = CUM.rearrange("p (c t) -> p c t", t=CHUNK)
                e = CHUNK - 1 if d == 0 else 0
                v.tensor_tensor(KE[d].rearrange("p (c t) -> p c t", t=CHUNK),
                                cv[:, :, e:e + 1].to_broadcast([P, NCK, CHUNK]), cv,
                                ALU.subtract).then_inc(tc_r[d], 1)

            def keys_(d):
                dve.wait_ge(e_r[d], h + 1)
                if d == 0:
                    dve.wait_ge(z_free, h * ZC + NCH * (B_Q + 1))
                v.tensor_tensor(QD[d], QD[d], Q, ALU.mult)
                v.tensor_tensor(KI[d], KI[d], K[d], ALU.mult)
                dve.wait_ge(e3_r[d], h + 1)
                v.tensor_tensor(KE[d], KE[d], K[d], ALU.mult).then_inc(k_r[d], 1)

            forget(0)
            sums(0)
            forget(1)
            keys_(0)
            sums(1)
            for a, n in ((0, 2), (N_CTX + 2, 3), (N_CTX + 5 + N_LAT, 1)):
                last = v.memset(XR[:, a:a + n], 0.0)
            ch(last)
            dve.wait_ge(z_free, h * ZC + NCH * (B_XR + 1))
            for j in range(4):
                for a, o, n in ((0, 0, N_CTX), (N_CTX + 3, N_CTX, N_LAT)):
                    xs, xo = XR[:, a + j:a + j + n], XC[:, o:o + n]
                    cw = pr[:, P_CW + j:P_CW + j + 1]
                    if j == 0:
                        ins = v.tensor_scalar(xo, xs, cw, pr[:, P_CB:P_CB + 1], ALU.mult, ALU.add)
                    else:
                        ins = v.scalar_tensor_tensor(out=xo, in0=xs, scalar=cw, in1=xo, op0=ALU.mult,
                                                     op1=ALU.add)
                if j < 3:
                    ch(ins)
                else:
                    ins.then_inc(xc_r, 1)
            keys_(1)

            for d in range(2):
                root = (CUM, SG[1])[d]
                dve.wait_ge(t2_r[d], h + 1)
                v.tensor_tensor(I[d], I[d], XC, ALU.mult)
                ch(v.tensor_scalar(SG[0], R[d], -1.0, -1.0, ALU.mult, ALU.add))
                ch(v.reciprocal(SG[0], SG[0]))
                v.scalar_tensor_tensor(out=R[d], in0=R[d], scalar=1.0, in1=SG[0], op0=ALU.subtract, op1=ALU.mult)
                ch(v.scalar_tensor_tensor(out=root, in0=root, scalar=-2.0, in1=SG[0], op0=ALU.mult, op1=ALU.mult))
                ch(v.tensor_tensor(I[d], I[d], root, ALU.mult))
                for a, n, first in ((0, N_CTX, 0.0), (N_CTX, N_LAT, pr[:, P_H0 + d:P_H0 + d + 1])):
                    views = [x[:, a:a + n] for x in (I[d], R[d])]
                    if d:
                        views = [x[:, ::-1] for x in views]
                    ins = v.tensor_tensor_scan(views[0], views[1], views[0], first, ALU.mult, ALU.add)
                ch(ins)
            v.tensor_copy(ef[:, 0:1], I[0][:, N_CTX - 1:N_CTX])
            ch(v.tensor_copy(ef[:, 1:2], I[1][:, 0:1]))
            ch(v.tensor_tensor(I[0], I[0], I[1], ALU.add))
            hc = hB[:, h, 0:N_CTX]
            v.tensor_tensor(hc, hc, I[0][:, 0:N_CTX], ALU.mult)
            hl = hB[:, h, N_CTX:T].rearrange("p (r c) -> p r c", c=GRID_W)
            v.tensor_tensor(hl, hl, I[0][:, N_CTX:T].rearrange("p (c r) -> p r c", r=GRID_H),
                            ALU.mult).then_inc(lru_done, 1)

            O, OS = K[0], K[1]

            def out_of(it):
                tt = tile_of(it)
                dve.wait_ge(o_r, h * TI + it + 1)
                o = O[:, tt * P:(tt + 1) * P]
                if it < TILES:
                    v.tensor_copy(o, PS[:, 7, 0:P]).then_inc(o_a, 1)
                else:
                    v.tensor_tensor(o, PS[:, 7, 0:P], o, ALU.add).then_inc(o_a, 1)

            for it in range(TI):
                d, tt = it // TILES, tile_of(it)
                wait_alone(dve, att_r, h * TI + it + 1)
                v.copy_predicated(ATT[:, d, it % 2, :], (mask_f, mask_b)[d][:].bitcast(I32),
                                  PS[:, 4, 0:P]).then_inc(att_m, 1)
                dve.wait_ge(ds_r, h * TI + it + 1)
                for jj in range(CPT):
                    if (it, jj) not in writes:
                        continue
                    j = jj if d == 0 else CPT - 1 - jj
                    st, cnt = reads[it, jj]
                    to, k, final = writes[it, jj]
                    if cnt is not None:
                        dve.wait_ge(s_r, h * NSU + cnt)
                    c = tt * CPT + j
                    ins = v.scalar_tensor_tensor(out=to, in0=st, scalar=dec[:, d, c:c + 1],
                                                 in1=PS[:, 5 + it % 2, j * P:(j + 1) * P],
                                                 op0=ALU.mult, op1=ALU.add)
                    ins.then_inc(s_r, 1)
                if it:
                    out_of(it - 1)
            out_of(TI - 1)
            dve.wait_ge(o_a, h * TI + TI)
            for n in range(NCH):
                sl = slice(n * CH, (n + 1) * CH)
                v.tensor_tensor(OS[:, sl], O[:, sl], O[:, sl], ALU.mult).then_inc(osq_r, 1)
            dve.wait_ge(z_free, (h + 1) * ZC)
            ch(v.reciprocal(QD[0], QD[0]))
            ch(v.scalar_tensor_tensor(out=O, in0=O, scalar=pr[:, P_HN:P_HN + 1], in1=QD[0], op0=ALU.mult,
                                      op1=ALU.mult))
            v.tensor_tensor(oA[:, h, :], oA[:, h, :], O, ALU.mult).then_inc(hg_done, 1)
            assert ch.n == per_head, ch.n
        stage_b_dve(dve)
    ctx.close()


def layout(x_prompt, x_sample, state_hgrn, state_rglru, c, c_ctx, w_mod, b_mod, norm1, w_in,
           hg_lb_logits, hg_norm, lru_conv_w, lru_conv_b, lru_w_r, lru_b_r, lru_w_i, lru_b_i,
           lru_lambda, w_branch_a, w_branch_b, w_out, norm2, pk_w_q, pk_sub_keys, pk_u, pk_v, norm_f):
    cat, cg = np.concatenate, np.ascontiguousarray
    x = cat([x_prompt[0], x_sample[0]], axis=0)
    blocks = lambda w: w.reshape(w.shape[0] // P, P, w.shape[1] // P, P).transpose(2, 1, 0, 3)
    wi = blocks(w_in[0])
    q, ff, fb, v, g, xr, xg = (wi[4 * n:4 * n + 4] for n in range(7))
    ga, gb = wi[28:36], wi[36:44]
    per = lambda a: a.reshape(a.shape[0], HEADS, P).transpose(1, 2, 0)
    lb = hg_lb_logits.transpose(2, 0, 1).reshape(HEADS, P, 4)
    par = cat([lb, per(lru_conv_w[0]), per(lru_conv_b), per(lru_b_r[0]), per(lru_b_i[0]), per(lru_lambda[0]),
               np.broadcast_to(hg_norm[0][None, :, None], (HEADS, P, 1)),
               per(state_rglru[0, 0])], axis=2)
    gate_w = np.stack([lru_w_r[0, 0], lru_w_i[0, 0], lru_w_r[0, 1], lru_w_i[0, 1]])
    return {
        "xT": cg(x.T.reshape(KD, P, T).transpose(1, 0, 2)),
        "x_tok": x.reshape(TILES, P, D),
        "cT": cg(np.stack([c_ctx, c[0]], axis=1).reshape(KD, P, 2).transpose(1, 0, 2)),
        "w_mod": cg(w_mod[0].reshape(KD, P, MODC, 512).transpose(2, 1, 0, 3)),
        "b_mod": cg(np.broadcast_to(b_mod[0], (2, MODW))),
        "n1T": cg(norm1[0].reshape(KD, P).T),
        "w_in": cg(np.stack([ff, q, fb, xr, g, v, xg], axis=1)),
        "par": cg(par),
        "wri": cg(gate_w.reshape(4, HEADS, 2, 64, 64).transpose(1, 2, 3, 0, 4)),
        "s0": cg(state_hgrn[0, 0].transpose(1, 2, 0, 3)),
        "w_mg": cg(cat([ga, gb, blocks(w_branch_a[0]), blocks(w_branch_b[0])], axis=2)),
        "w_out": cg(w_out[0].reshape(KD, P, D).transpose(1, 0, 2)),
        "n2": norm2[0],
        "nf": norm_f,
        "w_q": cg(pk_w_q[0].reshape(KD, P, 2 * D).transpose(1, 0, 2)),
        "keys": cg(pk_sub_keys[0].transpose(3, 1, 0, 2).reshape(P, 16 * P)),
        "uv": cg(cat([pk_u[0], pk_v[0]], axis=1)),
    }


_OUTS = {"y_out": (TILES, P, D), "hg_out": (2, HEADS, P, P), "lru_out": (HEADS, P, 2)}


def make(nc, shapes):
    args = [nc.dram_tensor(f"in_{n}", s, F32, kind="ExternalInput").ap() for n, s in shapes.items()]
    args += [nc.dram_tensor(f"out_{n}", s, F32, kind="ExternalOutput").ap() for n, s in _OUTS.items()]
    args.append(nc.dram_tensor("mod_scratch", (2, MODW), F32).ap())
    args.append(nc.dram_tensor("x1_scratch", (TILES, P, D), F32).ap())
    build(nc, *args)


def kernel(**inputs):
    import concourse.bacc as _bacc
    from concourse.bass_utils import run_bass_kernel_spmd as _run

    arrays = layout(**{k: np.asarray(a) for k, a in inputs.items()})
    nc = _bacc.Bacc("TRN2", target_bir_lowering=False, num_devices=1)
    make(nc, {n: a.shape for n, a in arrays.items()})
    r = _run(nc, [{f"in_{n}": a for n, a in arrays.items()}], core_ids=[0])
    y, hg, lru = (r.results[0][f"out_{n}"] for n in _OUTS)
    y = y.reshape(T, D)
    return (y[None, :N_CTX], y[None, N_CTX:], hg[None, None],
            np.ascontiguousarray(lru.transpose(2, 0, 1)).reshape(1, 1, 2, HEADS * P))
```

```python
from contextlib import ExitStack

import numpy as np
import concourse.bass as bass
from concourse import mybir

ALU = mybir.AluOpType
ACT = mybir.ActivationFunctionType
F32 = mybir.dt.float32
I32 = mybir.dt.int32
U32 = mybir.dt.uint32
AX_X = mybir.AxisListType.X

P = 128
D = 1024
KD = D // P
N_CTX = 128
N_LAT = 1024
T = N_CTX + N_LAT
TILES = T // P
NCH = 3
CH = T // NCH
GRID_W = 64
GRID_H = N_LAT // GRID_W
EPS = 1e-6
HEADS = 4
CHUNK = 32
CPT = P // CHUNK
NCK = T // CHUNK
LRU_C = 8.0
MODW = 6 * D
MODC = MODW // 512
MOD1 = 2 * D // 512
PK_HEADS = 8
TOPK = 16
NKEYS = 128
NEG = -3.0e38
RING = 8
ROUNDS = PK_HEADS * TOPK // RING
PAIRS = PK_HEADS // 2
RPP = ROUNDS // PAIRS
DVE_HEAD = 29
GATE_STEPS = 6
LRU_STEP = 11
GRP = 2

P_LB, P_CW, P_CB, P_BR, P_BI, P_LAM, P_HN, P_H0, NPAR = 0, 4, 8, 9, 11, 13, 15, 16, 18

B_FF, B_Q, B_FB, B_XR, B_V, B_GATES, B_G, B_XG, B_SSQ = 0, 1, 2, 3, 4, 5, 9, 10, 11
W_BLOCKS = (B_FF, B_Q, B_FB, B_XR, B_V, B_G, B_XG)
NB = len(W_BLOCKS)
ZC = (B_SSQ + 1) * NCH
TI = 2 * TILES

A_HT = 0
A_OA = A_HT + KD * T
A_HB = A_OA + HEADS * T
A_W = A_HB + HEADS * T
A_BUF = A_W + NB * D
XR_W = T + 8
A_S = A_BUF + 17 * T + XR_W
NS = 12
A_ATT = A_S + NS * P
A_KET = A_ATT + 4 * P
A_SM = A_KET + 2 * CPT * P
A_WRI = A_SM + T + CHUNK
A_S0 = A_WRI + 4 * P
A_SF = A_S0 + 2 * P
A_END = A_SF + 2 * P
A_MG = A_BUF
A_WM = A_W
WM = 24 * P
A_SIG = A_MG + KD * T
A_WO = A_END - KD * D
A_MOD = A_SIG + 4 * CH
assert A_MOD + KD * 512 + 4 * 512 <= A_WO
A_X = A_WM
A_WQ = 0
A_KEY = A_WQ + 16 * D
A_RING = A_W
A_B = A_RING + RING * 2 * D
assert A_KEY + 16 * P <= A_RING and A_WM + 2 * WM <= A_BUF and A_X + 6 * D <= A_BUF
assert A_B >= A_MG + KD * T and A_B + 8 * D + 64 <= A_WO


def late_chunk(c):
    return (B_G, B_XG)[c // NCH], c % NCH


def wait_alone(eng, sem, value):
    eng.wait_ge(sem, value)
    eng.nop(nofuse=True)


class Chain:

    def __init__(self, eng, sem, base=0):
        self.eng, self.sem, self.base, self.n = eng, sem, base, 0

    def __call__(self, ins, alone=False):
        self.n += 1
        ins.then_inc(self.sem, 1)
        if alone:
            wait_alone(self.eng, self.sem, self.base + self.n)
        else:
            self.eng.wait_ge(self.sem, self.base + self.n)


def build(nc, xT, x_tok, cT, w_mod, b_mod, n1T, w_in, par, wri, s0, w_mg, w_out, n2, nf, w_q, keys,
          uv, y_out, hg_out, lru_out, mod_d, x1_d):
    ctx = ExitStack()
    sb = lambda name, shape, dt=F32: nc.alloc_sbuf_tensor(name, shape, dt)
    sem = lambda name: nc.alloc_semaphore(name)

    AR = sb("arena", [P, A_END])
    ident = sb("ident", [P, P])
    ones = sb("ones", [P, P])
    zero = sb("zero", [P, P])
    mask_f = sb("mask_f", [P, P])
    mask_b = sb("mask_b", [P, P])
    cs = sb("cs", [P, KD, 2])
    n1 = sb("n1", [P, KD])
    sh1 = sb("sh1", [P, KD, 2])
    w1 = sb("w1", [P, KD, 2])
    eps = sb("eps", [P, 1])
    pr = sb("pr", [P, NPAR])
    ps_ = sb("ps_", [P, 40])
    dec = sb("dec", [P, 2, NCK])
    ef = sb("ef", [P, 2])
    PS = nc.alloc_psum_tensor("ps", [P, 8, 512], F32)

    hT = AR[:, A_HT:A_OA].rearrange("p (k t) -> p k t", k=KD)
    oA = AR[:, A_OA:A_HB].rearrange("p (k t) -> p k t", k=HEADS)
    hB = AR[:, A_HB:A_W].rearrange("p (k t) -> p k t", k=HEADS)
    W = AR[:, A_W:A_BUF].rearrange("p (b k c) -> p b k c", b=NB, k=KD)
    buf = lambda n: AR[:, A_BUF + n * T:A_BUF + (n + 1) * T]
    Q, SG, K, CUM = buf(0), [buf(1), buf(2)], [buf(3), buf(4)], buf(5)
    QD, KI, KE = [buf(6), buf(7)], [buf(8), buf(9)], [buf(10), buf(11)]
    V, XC, R, I = buf(12), buf(13), [buf(14), buf(15)], [buf(16), AR[:, A_BUF + 17 * T + 0:A_BUF + 17 * T + 0 + T]]
    XR = AR[:, A_BUF + 17 * T:A_BUF + 17 * T + XR_W]
    S = AR[:, A_S:A_ATT].rearrange("p (n v) -> p n v", n=NS)
    ATT = AR[:, A_ATT:A_KET].rearrange("p (d n t) -> p d n t", d=2, n=2)
    KET = AR[:, A_KET:A_SM].rearrange("p (n j k) -> p n j k", n=2, j=CPT)
    SM = AR[:, A_SM:A_WRI]
    WRI = AR[:, A_WRI:A_S0].rearrange("p (g c) -> p g c", g=4)
    S0 = AR[:, A_S0:A_SF].rearrange("p (d v) -> p d v", d=2)
    SF = AR[:, A_SF:A_END].rearrange("p (d v) -> p d v", d=2)
    WMOD = AR[:, A_BUF:A_BUF + MOD1 * 4096].rearrange("p (n k c) -> p n k c", n=MOD1, k=KD)
    a_mrow = A_BUF + MOD1 * 4096
    MROW, BROW = AR[0:2, a_mrow:a_mrow + 2 * D], AR[0:2, a_mrow + 2 * D:a_mrow + 4 * D]
    a_sq = A_OA
    SQ = [AR[:, a_sq + n * T:a_sq + (n + 1) * T] for n in range(2)]
    RS = AR[:, a_sq + 2 * T:a_sq + 3 * T]
    assert a_mrow + 4 * D <= A_ATT and 3 <= HEADS
    WMOD2 = AR[:, A_MOD:A_MOD + 4096].rearrange("p (k c) -> p k c", k=KD)
    MROW2 = [AR[0:2, A_MOD + 4096 + n * 512:A_MOD + 4096 + (n + 1) * 512] for n in range(2)]
    BROW2 = [AR[0:2, A_MOD + 4096 + n * 512:A_MOD + 4096 + (n + 1) * 512] for n in range(2, 4)]
    Vt = V.rearrange("p (t v) -> p t v", t=TILES)
    ROOT = [CUM, SG[1]]

    s_c, s_ms = sem("consts_ready"), sem("consts_step")
    l_x, l_c, l_b, s_silu = [sem(f"l_x{n}") for n in range(KD // 2)], sem("l_c"), sem("l_b"), sem("silu_ready")
    l_mw, l_mw2 = [sem(f"l_mw{c}") for c in range(MOD1)], sem("l_mw_late")
    m_ready, m_evac, s_dv = sem("mod_ready"), sem("mod_evac"), sem("dve_chain")
    s_act = sem("act_chain")
    t_ready, w1_ready = sem("modT_ready"), sem("w1_ready")
    sq_r, ssq_r, sd_r, h_ready = sem("square_ready"), sem("ssq_ready"), sem("sd_ready"), sem("h_ready")
    md_out = sem("mod_written")
    l_w = [sem(f"l_w{b}") for b in range(NB)]
    l_par = sem("l_par")
    z_ready, z_free = sem("z_ready"), sem("z_free")
    pa = [sem(f"par_{n}") for n in range(6)]
    f_r = [sem("f0_ready"), sem("f1_ready")]
    lf_r = [sem("lf0_ready"), sem("lf1_ready")]
    cum_r = [sem("cum0_ready"), sem("cum1_ready")]
    e_r = [sem("exp0_ready"), sem("exp1_ready")]
    tc_r = [sem("tc0_ready"), sem("tc1_ready")]
    e3_r = [sem("expend0_ready"), sem("expend1_ready")]
    k_r = [sem("kq0_ready"), sem("kq1_ready")]
    xc_r = sem("conv_ready")
    t2_r = [sem("tanh0_ready"), sem("tanh1_ready")]
    lru_done, hg_done = sem("lru_done"), sem("hg_done")
    ket_r, ket_e = sem("ket_ready"), sem("ket_evac")
    att_r, att_m = sem("att_ready"), sem("att_masked")
    ds_r, s_r = sem("ds_ready"), sem("state_ready")
    o_r, o_a = sem("o_ready"), sem("o_added")
    osq_r = sem("osq_ready")
    st_out = sem("state_out")

    def tile_of(it):
        return it if it < TILES else TI - 1 - it

    count, reads, writes = 0, {}, {}
    slot = 0
    for it in range(TI):
        d, tt = it // TILES, tile_of(it)
        first_ctx, first_lat = tt == 0, tt == (1 if d == 0 else TILES - 1)
        for jj in range(CPT):
            if jj == 0 and first_ctx:
                cur = (zero[:], None)
            elif jj == 0 and first_lat:
                cur = (S0[:, d, :], None)
            reads[it, jj] = cur
            last_lat = jj == CPT - 1 and tt == (TILES - 1 if d == 0 else 1)
            if last_lat:
                continue
            count += 1
            if jj == CPT - 1 and tt == 0:
                writes[it, jj] = (SF[:, d, :], count, True)
                cur = None
            else:
                writes[it, jj] = (S[:, slot % NS, :], count, False)
                cur = (S[:, slot % NS, :], count)
                slot += 1
    NSU = count
    LAST_CTX = max(k for _, k, final in writes.values() if final)
    state_of = lambda it, jj: reads[it, jj]


    MG = AR[:, A_MG:A_SIG].rearrange("p (k t) -> p k t", k=KD)
    WMG = [AR[:, A_WM + n * WM:A_WM + (n + 1) * WM].rearrange("p (b c) -> p b c", c=P) for n in range(2)]
    SIG = [[AR[:, A_SIG + (2 * n + g) * CH:A_SIG + (2 * n + g + 1) * CH] for g in range(2)] for n in range(2)]
    WO = AR[:, A_WO:A_WO + KD * D].rearrange("p (k c) -> p k c", k=KD)
    XT = [AR[:, A_X + n * D:A_X + (n + 1) * D] for n in range(6)]
    l_wm = [sem("l_wm0"), sem("l_wm1")]
    mg_ready, mg_sig, mg_free, mg_ch = sem("merge_ready"), sem("merge_gates"), sem("merged"), sem("merge_step")
    l_wo, l_g1, l_xt = sem("l_wo"), sem("l_g1"), [sem("l_xt0"), sem("l_xt1")]
    mix_r, mix_f, x1_r = sem("mix_ready"), sem("mix_read"), sem("x1_ready")
    x1_st = [sem("x1_st0"), sem("x1_st1")]
    NMG = KD * NCH

    WQ = AR[:, A_WQ:A_WQ + 16 * D].rearrange("p (k c) -> p k c", k=KD)
    KEYS = AR[:, A_KEY:A_KEY + 16 * P]
    RG = AR[:, A_RING:A_B].rearrange("p (s c) -> p s c", s=RING)
    bt = lambda n: AR[:, A_B + n * D:A_B + (n + 1) * D]
    XN, XE, H2N, H2C, H2T_, W2B, SH2B, G2B, _, NFB, QQ, DG_, Y, SC_, CD_, OH_ = [bt(n) for n in range(16)]
    assert A_B + 16 * D <= A_END
    H2T = H2T_.rearrange("p (k t) -> p k t", k=KD)
    QS, QTS = QQ[:, 0:512], QQ[:, 512:1024]
    DG = DG_.rearrange("p (s c) -> p s c", s=RING)
    SCS, SCW = SC_[:, 0:512], SC_[:, 512:1024]
    CAND, CANDW = CD_[:, 0:512], CD_[:, 512:1024]
    OH = [OH_[:, 0:512], OH_[:, 512:1024]]
    small = [A_B + 8 * D]

    def sm(*shape, dt=F32):
        n = int(np.prod(shape))
        ap = AR[:, small[0]:small[0] + n]
        small[0] += n
        assert small[0] <= A_B + 9 * D
        if dt != F32:
            ap = ap.bitcast(dt)
        names = "abc"[:len(shape)]
        return ap if len(shape) == 1 else ap.rearrange(
            f"p ({' '.join(names)}) -> p {' '.join(names)}", **{k: d for k, d in zip(names, shape)})

    st = sm(8)
    EIDX, GATE = sm(2 * P, dt=U32), sm(2 * P)
    IDXS = sm(2, RING, dt=U32)
    iota = sm(TOPK)
    SV, SI, SIF = sm(4, TOPK), sm(4, TOPK, dt=U32), sm(4, TOPK)
    BEST, POS = sm(2, TOPK), sm(2, TOPK, dt=U32)
    PRE, GEL, COEF = sm(RING), sm(RING), sm(RING)
    PHL = sb("places", [P, 2, 2, TOPK], U32)[:]
    PHF, EE = sb("places_f", [P, 2, 2, TOPK])[:], sb("key_numbers", [P, 2, 2, TOPK])[:]

    l_wq, l_rows, l_rows2, l_g2, l_nf = sem("l_wq"), sem("l_rows"), sem("l_rows_lat"), sem("l_g2"), sem("l_nf")
    l_xn, l_xe = sem("l_xn"), sem("l_xe")
    n_sq, n_sd, h2_r, h2t_r, h2t_e = sem("n_square"), sem("n_sd"), sem("h2_ready"), sem("h2T_ready"), sem("h2T_evac")
    q_r, q_e, qt_r, qt_e, sc_r, sc_e = (sem(x) for x in ("q_ready", "q_evac", "qT_ready", "qT_evac",
                                                         "scores_ready", "scores_evac"))
    top_r, ge_r = sem("top_ready"), sem("gate_exp_ready")
    c_pair, c_front, c_end = sem("pair_step"), sem("front_step"), sem("end_step")
    pair_done, idx_r = sem("pair_done"), sem("round_index_ready")
    gathered = [sem(f"gathered{n}") for n in range(RING)]
    dots, gel_r, coef_r, diag_r, v_used = (sem(x) for x in ("dots", "gelu_ready", "coef_ready", "diag_ready",
                                                            "v_used"))
    acc_free, e_sq, e_sd, y_r, y_st = (sem(x) for x in ("acc_free", "end_square", "end_sd", "y_ready", "y_stored"))
    it_r = sem("iota_ready")
    PAIR_STEPS, FRONT_STEPS, END_STEPS = 16, 2, 2

    def row(ap):
        return ap.partition_broadcast(P)

    def stage_b_sp(sp):
        def mod_load(j, slot):
            sp.dma_start(WMOD2, w_mod[j + MOD1]).then_inc(l_mw2, 16)
            sp.dma_start(BROW2[slot], b_mod[:, bass.ds((j + MOD1) * 512, 512)]).then_inc(l_mw2, 16)

        def block_done(i, u, more=True):
            j = i * 2 + u
            if more:
                wait_alone(sp, mg_ready, (j + 1) * NCH)
                sp.dma_start(WMG[u], w_mg[j + 2]).then_inc(l_wm[u], 16)
            wait_alone(sp, m_ready, j + 1 + MOD1)
            if more or u == 0:
                mod_load(j + 1, 1 - u)
            wait_alone(sp, m_evac, j + 1 + MOD1)
            sp.dma_start(mod_d[:, bass.ds((j + MOD1) * 512, 512)], MROW2[u]).then_inc(md_out, 16)
            wait_alone(sp, md_out, (j + 1) * 16)

        mod_load(0, 0)
        with sp.Fori(0, KD // 2 - 1) as i:
            for u in range(2):
                block_done(i, u)
        for u in range(2):
            block_done(KD // 2 - 1, u, more=False)
        sp.wait_ge(mg_free, NMG + 1)
        for s in range(2):
            sp.dma_start(XT[4 + s], row(mod_d[s, 2 * D:3 * D])).then_inc(l_g1, 16)
        for t in range(2):
            sp.dma_start(XT[t], x_tok[t]).then_inc(l_xt[t], 16)
        sp.dma_start(W2B, row(mod_d[0, 4 * D:5 * D])).then_inc(l_rows, 16)
        sp.dma_start(G2B, row(n2)).then_inc(l_rows, 16)
        sp.dma_start(SH2B, row(mod_d[0, 3 * D:4 * D])).then_inc(l_rows, 16)
        for k in range(4):
            sp.dma_start(WQ[:, 2 * k:2 * k + 2, :], w_q[:, 2 * k:2 * k + 2, :]).then_inc(l_wq, 16)
        sp.dma_start(KEYS, keys).then_inc(l_wq, 16)
        for t in range(TILES):
            sp.wait_ge(x1_r, t + 1)
            sp.dma_start(x1_d[t], XT[2 + t % 2]).then_inc(x1_st[t % 2], 16)
            if t + 2 < TILES:
                sp.dma_start(XT[t % 2], x_tok[t + 2]).then_inc(l_xt[t % 2], 16)
            if t == 1:
                sp.wait_ge(x1_st[0], 16)
                sp.dma_start(XN, x1_d[0]).then_inc(l_xn, 16)
                sp.dma_start(XE, x1_d[0]).then_inc(l_xe, 16)
        sp.wait_ge(x1_st[0], 16 * ((TILES + 1) // 2))
        sp.wait_ge(x1_st[1], 16 * (TILES // 2))
        sp.wait_ge(h2_r, 1)
        sp.dma_start(W2B, row(mod_d[1, 4 * D:5 * D])).then_inc(l_rows2, 16)
        sp.dma_start(SH2B, row(mod_d[1, 3 * D:4 * D])).then_inc(l_rows2, 16)
        sp.dma_start(XN, x1_d[1]).then_inc(l_xn, 16)
        sp.dma_start(NFB, row(nf)).then_inc(l_nf, 16)
        sp.wait_ge(c_shift, 2)
        sp.dma_start(G2B, row(mod_d[0, 5 * D:6 * D])).then_inc(l_g2, 16)

        def tile(t, last):
            if not last:
                sp.wait_ge(h2_r, t + 2)
                sp.dma_start(XN, x1_d[t + 2]).then_inc(l_xn, 16)
            sp.wait_ge(y_r, t + 1)
            sp.dma_start(y_out[t], Y).then_inc(y_st, 16)
            sp.dma_start(XE, x1_d[t + 1]).then_inc(l_xe, 16)

        tile(0, False)
        sp.dma_start(G2B, row(mod_d[1, 5 * D:6 * D])).then_inc(l_g2, 16)
        with sp.Fori(1, TILES - 2) as t:
            tile(t, False)
        tile(TILES - 2, True)
        sp.wait_ge(y_r, TILES)
        sp.dma_start(y_out[TILES - 1], Y).then_inc(y_st, 16)
        sp.wait_ge(y_st, 16 * TILES)
        sp.wait_ge(st_out, 48 * HEADS)

    def stage_b_pool(pool):
        pool.wait_ge(x1_st[0], 16 * ((TILES + 1) // 2))
        pool.wait_ge(x1_st[1], 16 * (TILES // 2))
        nc.gpsimd.iota(iota, pattern=[[1, TOPK]], base=0, channel_multiplier=0,
                       allow_small_or_imprecise_dtypes=True).then_inc(it_r, 1)

        def fetch(r, par_, first=False):
            pool.wait_ge(idx_r, r + 1)
            for s in range(RING):
                if not first:
                    wait_alone(pool, v_used, r * RING + (s + 1 - RING))
                nc.gpsimd.indirect_dma_start(
                    out=RG[:, s, :], out_offset=None, in_=uv,
                    in_offset=bass.IndirectOffsetOnAxis(ap=IDXS[:, par_, s:s + 1], axis=0),
                ).then_inc(gathered[s], 16)

        fetch(0, 0, first=True)
        fetch(1, 1)
        with pool.Fori(0, (TILES * ROUNDS - 2) // 2) as i:
            fetch(i * 2 + 2, 0)
            fetch(i * 2 + 3, 1)

    def stage_b_pe(pe):
        def merge(i, first=False):
            for u in range(2):
                pe.wait_ge(l_wm[u], i * 16 + 16)
                for n in range(NCH):
                    c = u * NCH + n
                    if not first or c >= 2:
                        pe.wait_ge(mg_free, i * 2 * NCH + c)
                    b = 4 * (c % 2)
                    sl = slice(n * CH, (n + 1) * CH)
                    for g, (src, w0, nk) in enumerate(((hT, 0, KD), (hT, KD, KD), (oA, 2 * KD, HEADS),
                                                       (hB, 2 * KD + HEADS, HEADS))):
                        if first and c == 0 and g == 2:
                            pe.wait_ge(hg_done, HEADS)
                            pe.wait_ge(lru_done, HEADS + 1)
                        if g == 3 and n == 0 and not (first and u == 0):
                            pe.wait_ge(m_evac, i * 2 + u + MOD1)
                        for k in range(nk):
                            mm = nc.tensor.matmul(PS[:, b + g, 0:CH], WMG[u][:, w0 + k, :], src[:, k, sl],
                                                  start=(k == 0), stop=(k == nk - 1))
                    mm.then_inc(mg_ready, 1)
                pe.wait_ge(mg_free, i * 2 * NCH + (u + 1) * NCH)
                pe.wait_ge(l_mw2, i * 64 + (u + 1) * 32)
                for k in range(KD):
                    mm = nc.tensor.matmul(PS[0:2, 4 * ((u + 1) * NCH % 2) + 3, :], cs[:, k, :], WMOD2[:, k, :],
                                          start=(k == 0), stop=(k == KD - 1))
                mm.then_inc(m_ready, 1)

        merge(0, first=True)
        with pe.Fori(1, KD // 2) as i:
            merge(i)
        pe.wait_ge(mg_free, NMG + 1)
        pe.wait_ge(m_evac, MODC)
        pe.wait_ge(l_wo, 16)
        for t in range(TILES):
            if t >= 2:
                pe.wait_ge(mix_f, t - 1)
            for n in range(2):
                for k in range(KD):
                    mm = nc.tensor.matmul(PS[:, 2 * (t % 2) + n, :], MG[:, k, t * P:(t + 1) * P],
                                          WO[:, k, n * 512:(n + 1) * 512], start=(k == 0), stop=(k == KD - 1))
            mm.then_inc(mix_r, 1)
        pe.wait_ge(mix_f, TILES - 1)
        pe.wait_ge(l_wq, 80)

        def front(tn):
            pe.wait_ge(h2_r, tn + 1)
            for k in range(KD):
                mm = nc.tensor.transpose(PS[:, 2 + k // 4, (k % 4) * P:(k % 4 + 1) * P],
                                         H2N[:, k * P:(k + 1) * P], ident[:])
            mm.then_inc(h2t_r, 1)

        def queries(tn, i, ks):
            if ks[0] == 0:
                wait_alone(pe, h2t_e, tn + 1)
            for k in ks:
                mm = nc.tensor.matmul(PS[:, 4, :], H2T[:, k, :], WQ[:, k, bass.ds(i * 512, 512)],
                                      start=(k == 0), stop=(k == KD - 1))
            if ks[-1] == KD - 1:
                mm.then_inc(q_r, 1)

        def turn(tn, i):
            pe.wait_ge(q_e, tn * PAIRS + i + 1)
            for c in range(4):
                mm = nc.tensor.transpose(PS[:, 5, c * P:(c + 1) * P], QS[:, c * P:(c + 1) * P], ident[:])
            mm.then_inc(qt_r, 1)

        def score(tn, i):
            pe.wait_ge(qt_e, tn * PAIRS + i + 1)
            for c in range(4):
                mm = nc.tensor.matmul(PS[:, 6, c * P:(c + 1) * P], QTS[:, c * P:(c + 1) * P],
                                      KEYS[:, bass.ds(i * 512 + c * P, P)], start=True, stop=True)
            mm.then_inc(sc_r, 1)

        def pair(tn, i):
            queries(tn, i, range(KD))
            turn(tn, i)
            score(tn, i)

        def pair_between(tn, i):
            return {2: lambda: queries(tn, i, range(4)), 3: lambda: queries(tn, i, range(4, KD)),
                    4: lambda: turn(tn, i), 5: lambda: score(tn, i)}

        def two_pairs_between(tn, i):
            return {0: lambda: queries(tn, i, range(4)), 1: lambda: queries(tn, i, range(4, KD)),
                    2: lambda: turn(tn, i), 3: lambda: score(tn, i),
                    5: lambda: queries(tn, i + 1, range(4)), 6: lambda: queries(tn, i + 1, range(4, KD)),
                    7: lambda: turn(tn, i + 1), 8: lambda: score(tn, i + 1)}

        def rounds(t, i, between):
            for q in range(RPP):
                for s in range(RING):
                    n0 = (t * ROUNDS + i * RPP + q) * RING + s + 1
                    pe.wait_ge(diag_r, n0)
                    for n in range(2):
                        mm = nc.tensor.matmul(PS[:, n, :], DG[:, s, :], RG[:, s, D + n * 512:D + (n + 1) * 512],
                                              start=False, stop=False, skip_group_check=True)
                    mm.then_inc(v_used, 1)
                    at = (q * RING + s + 1) / GRP - 1
                    if at in between:
                        between[at]()

        def clear():
            for n in range(2):
                nc.tensor.matmul(PS[:, n, :], zero[:], zero[:, 0:1].to_broadcast([P, 512]),
                                 start=True, stop=False, skip_group_check=True)

        def tile(t, last=False):
            pe.wait_ge(acc_free, t)
            clear()
            rounds(t, 0, {} if last else {1: lambda: front(t + 1)} | pair_between(t + 1, 0))
            with pe.Fori(1, PAIRS) as i:
                rounds(t, i, {} if last else pair_between(t + 1, i))

        front(0)
        for i in range(2):
            pair(0, i)
        pe.wait_ge(mix_f, TILES)
        clear()
        rounds(0, 0, two_pairs_between(0, 2))
        rounds(0, 1, {1: lambda: front(1)} | pair_between(1, 0))
        rounds(0, 2, pair_between(1, 1))
        rounds(0, 3, two_pairs_between(1, 2))
        with pe.Fori(1, TILES - 1) as t:
            tile(t)
        tile(TILES - 1, last=True)

    def stage_b_act(act):
        A = nc.scalar.activation
        with act.Fori(0, KD // 2) as i:
            for u in range(2):
                for n in range(NCH):
                    c = u * NCH + n
                    act.wait_ge(mg_ready, i * 2 * NCH + c + 1)
                    for g in range(2):
                        ins = A(SIG[c % 2][g], PS[:, 4 * (c % 2) + g, 0:CH], ACT.Sigmoid)
                    ins.then_inc(mg_sig, 1)

        def row_norm(tn):
            act.wait_ge(l_xn, tn * 16 + 16)
            A(H2T_, XN, ACT.Square, accum_out=st[:, 0:1]).then_inc(n_sq, 1)
            act.wait_ge(n_sq, tn + 1)
            A(st[:, 1:2], st[:, 0:1], ACT.Sqrt, bias=eps[:], scale=1.0 / D).then_inc(n_sd, 1)

        def rows_out(tn):
            act.wait_ge(h2t_r, tn + 1)
            for n in range(2):
                cp = A(H2T_[:, n * 512:(n + 1) * 512], PS[:, 2 + n, :], ACT.Copy)
            cp.then_inc(h2t_e, 1)

        def queries_out(tn, i):
            act.wait_ge(q_r, tn * PAIRS + i + 1)
            A(QS, PS[:, 4, :], ACT.Copy).then_inc(q_e, 1)

        def turned_out(tn, i):
            act.wait_ge(qt_r, tn * PAIRS + i + 1)
            A(QTS, PS[:, 5, :], ACT.Copy).then_inc(qt_e, 1)

        def scores_out(tn, i):
            act.wait_ge(sc_r, tn * PAIRS + i + 1)
            A(SCS, PS[:, 6, :], ACT.Copy).then_inc(sc_e, 1)

        def gates(tn, i):
            act.wait_ge(top_r, tn * PAIRS + i + 1)
            A(BEST, BEST, ACT.Exp).then_inc(ge_r, 1)

        def pair_between(tn, i):
            return {4: lambda: queries_out(tn, i), 5: lambda: turned_out(tn, i), 6: lambda: scores_out(tn, i),
                    14: lambda: gates(tn, i)}

        def two_pairs_between(tn, i):
            return {2: lambda: queries_out(tn, i), 3: lambda: turned_out(tn, i), 4: lambda: scores_out(tn, i),
                    7: lambda: queries_out(tn, i + 1), 8: lambda: turned_out(tn, i + 1),
                    9: lambda: scores_out(tn, i + 1), 10: lambda: gates(tn, i), 15: lambda: gates(tn, i + 1)}

        def rounds(t, i, between):
            for q in range(RPP):
                for g in range(RING // GRP):
                    n = (t * ROUNDS + i * RPP + q) * (RING // GRP) + g
                    act.wait_ge(dots, n + 1)
                    sl = slice(g * GRP, (g + 1) * GRP)
                    A(GEL[:, sl], PRE[:, sl], ACT.Gelu_apprx_tanh).then_inc(gel_r, 1)
                    at = q * (RING // GRP) + g
                    if at in between:
                        between[at]()
                    act.wait_ge(coef_r, n + 1)
                    for s in range(g * GRP, (g + 1) * GRP):
                        A(DG[:, s, :], ident[:], ACT.Copy, scale=COEF[:, s:s + 1]).then_inc(diag_r, 1)

        def end(t):
            act.wait_ge(e_sq, t + 1)
            A(st[:, 3:4], st[:, 2:3], ACT.Sqrt, bias=eps[:], scale=1.0 / D).then_inc(e_sd, 1)

        def front_between(tn):
            return {0: lambda: row_norm(tn), 2: lambda: rows_out(tn)} | pair_between(tn, 0)

        def tile(t, last=False):
            rounds(t, 0, {3: lambda: end(t - 1)} | ({} if last else front_between(t + 1)))
            with act.Fori(1, PAIRS) as i:
                rounds(t, i, {} if last else pair_between(t + 1, i))

        row_norm(0)
        rows_out(0)
        for i in range(2):
            queries_out(0, i)
            turned_out(0, i)
            scores_out(0, i)
            gates(0, i)
        rounds(0, 0, two_pairs_between(0, 2))
        rounds(0, 1, front_between(1))
        rounds(0, 2, pair_between(1, 1))
        rounds(0, 3, two_pairs_between(1, 2))
        with act.Fori(1, TILES - 1) as t:
            tile(t)
        tile(TILES - 1, last=True)
        end(TILES - 1)

    def stage_b_dve(dve):
        v = nc.vector
        dve.wait_ge(hg_done, HEADS)
        v.memset(mask_f[:, 0:1], 0.0).then_inc(mg_free, 1)
        with dve.Fori(0, KD // 2) as i:
            for u in range(2):
                for n in range(NCH):
                    c = u * NCH + n
                    dve.wait_ge(mg_sig, i * 2 * NCH + c + 1)
                    for g in range(2):
                        ins = v.tensor_tensor(SIG[c % 2][g], PS[:, 4 * (c % 2) + 2 + g, 0:CH], SIG[c % 2][g],
                                              ALU.mult)
                    ins.then_inc(mg_ch, 1)
                    dve.wait_ge(mg_ch, i * 2 * NCH + c + 1)
                    v.tensor_tensor(MG[:, i * 2 + u, n * CH:(n + 1) * CH], SIG[c % 2][0], SIG[c % 2][1],
                                    ALU.add).then_inc(mg_free, 1)
                dve.wait_ge(m_ready, i * 2 + u + 1 + MOD1)
                v.tensor_tensor(MROW2[u], PS[0:2, 4 * ((u + 1) * NCH % 2) + 3, :], BROW2[u],
                                ALU.add).then_inc(m_evac, 1)
        def front(tn, rows):
            ch = Chain(dve, c_front, tn * FRONT_STEPS)
            dve.wait_ge(n_sd, tn + 1)
            rows()
            ch(v.reciprocal(st[:, 4:5], st[:, 1:2]))
            ch(v.scalar_tensor_tensor(out=H2N, in0=XN, scalar=st[:, 4:5], in1=W2B, op0=ALU.mult, op1=ALU.mult))
            v.tensor_tensor(H2N, H2N, SH2B, ALU.add).then_inc(h2_r, 1)
            assert ch.n == FRONT_STEPS

        class Top16:
            lo, hi = slice(0, 8), slice(8, 16)

            def __init__(self, ch, n, vals, idx, src, work):
                self.ch, self.n, self.vals, self.idx, self.src, self.work = ch, n, vals, idx, src, work

            def best8(self):
                for c in range(self.n):
                    ins = v.max(self.vals(c, self.lo), self.src(c))
                self.ch(ins, alone=True)

            def places8(self):
                for c in range(self.n):
                    v.match_replace(self.work(c), self.vals(c, self.lo), self.src(c), NEG)
                    ins = v.max_index(self.idx(c, self.lo), self.vals(c, self.lo), self.src(c))
                self.ch(ins, alone=True)

            def next8(self):
                for c in range(self.n):
                    ins = v.max(self.vals(c, self.hi), self.work(c))
                self.ch(ins, alone=True)

            def next_places8(self):
                for c in range(self.n):
                    ins = v.max_index(self.idx(c, self.hi), self.vals(c, self.hi), self.work(c))
                self.ch(ins)

        four, half = [P, 2, TOPK, TOPK], TOPK * TOPK
        sv, sif = (x.rearrange("p (a h) k -> p a h k", h=2) for x in (SV, SIF))
        oh = [x.rearrange("p (a x y) -> p a x y", a=2, x=TOPK) for x in OH]

        class Pair:

            def __init__(self, tn, i, base=P):
                self.m, self.i = tn * PAIRS + i, i
                self.ch = Chain(dve, c_pair, self.m * PAIR_STEPS)
                self.keys = Top16(self.ch, 4, lambda c, s: SV[:, c, s], lambda c, s: SI[:, c, s],
                                  lambda c: SCS[:, c * P:(c + 1) * P], lambda c: SCW[:, c * P:(c + 1) * P])
                self.sums = Top16(self.ch, 2, lambda c, s: BEST[:, c, s], lambda c, s: POS[:, c, s],
                                  lambda c: CAND[:, c * half:(c + 1) * half],
                                  lambda c: CANDW[:, c * half:(c + 1) * half])
                self.at = bass.ds(i * 2 * TOPK + base, 2 * TOPK)

            def keys_best(self):
                wait_alone(dve, sc_e, self.m + 1)
                self.keys.best8()

            def candidates(self):
                self.keys.next_places8()
                v.tensor_copy(SIF, SI)
                cand = CAND.rearrange("p (a x y) -> p a x y", a=2, x=TOPK)
                self.ch(v.tensor_tensor(cand, sv[:, :, 0, :].unsqueeze(3).to_broadcast(four),
                                        sv[:, :, 1, :].unsqueeze(2).to_broadcast(four), ALU.add), alone=True)

            def sums_next(self):
                self.sums.next8()
                self.sums.next_places8()

            def places(self):
                ch = self.ch
                v.tensor_copy(EE[:, 0, :, 0:1], BEST[:, :, 0:1])
                v.tensor_scalar(PHL[:, 0], POS, 4, None, ALU.logical_shift_right)
                ch(v.tensor_scalar(PHL[:, 1], POS, TOPK - 1, None, ALU.bitwise_and))
                v.tensor_tensor(BEST, BEST, EE[:, 0, :, 0:1].to_broadcast([P, 2, TOPK]),
                                ALU.subtract).then_inc(top_r, 1)
                ch(v.tensor_copy(PHF, PHL))

            def key_numbers(self):
                for z in range(2):
                    ins = v.tensor_tensor(oh[z], PHF[:, z].unsqueeze(3).to_broadcast(four),
                                          iota.unsqueeze(1).unsqueeze(1).to_broadcast(four), ALU.is_equal)
                self.ch(ins)
                for z in range(2):
                    ins = v.tensor_tensor(oh[z], oh[z], sif[:, :, z, :].unsqueeze(2).to_broadcast(four), ALU.mult)
                self.ch(ins)

            def experts(self):
                ch, at = self.ch, self.at
                for z in range(2):
                    ins = v.tensor_reduce(EE[:, z], oh[z], AX_X, ALU.add)
                ch(ins)
                v.scalar_tensor_tensor(out=EIDX[:, at], in0=EE[:, 0].rearrange("p a k -> p (a k)"),
                                       scalar=float(NKEYS), in1=EE[:, 1].rearrange("p a k -> p (a k)"),
                                       op0=ALU.mult, op1=ALU.add)
                dve.wait_ge(ge_r, self.m + 1)
                ch(v.tensor_reduce(st[:, 5:7], BEST, AX_X, ALU.add))
                ch(v.reciprocal(st[:, 5:7], st[:, 5:7]))
                v.tensor_tensor(GATE[:, at].rearrange("p (a k) -> p a k", a=2), BEST,
                                st[:, 5:7].unsqueeze(2).to_broadcast([P, 2, TOPK]), ALU.mult).then_inc(pair_done, 1)
                dve.wait_ge(pair_done, self.m + 1)
                assert ch.n == PAIR_STEPS, ch.n

            def between(self):
                return {6: self.keys_best, 7: self.keys.places8, 8: self.keys.next8, 9: self.candidates,
                        10: self.sums.best8, 11: self.sums.places8, 12: self.sums_next, 13: self.places,
                        14: self.key_numbers, 15: self.experts}

            def at_once(self):
                for _, step in sorted(self.between().items()):
                    step()

        def in_turn(*steps):
            def run():
                for step in steps:
                    step()
            return run

        def two_pairs_between(a, b):
            return {4: a.keys_best, 5: a.keys.places8, 6: a.keys.next8, 7: in_turn(a.candidates, a.sums.best8),
                    8: in_turn(a.sums.places8, a.sums_next), 9: in_turn(a.places, a.key_numbers), 10: a.experts,
                    11: in_turn(b.keys_best, b.keys.places8), 12: in_turn(b.keys.next8, b.candidates),
                    13: in_turn(b.sums.best8, b.sums.places8, b.sums_next),
                    14: in_turn(b.places, b.key_numbers), 15: b.experts}

        def coef(t, i, q, g):
            n = (t * ROUNDS + i * RPP + q) * (RING // GRP) + g
            dve.wait_ge(gel_r, n + 1)
            sl = slice(g * GRP, (g + 1) * GRP)
            v.tensor_tensor(COEF[:, sl], GEL[:, sl],
                            GATE[:, bass.ds(i * RPP * RING + q * RING + g * GRP, GRP)],
                            ALU.mult).then_inc(coef_r, 1)

        def rounds(t, i, between, last=False):
            todo = None
            for q in range(RPP):
                for g in range(RING // GRP):
                    for s in range(g * GRP, (g + 1) * GRP):
                        dve.wait_ge(gathered[s], (t * ROUNDS + i * RPP + q) * 16 + 16)
                        ins = v.tensor_tensor_reduce(RG[:, s, 0:D], RG[:, s, 0:D], H2C, 1.0, 0.0, ALU.mult,
                                                     ALU.add, PRE[:, s:s + 1])
                        if todo:
                            coef(t, i, *todo)
                            todo = None
                    ins.then_inc(dots, 1)
                    todo = (q, g)
                    at = q * (RING // GRP) + g
                    if at in between:
                        between[at]()
                if not last or q < 2:
                    v.tensor_copy(IDXS[:, q % 2, :], EIDX[:, bass.ds(i * RPP * RING + (q + 2) * RING, RING)])\
                        .then_inc(idx_r, 1)
            coef(t, i, *todo)

        def shift():
            v.tensor_copy(EIDX[:, 0:P], EIDX[:, P:2 * P])
            v.tensor_copy(GATE[:, 0:P], GATE[:, P:2 * P])
            v.tensor_copy(H2C, H2N).then_inc(c_shift, 1)

        class End:

            def __init__(self, t):
                self.t, self.ch = t, Chain(dve, c_end, t * END_STEPS)

            def read_sum(self):
                t = self.t
                dve.wait_ge(v_used, (t + 1) * ROUNDS * RING)
                v.tensor_tensor(Y, PS[:, 0:2, :].rearrange("p b c -> p (b c)"), G2B, ALU.mult).then_inc(acc_free, 1)

            def residual(self):
                t = self.t
                dve.wait_ge(acc_free, t + 1)
                dve.wait_ge(l_xe, t * 16 + 16)
                self.ch(v.tensor_tensor(Y, Y, XE, ALU.add))
                v.tensor_tensor_reduce(XE, Y, Y, 1.0, 0.0, ALU.mult, ALU.add, st[:, 2:3]).then_inc(e_sq, 1)

            def norm(self):
                dve.wait_ge(e_sd, self.t + 1)
                self.ch(v.reciprocal(st[:, 7:8], st[:, 3:4]))
                v.scalar_tensor_tensor(out=Y, in0=Y, scalar=st[:, 7:8], in1=NFB, op0=ALU.mult,
                                       op1=ALU.mult).then_inc(y_r, 1)
                assert self.ch.n == END_STEPS, self.ch.n

        def front_between(tn):
            return {1: lambda: front(tn, lambda: dve.wait_ge(l_rows2, 32))} | Pair(tn, 0).between()

        def next_tile(t):
            dve.wait_ge(dots, (t + 1) * ROUNDS * (RING // GRP))
            dve.wait_ge(coef_r, (t + 1) * ROUNDS * (RING // GRP))
            dve.wait_ge(idx_r, (t + 1) * ROUNDS + 2)
            shift()
            dve.wait_ge(c_shift, t + 3)

        def tile(t, last=False):
            end = End(t - 1)
            between = {0: end.read_sum, 2: end.residual, 4: end.norm}
            rounds(t, 0, between if last else between | front_between(t + 1))
            with dve.Fori(1, PAIRS - last) as i:
                rounds(t, i, {} if last else Pair(t + 1, i).between())
            dve.wait_ge(y_st, t * 16)
            dve.wait_ge(l_g2, 32)
            if last:
                rounds(t, PAIRS - 1, {}, last=True)
            else:
                next_tile(t)

        def first_rows():
            dve.wait_ge(l_rows, 48)
            v.scalar_tensor_tensor(out=W2B, in0=W2B, scalar=1.0, in1=G2B, op0=ALU.add, op1=ALU.mult)

        dve.wait_ge(l_g1, 32)
        for t in range(TILES):
            dve.wait_ge(mix_r, t + 1)
            if t >= 2:
                dve.wait_ge(x1_st[t % 2], 16 * (t // 2))
            o = XT[2 + t % 2]
            g1 = XT[4 + (t > 0)]
            v.tensor_tensor(o, PS[:, 2 * (t % 2):2 * (t % 2) + 2, :].rearrange("p b c -> p (b c)"), g1,
                            ALU.mult).then_inc(mix_f, 1)
            dve.wait_ge(mix_f, t + 1)
            dve.wait_ge(l_xt[t % 2], 16 * (t // 2 + 1))
            v.tensor_tensor(o, o, XT[t % 2], ALU.add).then_inc(x1_r, 1)
            if t == TILES - 3:
                front(0, first_rows)
        dve.wait_ge(it_r, 1)
        Pair(0, 0, base=0).at_once()
        for q in range(2):
            v.tensor_copy(IDXS[:, q, :], EIDX[:, q * RING:(q + 1) * RING]).then_inc(idx_r, 1)
        v.tensor_copy(H2C, H2N).then_inc(c_shift, 1)
        dve.wait_ge(l_rows2, 32)
        v.scalar_tensor_tensor(out=W2B, in0=W2B, scalar=1.0, in1=G2B, op0=ALU.add, op1=ALU.mult).then_inc(c_shift, 1)
        Pair(0, 1, base=0).at_once()
        dve.wait_ge(c_shift, 2)
        rounds(0, 0, two_pairs_between(Pair(0, 2, base=0), Pair(0, 3, base=0)))
        rounds(0, 1, front_between(1))
        rounds(0, 2, Pair(1, 1).between())
        rounds(0, 3, two_pairs_between(Pair(1, 2), Pair(1, 3)))
        dve.wait_ge(l_nf, 16)
        dve.wait_ge(l_g2, 16)
        next_tile(0)
        with dve.Fori(1, TILES - 1) as t:
            tile(t)
        tile(TILES - 1, last=True)
        end = End(TILES - 1)
        end.read_sum()
        end.residual()
        end.norm()

    c_shift = sem("shifted")
    block = ctx.enter_context(nc.Block())

    @block.sync
    def _(sp):
        sp.dma_start(cs[:], cT).then_inc(l_c, 16)
        sp.dma_start(n1[:], n1T).then_inc(l_c, 16)
        for k in range(0, KD, 2):
            sp.dma_start(hT[:, k:k + 2], xT[:, k:k + 2]).then_inc(l_x[k // 2], 16)
        for c in range(MOD1):
            sp.dma_start(WMOD[:, c], w_mod[c]).then_inc(l_mw[c], 16)
        sp.dma_start(BROW, b_mod[:, 0:2 * D]).then_inc(l_b, 16)

        def weights(h, b):
            sp.dma_start(W[:, b], w_in[h, b]).then_inc(l_w[b], 16)

        def params(h):
            sp.dma_start(pr[:], par[h]).then_inc(l_par, 16)
            for half in range(2):
                a = half * 64
                sp.dma_start(WRI[a:a + 64, :, a:a + 64], wri[h, half]).then_inc(l_par, 16)
            sp.dma_start(S0, s0[h]).then_inc(l_par, 16)

        def results(h):
            sp.wait_ge(s_r, h * NSU + LAST_CTX)
            for d in range(2):
                sp.dma_start(hg_out[d, h], SF[:, d]).then_inc(st_out, 16)
            wait_alone(sp, hg_done, h + 1)
            sp.wait_ge(lru_done, h + 2)
            sp.dma_start(lru_out[h], ef[:]).then_inc(st_out, 16)

        for b in range(NB):
            weights(0, b)
        sp.wait_ge(s_c, 2)
        params(0)
        with sp.Fori(0, HEADS - 1) as h:
            for b in range(NB):
                sp.wait_ge(z_ready, h * ZC + (W_BLOCKS[b] + 1) * NCH)
                weights(h + 1, b)
            results(h)
            params(h + 1)
            wait_alone(sp, st_out, (h + 1) * 48)
        sp.wait_ge(z_ready, (HEADS - 1) * ZC + B_SSQ * NCH)
        for n in range(2):
            sp.dma_start(WMG[n], w_mg[n]).then_inc(l_wm[n], 16)
        results(HEADS - 1)
        sp.wait_ge(st_out, 48 * HEADS)
        sp.dma_start(WO, w_out).then_inc(l_wo, 16)
        stage_b_sp(sp)

    @block.gpsimd
    def _(pool):
        ch = Chain(pool, s_ms)
        ch(nc.gpsimd.memset(ones[:], 1.0))
        keep = dict(fill=0.0)
        ch(nc.gpsimd.affine_select(out=mask_f[:], in_=ones[:], compare_op=ALU.is_ge, fill=0.0, base=0,
                                   pattern=[[1, P]], channel_multiplier=-1))
        ch(nc.gpsimd.affine_select(out=mask_b[:], in_=ones[:], compare_op=ALU.is_ge, fill=0.0, base=0,
                                   pattern=[[-1, P]], channel_multiplier=1))
        ch(nc.gpsimd.affine_select(out=ident[:], in_=mask_f[:], compare_op=ALU.is_ge, fill=0.0, base=0,
                                   pattern=[[-1, P]], channel_multiplier=1))
        for m in (mask_f, mask_b):
            v = m[:].rearrange("p (c t) -> p c t", c=CPT)
            ch(nc.gpsimd.affine_select(out=v, in_=v, compare_op=ALU.is_ge, fill=0.0, base=0,
                                       pattern=[[-CHUNK, CPT], [0, CHUNK]], channel_multiplier=1))
            ch(nc.gpsimd.affine_select(out=v, in_=v, compare_op=ALU.is_ge, fill=0.0, base=CHUNK - 1,
                                       pattern=[[CHUNK, CPT], [0, CHUNK]], channel_multiplier=-1))
        nc.gpsimd.memset(zero[:], 0.0)
        nc.gpsimd.memset(eps[:], EPS).then_inc(s_c, 1)
        ch(nc.gpsimd.memset(AR[:, A_ATT:A_SM], 0.0))
        ch(nc.gpsimd.memset(AR[:, A_SM:A_WRI], 1.0))
        ch(nc.gpsimd.memset(SM.rearrange("p (n c) -> p n c", c=CHUNK)[:, :, 0:1], 0.0))
        nc.gpsimd.memset(AR[:, A_WRI:A_S0], 0.0).then_inc(s_c, 1)
        stage_b_pool(pool)

    @block.tensor
    def _(pe):
        pe.wait_ge(s_silu, 1)
        pe.wait_ge(s_c, 1)
        for k in range(KD):
            pe.wait_ge(sq_r, k + 1)
            for n in range(NCH):
                mm = nc.tensor.matmul(PS[:, 3 + n, 0:CH], ones[:], SQ[k % 2][:, n * CH:(n + 1) * CH],
                                      start=(k == 0), stop=(k == KD - 1))
            mm.then_inc(ssq_r, 1)
        for c in range(MOD1):
            pe.wait_ge(l_mw[c], 16)
            if c >= 2:
                pe.wait_ge(m_evac, c - 1)
            for k in range(KD):
                mm = nc.tensor.matmul(PS[0:2, c % 2, :], cs[:, k, :], WMOD[:, c, k, :],
                                      start=(k == 0), stop=(k == KD - 1))
            mm.then_inc(m_ready, 1)
        pe.wait_ge(m_evac, MOD1)
        for n in range(2 * KD):
            mm = nc.tensor.transpose(PS[:, 2, 2 * n:2 * n + 2], MROW[:, n * P:(n + 1) * P], ident[0:2, 0:2])
        mm.then_inc(t_ready, 1)

        with pe.Fori(0, HEADS) as h:
            def z_bank(b, n):
                c = b * NCH + n
                if c >= NCH:
                    pe.wait_ge(z_free, h * ZC + c - NCH + 1)
                return PS[:, n, 0:CH]

            def project(b, n, ks=range(KD)):
                if ks[0] == 0:
                    pe.wait_ge(l_w[W_BLOCKS.index(b)], h * 16 + 16)
                    z_bank(b, n)
                z = PS[:, n, 0:CH]
                w = W[:, W_BLOCKS.index(b)]
                if b == B_V:
                    for u in range(CH // P):
                        t = n * (CH // P) + u
                        for k in ks:
                            mm = nc.tensor.matmul(z[:, u * P:(u + 1) * P], hT[:, k, t * P:(t + 1) * P],
                                                  w[:, k, :], start=(k == 0), stop=(k == KD - 1))
                else:
                    for k in ks:
                        if b == B_FF and n == 0:
                            pe.wait_ge(h_ready, k + 1)
                        mm = nc.tensor.matmul(z, w[:, k, :], hT[:, k, n * CH:(n + 1) * CH],
                                              start=(k == 0), stop=(k == KD - 1))
                if ks[-1] == KD - 1:
                    mm.then_inc(z_ready, 1)

            for b in (B_FF, B_Q, B_FB, B_XR, B_V):
                for n in range(NCH):
                    project(b, n)

            def lru_gate(c):
                if c == 0:
                    pe.wait_ge(xc_r, h + 1)
                    pe.wait_ge(l_par, h * 64 + 64)
                g, n = divmod(c, NCH)
                z = z_bank(B_GATES + g, n)
                nc.tensor.matmul(z, WRI[:, g, :], XC[:, n * CH:(n + 1) * CH],
                                 start=True, stop=True).then_inc(z_ready, 1)

            def fill(it):
                if it < GATE_STEPS:
                    for c in range(2):
                        lru_gate(2 * it + c)
                else:
                    c, part = divmod(it - GATE_STEPS, 2)
                    project(*late_chunk(c), range(part * KD // 2, (part + 1) * KD // 2))

            def scores(it):
                d, tt = it // TILES, tile_of(it)
                if it % TILES == 0:
                    pe.wait_ge(k_r[d], h + 1)
                sl = slice(tt * P, (tt + 1) * P)
                nc.tensor.transpose(PS[:, 3, 0:P], KE[d][:, sl], ident[:]).then_inc(ket_r, 1)
                if it:
                    pe.wait_ge(att_m, h * TI + it)
                nc.tensor.matmul(PS[:, 4, 0:P], KI[d][:, sl], QD[d][:, sl],
                                 start=True, stop=True).then_inc(att_r, 1)

            def shares(it):
                pe.wait_ge(ket_e, h * TI + it + 1)
                for j in range(CPT):
                    mm = nc.tensor.matmul(PS[:, 5 + it % 2, j * P:(j + 1) * P], KET[:, it % 2, j, :],
                                          Vt[:, tile_of(it), :], start=True, stop=True)
                mm.then_inc(ds_r, 1)

            def outputs(it):
                d, tt = it // TILES, tile_of(it)
                pe.wait_ge(att_m, h * TI + it + 1)
                if it:
                    pe.wait_ge(o_a, h * TI + it)
                nc.tensor.matmul(PS[:, 7, 0:P], Vt[:, tt, :], ATT[:, d, it % 2, :], start=True, stop=False)
                for jj in range(CPT):
                    j = jj if d == 0 else CPT - 1 - jj
                    st, cnt = state_of(it, jj)
                    if cnt is not None:
                        pe.wait_ge(s_r, h * NSU + cnt)
                    c = slice(tt * P + j * CHUNK, tt * P + (j + 1) * CHUNK)
                    mm = nc.tensor.matmul(PS[:, 7, j * CHUNK:(j + 1) * CHUNK], st, QD[d][:, c],
                                          start=False, stop=(jj == CPT - 1))
                mm.then_inc(o_r, 1)

            pe.wait_ge(z_free, h * ZC + (B_V + 1) * NCH)
            scores(0)
            shares(0)
            for it in range(TI):
                if it + 1 < TI:
                    scores(it + 1)
                fill(it)
                if it + 1 < TI:
                    shares(it + 1)
                outputs(it)
            for n in range(NCH):
                pe.wait_ge(osq_r, h * NCH + n + 1)
                z = z_bank(B_SSQ, n)
                nc.tensor.matmul(z, ones[:], K[1][:, n * CH:(n + 1) * CH], start=True, stop=True)\
                    .then_inc(z_ready, 1)
            pe.wait_ge(z_free, (h + 1) * ZC)
        stage_b_pe(pe)

    @block.scalar
    def _(act):
        A = nc.scalar.activation
        act.wait_ge(l_c, 32)
        A(cs[:], cs[:], ACT.Silu).then_inc(s_silu, 1)
        for k in range(KD):
            if k % 2 == 0:
                act.wait_ge(l_x[k // 2], 16)
            if k >= 2:
                act.wait_ge(ssq_r, k - 1)
            A(SQ[k % 2], hT[:, k, :], ACT.Square).then_inc(sq_r, 1)
        act.wait_ge(ssq_r, KD)
        act.wait_ge(s_c, 1)
        for n in range(NCH):
            last = A(RS[:, n * CH:(n + 1) * CH], PS[:, 3 + n, 0:CH], ACT.Sqrt, bias=eps[:], scale=1.0 / D)
        last.then_inc(sd_r, 1)
        act.wait_ge(h_ready, KD)

        act.wait_ge(s_c, 2)
        with act.Fori(0, HEADS) as h:
            def evac(b, n, out, func, in_=None, **kw):
                act.wait_ge(z_ready, h * ZC + b * NCH + n + 1)
                return A(out, PS[:, n, 0:CH] if in_ is None else in_, func, **kw)

            def block_out(b, out, func, **kw):
                for n in range(NCH):
                    evac(b, n, out[:, n * CH:(n + 1) * CH], func, **kw).then_inc(z_free, 1)

            block_out(B_FF, SG[0], ACT.Sigmoid)
            act.wait_ge(pa[0], h + 1)
            A(ps_[:, 8:12], ps_[:, 4:8], ACT.Exp)
            A(ps_[:, 16:18], ps_[:, 14:16], ACT.Exp, scale=-1.0).then_inc(pa[1], 1)
            act.wait_ge(pa[2], h + 1)
            A(ps_[:, 20:22], ps_[:, 18:20], ACT.Ln).then_inc(pa[3], 1)
            block_out(B_Q, Q, ACT.Silu)
            act.wait_ge(f_r[0], h + 1)
            A(SG[0], SG[0], ACT.Ln).then_inc(lf_r[0], 1)
            act.wait_ge(lru_done, h + 1)
            block_out(B_FB, SG[1], ACT.Sigmoid)

            def exps(d):
                act.wait_ge(cum_r[d], h + 1)
                A(QD[d], CUM, ACT.Exp)
                A(KI[d], CUM, ACT.Exp, scale=-1.0)
                e = CHUNK - 1 if d == 0 else 0
                ends = CUM.rearrange("p (c t) -> p c t", t=CHUNK)[:, :, e]
                A(dec[:, d, :], ends, ACT.Exp).then_inc(e_r[d], 1)
                act.wait_ge(tc_r[d], h + 1)
                A(KE[d], KE[d], ACT.Exp).then_inc(e3_r[d], 1)

            act.wait_ge(f_r[1], h + 1)
            A(SG[1], SG[1], ACT.Ln).then_inc(lf_r[1], 1)
            exps(0)
            xl = XR[:, N_CTX + 5:N_CTX + 5 + N_LAT].rearrange("p (c r) -> p r c", r=GRID_H)
            evac(B_XR, 0, XR[:, 2:2 + N_CTX], ACT.Copy, in_=PS[:, 0, 0:N_CTX])
            r0 = 0
            for n in range(NCH):
                lo = N_CTX if n == 0 else 0
                rows = (CH - lo) // GRID_W
                src = PS[:, n, lo:CH].rearrange("p (r c) -> p r c", c=GRID_W)
                evac(B_XR, n, xl[:, r0:r0 + rows, :], ACT.Copy, in_=src).then_inc(z_free, 1)
                r0 += rows
            exps(1)
            block_out(B_V, V, ACT.Copy)

            def ket_out(it):
                act.wait_ge(ket_r, h * TI + it + 1)
                if it >= 2:
                    act.wait_ge(ds_r, h * TI + it - 1)
                for j in range(CPT):
                    rows = slice(j * CHUNK, (j + 1) * CHUNK)
                    cp = A(KET[rows, it % 2, j, :], PS[rows, 3, 0:P], ACT.Copy)
                cp.then_inc(ket_e, 1)

            def fill_out(it):
                if it < GATE_STEPS:
                    for c in range(2 * it, 2 * it + 2):
                        g, n = divmod(c, NCH)
                        d, out = g // 2, (R, I)[g % 2][g // 2]
                        bias = (P_BR, P_BI)[g % 2] + d
                        evac(B_GATES + g, n, out[:, n * CH:(n + 1) * CH], ACT.Sigmoid,
                             bias=pr[:, bias:bias + 1]).then_inc(z_free, 1)
                elif (it - GATE_STEPS) % 2:
                    b, n = late_chunk((it - GATE_STEPS) // 2)
                    out, func = ((oA, ACT.Silu), (hB, ACT.Gelu_apprx_tanh))[b == B_XG]
                    evac(b, n, out[:, h, n * CH:(n + 1) * CH], func).then_inc(z_free, 1)

            def decay(it):
                if it == GATE_STEPS:
                    act.wait_ge(z_free, h * ZC + B_G * NCH)
                    for d in range(2):
                        A(ROOT[d], R[d], ACT.Tanh, scale=ps_[:, 34 + d:35 + d]).then_inc(s_act, 1)
                elif it == GATE_STEPS + 2:
                    act.wait_ge(s_act, h * 2 + 2)
                    for d in range(2):
                        A(ROOT[d], ROOT[d], ACT.Sqrt)
                elif it == GATE_STEPS + 4:
                    for d in range(2):
                        A(R[d], R[d], ACT.Exp, scale=ps_[:, 36 + d:37 + d]).then_inc(t2_r[d], 1)

            act.wait_ge(pa[4], h + 1)
            ket_out(0)
            for it in range(TI):
                if it + 1 < TI:
                    ket_out(it + 1)
                fill_out(it)
                decay(it)
            block_out(B_SSQ, QD[0], ACT.Sqrt, bias=eps[:], scale=1.0 / P)
        stage_b_act(act)

    @block.vector
    def _(dve):
        v = nc.vector
        ch = Chain(dve, s_dv)
        dve.wait_ge(sd_r, 1)
        ch(v.reciprocal(RS, RS))
        dve.wait_ge(l_b, 16)
        for c in range(MOD1):
            dve.wait_ge(m_ready, c + 1)
            sl = slice(c * 512, (c + 1) * 512)
            v.tensor_tensor(MROW[:, sl], PS[0:2, c % 2, :], BROW[:, sl], ALU.add).then_inc(m_evac, 1)
        dve.wait_ge(t_ready, 1)
        mt = PS[:, 2, 0:4 * KD].rearrange("p (s k c) -> p s k c", s=2, c=2)
        v.tensor_copy(sh1[:], mt[:, 0])
        ch(v.tensor_scalar(w1[:], mt[:, 1], 1.0, None, ALU.add))
        ch(v.tensor_tensor(w1[:], w1[:], n1[:].unsqueeze(2).to_broadcast([P, KD, 2]), ALU.mult))
        for k in range(KD):
            for s, sl in enumerate((slice(0, N_CTX), slice(N_CTX, T))):
                ins = v.scalar_tensor_tensor(out=hT[:, k, sl], in0=hT[:, k, sl], scalar=w1[:, k, s:s + 1],
                                             in1=RS[:, sl], op0=ALU.mult, op1=ALU.mult)
                if s == 1:
                    ch(ins)
            for s, sl in enumerate((slice(0, N_CTX), slice(N_CTX, T))):
                ins = v.tensor_scalar(hT[:, k, sl], hT[:, k, sl], sh1[:, k, s:s + 1], None, ALU.add)
            ins.then_inc(h_ready, 1)
        base = ch.n
        dve.wait_ge(s_c, 2)
        per_head = DVE_HEAD
        v.memset(ef[:], 0.0).then_inc(lru_done, 1)
        with dve.Fori(0, HEADS) as h:
            ch = Chain(dve, s_dv, base + h * per_head)
            dve.wait_ge(l_par, h * 64 + 64)
            lg = pr[:, P_LB:P_LB + 4].rearrange("p (d l) -> p d l", d=2)
            ch(v.tensor_tensor(ps_[:, 0:2], lg[:, :, 0], lg[:, :, 1], ALU.max))
            v.tensor_tensor(ps_[:, 4:8].rearrange("p (d l) -> p d l", d=2), lg,
                            ps_[:, 0:2].unsqueeze(2).to_broadcast([P, 2, 2]), ALU.subtract)
            lam = pr[:, P_LAM:P_LAM + 2]
            v.scalar_tensor_tensor(out=ps_[:, 14:16], in0=lam, scalar=-1.0, in1=lam, op0=ALU.mult,
                                   op1=ALU.max).then_inc(pa[0], 1)
            dve.wait_ge(pa[1], h + 1)
            ex = ps_[:, 8:12].rearrange("p (d l) -> p d l", d=2)
            v.tensor_scalar(ps_[:, 18:20], ps_[:, 16:18], 1.0, None, ALU.add).then_inc(pa[2], 1)
            ch(v.tensor_tensor(ps_[:, 2:4], ex[:, :, 0], ex[:, :, 1], ALU.add))
            ch(v.reciprocal(ps_[:, 2:4], ps_[:, 2:4]))
            ch(v.tensor_tensor(ps_[:, 24:26], ex[:, :, 0], ps_[:, 2:4], ALU.mult))
            v.tensor_scalar(ps_[:, 26:28], ps_[:, 24:26], -1.0, 1.0, ALU.mult, ALU.add)
            ch(v.tensor_scalar(ps_[:, 22:24], ps_[:, 18:20], -1.0, None, ALU.add))
            ch(v.tensor_scalar(ps_[:, 28:30], ps_[:, 22:24], 0.0, None, ALU.is_equal))
            ch(v.tensor_tensor(ps_[:, 22:24], ps_[:, 22:24], ps_[:, 28:30], ALU.add))
            ch(v.reciprocal(ps_[:, 22:24], ps_[:, 22:24]))
            dve.wait_ge(pa[3], h + 1)
            ch(v.tensor_tensor(ps_[:, 20:22], ps_[:, 20:22], ps_[:, 28:30], ALU.add))
            ch(v.tensor_tensor(ps_[:, 20:22], ps_[:, 20:22], ps_[:, 22:24], ALU.mult))
            ch(v.tensor_tensor(ps_[:, 20:22], ps_[:, 20:22], ps_[:, 16:18], ALU.mult))
            ch(v.tensor_scalar(ps_[:, 30:32], lam, -1.0, 0.0, ALU.mult, ALU.max))
            ch(v.tensor_tensor(ps_[:, 20:22], ps_[:, 20:22], ps_[:, 30:32], ALU.add))
            v.tensor_scalar(ps_[:, 34:36], ps_[:, 20:22], LRU_C / 2, None, ALU.mult)
            v.tensor_scalar(ps_[:, 36:38], ps_[:, 20:22], -LRU_C, None, ALU.mult).then_inc(pa[4], 1)

            def forget(d):
                dve.wait_ge(z_free, h * ZC + NCH * ((B_FF, B_FB)[d] + 1))
                ch(v.tensor_scalar(SG[d], SG[d], ps_[:, 26 + d:27 + d], ps_[:, 24 + d:25 + d],
                                   ALU.mult, ALU.add))
                v.tensor_scalar(K[d], SG[d], -1.0, 1.0, ALU.mult, ALU.add).then_inc(f_r[d], 1)

            def sums(d):
                dve.wait_ge(lf_r[d], h + 1)
                if d:
                    dve.wait_ge(e_r[0], h + 1)
                if d == 0:
                    ins = v.tensor_tensor_scan(CUM, SM[:, 0:T], SG[0], 0.0, ALU.mult, ALU.add)
                else:
                    ins = v.tensor_tensor_scan(CUM[:, ::-1], SM[:, 1:T + 1][:, ::-1], SG[1][:, ::-1], 0.0,
                                               ALU.mult, ALU.add)
                ins.then_inc(cum_r[d], 1)
                dve.wait_ge(cum_r[d], h + 1)
                cv = CUM.rearrange("p (c t) -> p c t", t=CHUNK)
                e = CHUNK - 1 if d == 0 else 0
                v.tensor_tensor(KE[d].rearrange("p (c t) -> p c t", t=CHUNK),
                                cv[:, :, e:e + 1].to_broadcast([P, NCK, CHUNK]), cv,
                                ALU.subtract).then_inc(tc_r[d], 1)

            def keys_(d):
                dve.wait_ge(e_r[d], h + 1)
                if d == 0:
                    dve.wait_ge(z_free, h * ZC + NCH * (B_Q + 1))
                v.tensor_tensor(QD[d], QD[d], Q, ALU.mult)
                v.tensor_tensor(KI[d], KI[d], K[d], ALU.mult)
                dve.wait_ge(e3_r[d], h + 1)
                v.tensor_tensor(KE[d], KE[d], K[d], ALU.mult).then_inc(k_r[d], 1)

            forget(0)
            sums(0)
            forget(1)
            keys_(0)
            sums(1)
            for a, n in ((0, 2), (N_CTX + 2, 3), (N_CTX + 5 + N_LAT, 1)):
                last = v.memset(XR[:, a:a + n], 0.0)
            ch(last)
            dve.wait_ge(z_free, h * ZC + NCH * (B_XR + 1))
            for j in range(4):
                for a, o, n in ((0, 0, N_CTX), (N_CTX + 3, N_CTX, N_LAT)):
                    xs, xo = XR[:, a + j:a + j + n], XC[:, o:o + n]
                    cw = pr[:, P_CW + j:P_CW + j + 1]
                    if j == 0:
                        ins = v.tensor_scalar(xo, xs, cw, pr[:, P_CB:P_CB + 1], ALU.mult, ALU.add)
                    else:
                        ins = v.scalar_tensor_tensor(out=xo, in0=xs, scalar=cw, in1=xo, op0=ALU.mult,
                                                     op1=ALU.add)
                if j < 3:
                    ch(ins)
                else:
                    ins.then_inc(xc_r, 1)
            keys_(1)

            def lru(it):
                d, part = divmod(it - LRU_STEP, 3)
                if d < 0:
                    return
                if part == 0:
                    dve.wait_ge(t2_r[d], h + 1)
                    v.tensor_tensor(I[d], I[d], XC, ALU.mult)
                    ch(v.scalar_tensor_tensor(out=ROOT[d], in0=R[d], scalar=1.0, in1=ROOT[d], op0=ALU.add,
                                              op1=ALU.mult))
                elif part == 1:
                    ch(v.tensor_tensor(I[d], I[d], ROOT[d], ALU.mult))
                else:
                    for a, n, first in ((0, N_CTX, 0.0), (N_CTX, N_LAT, pr[:, P_H0 + d:P_H0 + d + 1])):
                        views = [x[:, a:a + n] for x in (I[d], R[d])]
                        if d:
                            views = [x[:, ::-1] for x in views]
                        ins = v.tensor_tensor_scan(views[0], views[1], views[0], first, ALU.mult, ALU.add)
                    ch(ins)

            O, OS = K[0], K[1]

            def out_of(it):
                tt = tile_of(it)
                dve.wait_ge(o_r, h * TI + it + 1)
                o = O[:, tt * P:(tt + 1) * P]
                if it < TILES:
                    v.tensor_copy(o, PS[:, 7, 0:P]).then_inc(o_a, 1)
                else:
                    v.tensor_tensor(o, PS[:, 7, 0:P], o, ALU.add).then_inc(o_a, 1)

            for it in range(TI):
                d, tt = it // TILES, tile_of(it)
                wait_alone(dve, att_r, h * TI + it + 1)
                v.copy_predicated(ATT[:, d, it % 2, :], (mask_f, mask_b)[d][:].bitcast(I32),
                                  PS[:, 4, 0:P]).then_inc(att_m, 1)
                if it:
                    lru(it - 1)
                dve.wait_ge(ds_r, h * TI + it + 1)
                for jj in range(CPT):
                    if (it, jj) not in writes:
                        continue
                    j = jj if d == 0 else CPT - 1 - jj
                    st, cnt = reads[it, jj]
                    to, k, final = writes[it, jj]
                    if cnt is not None:
                        dve.wait_ge(s_r, h * NSU + cnt)
                    c = tt * CPT + j
                    ins = v.scalar_tensor_tensor(out=to, in0=st, scalar=dec[:, d, c:c + 1],
                                                 in1=PS[:, 5 + it % 2, j * P:(j + 1) * P],
                                                 op0=ALU.mult, op1=ALU.add)
                    ins.then_inc(s_r, 1)
                if it:
                    out_of(it - 1)
            out_of(TI - 1)
            dve.wait_ge(o_a, h * TI + TI)
            for n in range(NCH):
                sl = slice(n * CH, (n + 1) * CH)
                v.tensor_tensor(OS[:, sl], O[:, sl], O[:, sl], ALU.mult).then_inc(osq_r, 1)
            v.tensor_copy(ef[:, 0:1], I[0][:, N_CTX - 1:N_CTX])
            ch(v.tensor_copy(ef[:, 1:2], I[1][:, 0:1]))
            ch(v.tensor_tensor(I[0], I[0], I[1], ALU.add))
            dve.wait_ge(z_free, h * ZC + B_SSQ * NCH)
            hc = hB[:, h, 0:N_CTX]
            v.tensor_tensor(hc, hc, I[0][:, 0:N_CTX], ALU.mult)
            hl = hB[:, h, N_CTX:T].rearrange("p (r c) -> p r c", c=GRID_W)
            v.tensor_tensor(hl, hl, I[0][:, N_CTX:T].rearrange("p (c r) -> p r c", r=GRID_H),
                            ALU.mult).then_inc(lru_done, 1)
            dve.wait_ge(z_free, (h + 1) * ZC)
            ch(v.reciprocal(QD[0], QD[0]))
            ch(v.scalar_tensor_tensor(out=O, in0=O, scalar=pr[:, P_HN:P_HN + 1], in1=QD[0], op0=ALU.mult,
                                      op1=ALU.mult))
            v.tensor_tensor(oA[:, h, :], oA[:, h, :], O, ALU.mult).then_inc(hg_done, 1)
            assert ch.n == per_head, ch.n
        stage_b_dve(dve)
    ctx.close()


def layout(x_prompt, x_sample, state_hgrn, state_rglru, c, c_ctx, w_mod, b_mod, norm1, w_in,
           hg_lb_logits, hg_norm, lru_conv_w, lru_conv_b, lru_w_r, lru_b_r, lru_w_i, lru_b_i,
           lru_lambda, w_branch_a, w_branch_b, w_out, norm2, pk_w_q, pk_sub_keys, pk_u, pk_v, norm_f):
    cat, cg = np.concatenate, np.ascontiguousarray
    x = cat([x_prompt[0], x_sample[0]], axis=0)
    blocks = lambda w: w.reshape(w.shape[0] // P, P, w.shape[1] // P, P).transpose(2, 1, 0, 3)
    wi = blocks(w_in[0])
    q, ff, fb, v, g, xr, xg = (wi[4 * n:4 * n + 4] for n in range(7))
    ga, gb = wi[28:36], wi[36:44]
    per = lambda a: a.reshape(a.shape[0], HEADS, P).transpose(1, 2, 0)
    lb = hg_lb_logits.transpose(2, 0, 1).reshape(HEADS, P, 4)
    par = cat([lb, per(lru_conv_w[0]), per(lru_conv_b), per(lru_b_r[0]), per(lru_b_i[0]), per(lru_lambda[0]),
               np.broadcast_to(hg_norm[0][None, :, None], (HEADS, P, 1)),
               per(state_rglru[0, 0])], axis=2)
    gate_w = np.stack([lru_w_r[0, 0], lru_w_i[0, 0], lru_w_r[0, 1], lru_w_i[0, 1]])
    return {
        "xT": cg(x.T.reshape(KD, P, T).transpose(1, 0, 2)),
        "x_tok": x.reshape(TILES, P, D),
        "cT": cg(np.stack([c_ctx, c[0]], axis=1).reshape(KD, P, 2).transpose(1, 0, 2)),
        "w_mod": cg(w_mod[0].reshape(KD, P, MODC, 512).transpose(2, 1, 0, 3)),
        "b_mod": cg(np.broadcast_to(b_mod[0], (2, MODW))),
        "n1T": cg(norm1[0].reshape(KD, P).T),
        "w_in": cg(np.stack([ff, q, fb, xr, v, g, xg], axis=1)),
        "par": cg(par),
        "wri": cg(gate_w.reshape(4, HEADS, 2, 64, 64).transpose(1, 2, 3, 0, 4)),
        "s0": cg(state_hgrn[0, 0].transpose(1, 2, 0, 3)),
        "w_mg": cg(cat([ga, gb, blocks(w_branch_a[0]), blocks(w_branch_b[0])], axis=2)),
        "w_out": cg(w_out[0].reshape(KD, P, D).transpose(1, 0, 2)),
        "n2": norm2[0],
        "nf": norm_f,
        "w_q": cg(pk_w_q[0].reshape(KD, P, 2 * D).transpose(1, 0, 2)),
        "keys": cg(pk_sub_keys[0].transpose(3, 1, 0, 2).reshape(P, 16 * P)),
        "uv": cg(cat([pk_u[0], pk_v[0]], axis=1)),
    }


_OUTS = {"y_out": (TILES, P, D), "hg_out": (2, HEADS, P, P), "lru_out": (HEADS, P, 2)}


def make(nc, shapes):
    args = [nc.dram_tensor(f"in_{n}", s, F32, kind="ExternalInput").ap() for n, s in shapes.items()]
    args += [nc.dram_tensor(f"out_{n}", s, F32, kind="ExternalOutput").ap() for n, s in _OUTS.items()]
    args.append(nc.dram_tensor("mod_scratch", (2, MODW), F32).ap())
    args.append(nc.dram_tensor("x1_scratch", (TILES, P, D), F32).ap())
    build(nc, *args)


def kernel(**inputs):
    import concourse.bacc as _bacc
    from concourse.bass_utils import run_bass_kernel_spmd as _run

    arrays = layout(**{k: np.asarray(a) for k, a in inputs.items()})
    nc = _bacc.Bacc("TRN2", target_bir_lowering=False, num_devices=1)
    make(nc, {n: a.shape for n, a in arrays.items()})
    r = _run(nc, [{f"in_{n}": a for n, a in arrays.items()}], core_ids=[0])
    y, hg, lru = (r.results[0][f"out_{n}"] for n in _OUTS)
    y = y.reshape(T, D)
    return (y[None, :N_CTX], y[None, N_CTX:], hg[None, None],
            np.ascontiguousarray(lru.transpose(2, 0, 1)).reshape(1, 1, 2, HEADS * P))
```
